# Optimizing a Trainium2 kernel written in Bass

```python
import jax, jax.numpy as jnp
from jax import lax
import numpy as np
import math

D_MODEL = 1024
BATCH = 1
SEQ = 256
DEPTH = 2

CTX_LEN = 256
GRID_W = 64
N_MOD = 9
D_FF = 2816
EPS = 1e-6
A_HEADS = 4
A_HEAD_DIM = 128
A_WIDTH = A_HEADS * A_HEAD_DIM
MLSTM_CHUNK = 128
CONV_W = 3
B_GROUPS = 4
B_GROUP_DIM = 128
B_WIDTH = B_GROUPS * B_GROUP_DIM
SGU_CHUNK = 128
EVEN_IN = 4 * A_WIDTH + 4 * A_HEADS + 2 * B_WIDTH
EVEN_MIX = A_WIDTH + B_WIDTH
C_HEADS = 16
C_KV_HEADS = 4
C_GROUP = C_HEADS // C_KV_HEADS
C_HEAD_DIM = 64
WINDOW = 128
ATTN_BLOCK = 128
ODD_QKV = (C_HEADS + 2 * C_KV_HEADS) * C_HEAD_DIM
ROPE_BASE = 10000.0
N_EVEN = (DEPTH + 1) // 2
N_ODD = DEPTH // 2


f32 = jnp.float32

def _rms_norm(t):
    tf = t.astype(f32)
    return (tf * lax.rsqrt(jnp.mean(tf * tf, axis=-1, keepdims=True) + EPS)).astype(t.dtype)

def _modulation(s, w, b):
    m = s @ w + b
    return m.reshape(s.shape[0], N_MOD, 1, D_MODEL)

def _modulate(h, shift, scale):
    return _rms_norm(h) * (1.0 + scale) + shift

def _swiglu(h, w_in, w_out):
    g, u = jnp.split(h @ w_in, 2, axis=-1)
    return (jax.nn.silu(g) * u) @ w_out

def _axial_rope_tables(T):
    rows = T // GRID_W
    row, col = jnp.meshgrid(jnp.arange(rows), jnp.arange(GRID_W), indexing='ij')
    n_freq = C_HEAD_DIM // 4
    inv = ROPE_BASE ** (-jnp.arange(n_freq, dtype=f32) / n_freq)
    ang = jnp.concatenate([row.reshape(-1, 1).astype(f32) * inv,
                           col.reshape(-1, 1).astype(f32) * inv], axis=-1)
    return jnp.cos(ang), jnp.sin(ang)

def _apply_rope(t, cos, sin):
    x1, x2 = t[..., 0::2], t[..., 1::2]
    cs = cos[None, :, None, :].astype(t.dtype)
    sn = sin[None, :, None, :].astype(t.dtype)
    return jnp.stack([x1 * cs - x2 * sn, x1 * sn + x2 * cs], axis=-1).reshape(t.shape)

def _centred_depthwise_conv(x, w):
    C = x.shape[-1]
    return lax.conv_general_dilated(x, w[:, None, :].astype(x.dtype), window_strides=(1,),
                                    padding=[(CONV_W // 2, CONV_W // 2)],
                                    dimension_numbers=('NWC', 'WIO', 'NWC'),
                                    feature_group_count=C)

def _zero_state(B_):
    return (jnp.zeros((B_, A_HEADS, A_HEAD_DIM, A_HEAD_DIM), f32),
            jnp.zeros((B_, A_HEADS, A_HEAD_DIM), f32),
            jnp.zeros((B_, A_HEADS), f32))

def _mlstm_chunkwise(q, k, v, ig, lf, state):
    B_, H, T, d = q.shape
    L = MLSTM_CHUNK
    N = T // L
    q = q.reshape(B_, H, N, L, d)
    k = k.reshape(B_, H, N, L, d)
    v = v.reshape(B_, H, N, L, d)
    ig = ig.reshape(B_, H, N, L)
    b = jnp.cumsum(lf.reshape(B_, H, N, L), axis=-1)
    g = b[..., -1]
    a = g[..., None] - b + ig
    m_loc = jnp.max(a, axis=-1)
    w = jnp.exp(a - m_loc[..., None])
    C_loc = jnp.einsum('bhnl,bhnld,bhnle->bhnde', w, k, v)
    n_loc = jnp.einsum('bhnl,bhnld->bhnd', w, k)

    def step(carry, xs):
        C, n, m = carry
        g_j, m_loc_j, C_loc_j, n_loc_j = xs
        m_new = jnp.maximum(g_j + m, m_loc_j)
        dec = jnp.exp(g_j + m - m_new)
        add = jnp.exp(m_loc_j - m_new)
        C_new = dec[..., None, None] * C + add[..., None, None] * C_loc_j
        n_new = dec[..., None] * n + add[..., None] * n_loc_j
        return (C_new, n_new, m_new), (C, n, m)

    xs = (jnp.moveaxis(g, 2, 0), jnp.moveaxis(m_loc, 2, 0),
          jnp.moveaxis(C_loc, 2, 0), jnp.moveaxis(n_loc, 2, 0))
    final, (C_prev, n_prev, m_prev) = lax.scan(step, state, xs)
    C_prev = jnp.moveaxis(C_prev, 0, 2)
    n_prev = jnp.moveaxis(n_prev, 0, 2)
    m_prev = jnp.moveaxis(m_prev, 0, 2)

    e = b + m_prev[..., None]
    tril = jnp.tril(jnp.ones((L, L), dtype=bool))
    Dm = jnp.where(tril, b[..., :, None] - b[..., None, :] + ig[..., None, :], -jnp.inf)
    m_t = jnp.maximum(e, jnp.max(Dm, axis=-1))
    S = jnp.einsum('bhntd,bhnsd->bhnts', q, k) * jnp.exp(Dm - m_t[..., None])
    inter = jnp.exp(e - m_t)
    num = (jnp.einsum('bhnts,bhnse->bhnte', S, v)
           + inter[..., None] * jnp.einsum('bhntd,bhnde->bhnte', q, C_prev))
    den = jnp.sum(S, axis=-1) + inter * jnp.einsum('bhntd,bhnd->bhnt', q, n_prev)
    h = num / jnp.maximum(jnp.abs(den), jnp.exp(-m_t))[..., None]
    return h.reshape(B_, H, T, d), final

def _flip(ts):
    return tuple(jnp.flip(t, axis=2) for t in ts)

def _even_stream_inputs(n, w_in, conv_w, gate_b):
    B_, T, _ = n.shape
    p = n @ w_in
    qk, v, o, gates, uv = jnp.split(
        p, [2 * A_WIDTH, 3 * A_WIDTH, 4 * A_WIDTH, 4 * A_WIDTH + 4 * A_HEADS], axis=-1)
    q, k = jnp.split(jax.nn.silu(_centred_depthwise_conv(qk, conv_w)), 2, axis=-1)

    def heads(t):
        return t.reshape(B_, T, A_HEADS, A_HEAD_DIM).transpose(0, 2, 1, 3).astype(f32)

    q, k, v = heads(q), heads(k) * (A_HEAD_DIM ** -0.5), heads(v)
    gt = (gates.astype(f32) + gate_b.reshape(-1).astype(f32)).reshape(B_, T, 4, A_HEADS).transpose(2, 0, 3, 1)
    fwd = (gt[0], jax.nn.log_sigmoid(gt[1]))
    bwd = (gt[2], jax.nn.log_sigmoid(gt[3]))
    return (q, k, v), fwd, bwd, o, uv

def _spatial_gating(uv, norm_g, ws, sb):
    u, v = jnp.split(jax.nn.gelu(uv), 2, axis=-1)
    v = _rms_norm(v) * norm_g
    B_, T, _ = v.shape
    vb = v.reshape(B_, T // SGU_CHUNK, SGU_CHUNK, B_GROUPS, B_GROUP_DIM)
    mixed = jnp.einsum('gpq,bnqgc->bnpgc', ws, vb) + sb.T[:, :, None]
    return u * mixed.reshape(B_, T, B_WIDTH)

def _even_output(hsum, o, uv, mnorm, sgu_g, ws, sb, w_out):
    B_, H, T, d = hsum.shape
    hn = hsum * lax.rsqrt(jnp.mean(hsum * hsum, axis=-1, keepdims=True) + EPS) * mnorm[None, :, None, :].astype(f32)
    h_a = jax.nn.sigmoid(o) * hn.transpose(0, 2, 1, 3).reshape(B_, T, A_WIDTH).astype(o.dtype)
    h_b = _spatial_gating(uv, sgu_g, ws, sb)
    return jnp.concatenate([h_a, h_b], axis=-1) @ w_out

def _even_mixer(nx, nc, w_in, w_out, conv_w, gate_b, mnorm, sgu_g, ws, sb, need_ctx):
    qkv_c, fw_c, bw_c, o_c, uv_c = _even_stream_inputs(nc, w_in, conv_w, gate_b)
    qkv_x, fw_x, bw_x, o_x, uv_x = _even_stream_inputs(nx, w_in, conv_w, gate_b)
    zero = _zero_state(nx.shape[0])
    hc_f, st_f = _mlstm_chunkwise(*qkv_c, *fw_c, zero)
    hc_b, st_b = _mlstm_chunkwise(*_flip(qkv_c), *_flip(bw_c), zero)
    hx_f, _ = _mlstm_chunkwise(*qkv_x, *fw_x, st_f)
    hx_b, _ = _mlstm_chunkwise(*_flip(qkv_x), *_flip(bw_x), st_b)
    yx = _even_output(hx_f + jnp.flip(hx_b, axis=2), o_x, uv_x, mnorm, sgu_g, ws, sb, w_out)
    yc = None
    if need_ctx:
        yc = _even_output(hc_f + jnp.flip(hc_b, axis=2), o_c, uv_c, mnorm, sgu_g, ws, sb, w_out)
    return yx, yc

def _softmax_with_sink(sink, *scores):
    ref = scores[0]
    s0 = jnp.broadcast_to(sink[None, :, :, None, None].astype(f32), ref.shape[:-1] + (1,))
    p = jax.nn.softmax(jnp.concatenate([s0] + [s.astype(f32) for s in scores], axis=-1), axis=-1)
    parts = []
    off = 1
    for s in scores:
        parts.append(p[..., off:off + s.shape[-1]])
        off += s.shape[-1]
    return parts

def _window_attention(q, k, v, kc, vc, sink):
    B_, T, _, _ = q.shape
    nb = T // ATTN_BLOCK
    scale = C_HEAD_DIM ** -0.5
    qb = (q * scale).reshape(B_, nb, ATTN_BLOCK, C_KV_HEADS, C_GROUP, C_HEAD_DIM).transpose(1, 0, 2, 3, 4, 5)
    pad = ((0, 0), (ATTN_BLOCK, ATTN_BLOCK), (0, 0), (0, 0))
    kp, vp = jnp.pad(k, pad), jnp.pad(v, pad)
    offs = jnp.arange(ATTN_BLOCK)
    band_offs = jnp.arange(3 * ATTN_BLOCK) - ATTN_BLOCK

    def block(args):
        qj, j = args
        start = j * ATTN_BLOCK
        kj = lax.dynamic_slice_in_dim(kp, start, 3 * ATTN_BLOCK, axis=1)
        vj = lax.dynamic_slice_in_dim(vp, start, 3 * ATTN_BLOCK, axis=1)
        qpos = start + offs
        kpos = start + band_offs
        valid = (jnp.abs(qpos[:, None] - kpos[None, :]) <= WINDOW) & (kpos[None, :] >= 0) & (kpos[None, :] < T)
        s_band = jnp.where(valid, jnp.einsum('bqhgd,bkhd->bhgqk', qj, kj).astype(f32), -jnp.inf)
        s_ctx = jnp.einsum('bqhgd,bkhd->bhgqk', qj, kc)
        p_ctx, p_band = _softmax_with_sink(sink, s_ctx, s_band)
        return (jnp.einsum('bhgqk,bkhd->bqhgd', p_ctx.astype(vc.dtype), vc)
                + jnp.einsum('bhgqk,bkhd->bqhgd', p_band.astype(vj.dtype), vj))

    out = lax.map(block, (qb, jnp.arange(nb)))
    return out.transpose(1, 0, 2, 3, 4, 5).reshape(B_, T, C_HEADS * C_HEAD_DIM)

def _context_attention(qc, kc, vc, sink):
    B_, Tc = qc.shape[:2]
    q = (qc * (C_HEAD_DIM ** -0.5)).reshape(B_, Tc, C_KV_HEADS, C_GROUP, C_HEAD_DIM)
    (p,) = _softmax_with_sink(sink, jnp.einsum('bqhgd,bkhd->bhgqk', q, kc))
    return jnp.einsum('bhgqk,bkhd->bqhgd', p.astype(vc.dtype), vc).reshape(B_, Tc, C_HEADS * C_HEAD_DIM)

def _odd_mixer(nx, nc, w_qkv, w_out, sink, cos, sin, need_ctx):
    B_, T, _ = nx.shape
    Tc = nc.shape[1]
    qdim = C_HEADS * C_HEAD_DIM
    kvdim = C_KV_HEADS * C_HEAD_DIM
    q, k, v = jnp.split(nx @ w_qkv, [qdim, qdim + kvdim], axis=-1)
    q = _apply_rope(q.reshape(B_, T, C_HEADS, C_HEAD_DIM), cos, sin)
    k = _apply_rope(k.reshape(B_, T, C_KV_HEADS, C_HEAD_DIM), cos, sin)
    v = v.reshape(B_, T, C_KV_HEADS, C_HEAD_DIM)
    kc, vc = jnp.split(nc @ w_qkv[:, qdim:], 2, axis=-1)
    kc = kc.reshape(B_, Tc, C_KV_HEADS, C_HEAD_DIM)
    vc = vc.reshape(B_, Tc, C_KV_HEADS, C_HEAD_DIM)
    sink = sink.reshape(C_KV_HEADS, C_GROUP)
    yx = _window_attention(q, k, v, kc, vc, sink) @ w_out
    yc = None
    if need_ctx:
        qc = (nc @ w_qkv[:, :qdim]).reshape(B_, Tc, C_HEADS, C_HEAD_DIM)
        yc = _context_attention(qc, kc, vc, sink) @ w_out
    return yx, yc

def first_inputs(seed: int = 0) -> dict:
    key = jax.random.key(seed)
    ks = jax.random.split(key, 20)
    D = D_MODEL

    def nrm(k, shape, scale):
        return jax.random.normal(k, shape, jnp.float32) * scale

    is_forget = jnp.array([0.0, 1.0, 0.0, 1.0], jnp.float32)[:, None]
    forget_lin = jnp.linspace(3.0, 6.0, A_HEADS, dtype=jnp.float32)[None, :]
    return {
        'x': nrm(ks[0], (BATCH, SEQ, D), 1.0),
        'c': nrm(ks[1], (BATCH, D), 1.0),
        'ctx': nrm(ks[2], (BATCH, CTX_LEN, D), 1.0),
        'c_ctx': nrm(ks[3], (D,), 1.0),
        'ada_w': nrm(ks[4], (DEPTH, D, N_MOD * D), 0.5 * D ** -0.5),
        'ada_b': nrm(ks[5], (DEPTH, N_MOD * D), 0.02),
        'ffn_w_in': nrm(ks[6], (DEPTH, 2, D, 2 * D_FF), D ** -0.5),
        'ffn_w_out': nrm(ks[7], (DEPTH, 2, D_FF, D), D_FF ** -0.5),
        'even_w_in': nrm(ks[8], (N_EVEN, D, EVEN_IN), D ** -0.5),
        'even_w_out': nrm(ks[9], (N_EVEN, EVEN_MIX, D), EVEN_MIX ** -0.5),
        'mlstm_conv': nrm(ks[10], (N_EVEN, CONV_W, 2 * A_WIDTH), CONV_W ** -0.5),
        'mlstm_gate_b': is_forget * forget_lin + nrm(ks[11], (N_EVEN, 4, A_HEADS), 0.1),
        'mlstm_norm': 1.0 + nrm(ks[12], (N_EVEN, A_HEADS, A_HEAD_DIM), 0.05),
        'sgu_norm': 1.0 + nrm(ks[13], (N_EVEN, B_WIDTH), 0.05),
        'sgu_ws': nrm(ks[14], (N_EVEN, B_GROUPS, SGU_CHUNK, SGU_CHUNK), SGU_CHUNK ** -0.5),
        'sgu_b': 1.0 + nrm(ks[15], (N_EVEN, B_GROUPS, SGU_CHUNK), 0.1),
        'odd_w_qkv': nrm(ks[16], (N_ODD, D, ODD_QKV), D ** -0.5),
        'odd_w_out': nrm(ks[17], (N_ODD, C_HEADS * C_HEAD_DIM, D), (C_HEADS * C_HEAD_DIM) ** -0.5),
        'attn_sink': nrm(ks[18], (N_ODD, C_HEADS), 0.5),
        'final_norm': 1.0 + nrm(ks[19], (D,), 0.05),
    }

def first_block(x, c, ctx, c_ctx, ada_w, ada_b, ffn_w_in, ffn_w_out, even_w_in, even_w_out,
              mlstm_conv, mlstm_gate_b, mlstm_norm, sgu_norm, sgu_ws, sgu_b,
              odd_w_qkv, odd_w_out, attn_sink, final_norm):
    cos, sin = _axial_rope_tables(x.shape[1])
    sc = jax.nn.silu(c)
    scc = jax.nn.silu(c_ctx)[None]
    h, hc = x, ctx
    for layer in range(DEPTH):
        last = layer == DEPTH - 1
        mod = _modulation(sc, ada_w[layer], ada_b[layer])
        modc = _modulation(scc, ada_w[layer], ada_b[layer])
        h = h + 0.5 * mod[:, 2] * _swiglu(_modulate(h, mod[:, 0], mod[:, 1]),
                                          ffn_w_in[layer, 0], ffn_w_out[layer, 0])
        hc = hc + 0.5 * modc[:, 2] * _swiglu(_modulate(hc, modc[:, 0], modc[:, 1]),
                                             ffn_w_in[layer, 0], ffn_w_out[layer, 0])
        nx = _modulate(h, mod[:, 3], mod[:, 4])
        nc = _modulate(hc, modc[:, 3], modc[:, 4])
        if layer % 2 == 0:
            e = layer // 2
            yx, yc = _even_mixer(nx, nc, even_w_in[e], even_w_out[e], mlstm_conv[e], mlstm_gate_b[e],
                                 mlstm_norm[e], sgu_norm[e], sgu_ws[e], sgu_b[e], not last)
        else:
            o = layer // 2
            yx, yc = _odd_mixer(nx, nc, odd_w_qkv[o], odd_w_out[o], attn_sink[o], cos, sin, not last)
        h = h + mod[:, 5] * yx
        h = h + 0.5 * mod[:, 8] * _swiglu(_modulate(h, mod[:, 6], mod[:, 7]),
                                          ffn_w_in[layer, 1], ffn_w_out[layer, 1])
        if not last:
            hc = hc + modc[:, 5] * yc
            hc = hc + 0.5 * modc[:, 8] * _swiglu(_modulate(hc, modc[:, 6], modc[:, 7]),
                                                 ffn_w_in[layer, 1], ffn_w_out[layer, 1])
    return _rms_norm(h) * final_norm


DEPTH_2 = 1


N_ATTN_HEADS = 16
QK_NOPE_DIM = 64
QK_ROPE_DIM = 32
V_HEAD_DIM = 64
Q_LORA_RANK = 384
KV_LORA_RANK = 256
ROPE_THETA = 10000.0
Q_BLOCK = 128
ATTN_SCALE = (QK_NOPE_DIM + QK_ROPE_DIM) ** -0.5

N_SSD_HEADS = 16
SSD_HEAD_DIM = 64
SSD_GROUPS = 2
HEADS_PER_GROUP = N_SSD_HEADS // SSD_GROUPS
SSD_STATE = 128
SSD_CONV = 5
SSD_CHUNK = 128
D_INNER = N_SSD_HEADS * SSD_HEAD_DIM
GN = SSD_GROUPS * SSD_STATE
XBC_WIDTH = D_INNER + 2 * GN

ATTN_WIDTH = N_ATTN_HEADS * V_HEAD_DIM
MIX_WIDTH = ATTN_WIDTH + D_INNER

FFN_CONV = 3

N_MOD_2 = 6

IN_SPLITS = (Q_LORA_RANK, KV_LORA_RANK, QK_ROPE_DIM, D_INNER, XBC_WIDTH, 2 * N_SSD_HEADS)
IN_WIDTH = sum(IN_SPLITS)
IN_OFFSETS = tuple(int(o) for o in np.cumsum(IN_SPLITS)[:-1])


def rms_norm(x, w):
    xf = x.astype(jnp.float32)
    y = xf * lax.rsqrt(jnp.mean(xf * xf, axis=-1, keepdims=True) + EPS)
    return (y * w.astype(jnp.float32)).astype(x.dtype)

def modulate(h, shift, scale):
    return h * (1 + scale) + shift

def in_split(h):
    return jnp.split(h, IN_OFFSETS, axis=-1)

def depthwise_conv(x, w, b):
    k = w.shape[0]
    out = lax.conv_general_dilated(
        x, w[:, None, :].astype(x.dtype), window_strides=(1,), padding=((k // 2, k // 2),),
        dimension_numbers=("NWC", "WIO", "NWC"), feature_group_count=x.shape[-1])
    return out + b

def axial_rope_tables(seq_len):
    n_rows = seq_len // GRID_W
    row = jnp.repeat(jnp.arange(n_rows), GRID_W).astype(jnp.float32)
    col = jnp.tile(jnp.arange(GRID_W), n_rows).astype(jnp.float32)
    axis_dim = QK_ROPE_DIM // 2
    inv_freq = ROPE_THETA ** (-jnp.arange(0, axis_dim, 2, dtype=jnp.float32) / axis_dim)
    ang_r = row[:, None] * inv_freq
    ang_c = col[:, None] * inv_freq
    ang = jnp.concatenate([ang_r, ang_r, ang_c, ang_c], axis=-1)
    return jnp.cos(ang), jnp.sin(ang)

def rotate_half_axial(x):
    def rh(t):
        a, b = jnp.split(t, 2, axis=-1)
        return jnp.concatenate([-b, a], axis=-1)
    xr, xc = jnp.split(x, 2, axis=-1)
    return jnp.concatenate([rh(xr), rh(xc)], axis=-1)

def apply_rope(x, cos, sin):
    xf = x.astype(jnp.float32)
    return (xf * cos + rotate_half_axial(xf) * sin).astype(x.dtype)

def mla_queries(cq, q_norm_w, w_q_up):
    b, l, _ = cq.shape
    q = (rms_norm(cq, q_norm_w) @ w_q_up).reshape(b, l, N_ATTN_HEADS, QK_NOPE_DIM + QK_ROPE_DIM)
    return q[..., :QK_NOPE_DIM], q[..., QK_NOPE_DIM:]

def mla_keys_values(ckv, kv_norm_w, w_kv_up):
    b, l, _ = ckv.shape
    kv = (rms_norm(ckv, kv_norm_w) @ w_kv_up).reshape(b, l, N_ATTN_HEADS, QK_NOPE_DIM + V_HEAD_DIM)
    return kv[..., :QK_NOPE_DIM], kv[..., QK_NOPE_DIM:]

def attend(q_nope, q_rope, k_nope, k_rope, v):
    s = (jnp.einsum("bqhd,bkhd->bhqk", q_nope, k_nope)
         + jnp.einsum("bqhr,bkr->bhqk", q_rope, k_rope)) * ATTN_SCALE
    p = jax.nn.softmax(s.astype(jnp.float32), axis=-1).astype(v.dtype)
    return jnp.einsum("bhqk,bkhd->bqhd", p, v)

def latent_attention(q_nope, q_rope, k_nope, k_rope, v):
    b, s, h, _ = q_nope.shape
    nb = s // Q_BLOCK

    def to_blocks(t):
        return jnp.moveaxis(t.reshape(b, nb, Q_BLOCK, *t.shape[2:]), 1, 0)

    out = lax.map(lambda qb: attend(qb[0], qb[1], k_nope, k_rope, v),
                  (to_blocks(q_nope), to_blocks(q_rope)))
    return jnp.moveaxis(out, 0, 1).reshape(b, s, h * V_HEAD_DIM)

def ssd_prepare(xbc, dt_raw, conv_w, conv_b, dt_bias):
    b, l, _ = xbc.shape
    xbc = jax.nn.silu(depthwise_conv(xbc, conv_w, conv_b))
    xs, bm, cm = jnp.split(xbc, [D_INNER, D_INNER + GN], axis=-1)
    xs = xs.reshape(b, l, SSD_GROUPS, HEADS_PER_GROUP, SSD_HEAD_DIM)
    bm = bm.reshape(b, l, SSD_GROUPS, SSD_STATE)
    cm = cm.reshape(b, l, SSD_GROUPS, SSD_STATE)
    dt = jax.nn.softplus(dt_raw.astype(jnp.float32).reshape(b, l, 2, SSD_GROUPS, HEADS_PER_GROUP)
                         + dt_bias.astype(jnp.float32).reshape(2, SSD_GROUPS, HEADS_PER_GROUP))
    return xs, bm, cm, dt

def segment_decay(cum):
    n = cum.shape[-1]
    diff = cum[..., :, None] - cum[..., None, :]
    mask = jnp.tril(jnp.ones((n, n), dtype=bool))
    return jnp.exp(jnp.where(mask, diff, -jnp.inf))

def ssd_states(xh, dt, A, bm, cm, init_state):
    b, l, g, e, p = xh.shape
    nc = l // SSD_CHUNK
    xd = (xh * dt[..., None]).reshape(b, nc, SSD_CHUNK, g, e, p)
    a_cum = jnp.cumsum(jnp.moveaxis((dt * A).reshape(b, nc, SSD_CHUNK, g, e), 2, -1), axis=-1)
    bc = bm.reshape(b, nc, SSD_CHUNK, g, -1)
    cc = cm.reshape(b, nc, SSD_CHUNK, g, -1)
    decay_to_end = jnp.exp(a_cum[..., -1:] - a_cum)
    chunk_states = jnp.einsum("bclgn,bcgel,bclgep->bcgepn", bc, decay_to_end, xd)
    states = jnp.concatenate([init_state[:, None], chunk_states], axis=1)
    chunk_cum = jnp.cumsum(jnp.pad(a_cum[..., -1], ((0, 0), (1, 0), (0, 0), (0, 0))), axis=1)
    decay_chunks = segment_decay(jnp.moveaxis(chunk_cum, 1, -1))
    states = jnp.einsum("bgezc,bcgepn->bzgepn", decay_chunks, states)
    return (xd, a_cum, bc, cc), states[:, :-1], states[:, -1]

def ssd_output(pieces, entering_states):
    xd, a_cum, bc, cc = pieces
    within = segment_decay(a_cum)
    cb = jnp.einsum("bclgn,bcsgn->bcgls", cc, bc)
    y_diag = jnp.einsum("bcgls,bcgels,bcsgep->bclgep", cb, within, xd)
    y_off = jnp.einsum("bclgn,bcgepn,bcgel->bclgep", cc, entering_states, jnp.exp(a_cum))
    b, nc, q, g, e, p = y_diag.shape
    return (y_diag + y_off).reshape(b, nc * q, g, e, p)

def ssd_finish(y, xs, z, d_skip, norm_w):
    b, l = y.shape[:2]
    y = y + d_skip.reshape(SSD_GROUPS, HEADS_PER_GROUP, 1) * xs
    y = y.reshape(b, l, D_INNER).astype(z.dtype)
    return rms_norm(y * jax.nn.silu(z), norm_w)

def conv_glu(h, w_up, conv_w, conv_b, w_down):
    gate, val = jnp.split(h @ w_up, 2, axis=-1)
    gate = depthwise_conv(gate, conv_w, conv_b)
    return (jax.nn.gelu(gate, approximate=False) * val) @ w_down

def second_inputs(seed: int = 0) -> dict:
    key = jax.random.key(seed)
    ks = jax.random.split(key, 32)
    f32 = jnp.float32
    L = DEPTH_2

    def dense(k, shape, fan_in):
        return jax.random.normal(k, shape, f32) * fan_in ** -0.5

    def gain(k, shape):
        return 1.0 + 0.1 * jax.random.normal(k, shape, f32)

    def bias(k, shape):
        return 0.02 * jax.random.normal(k, shape, f32)

    dt0 = jnp.exp(jax.random.uniform(ks[15], (L, 2, N_SSD_HEADS), f32, math.log(1e-3), math.log(1e-1)))
    return {
        "x": jax.random.normal(ks[0], (BATCH, SEQ, D_MODEL), f32),
        "c": jax.random.normal(ks[1], (BATCH, D_MODEL), f32),
        "ctx": jax.random.normal(ks[2], (BATCH, CTX_LEN, D_MODEL), f32),
        "c_ctx": jax.random.normal(ks[3], (D_MODEL,), f32),
        "w_mod": dense(ks[4], (L, D_MODEL, N_MOD_2 * D_MODEL), D_MODEL),
        "b_mod": bias(ks[5], (L, N_MOD_2 * D_MODEL)),
        "mix_pre_norm": gain(ks[6], (L, D_MODEL)),
        "mix_post_norm": gain(ks[7], (L, D_MODEL)),
        "w_in": dense(ks[8], (L, D_MODEL, IN_WIDTH), D_MODEL),
        "q_norm": gain(ks[9], (L, Q_LORA_RANK)),
        "w_q_up": dense(ks[10], (L, Q_LORA_RANK, N_ATTN_HEADS * (QK_NOPE_DIM + QK_ROPE_DIM)), Q_LORA_RANK),
        "kv_norm": gain(ks[11], (L, KV_LORA_RANK)),
        "w_kv_up": dense(ks[12], (L, KV_LORA_RANK, N_ATTN_HEADS * (QK_NOPE_DIM + V_HEAD_DIM)), KV_LORA_RANK),
        "ssd_conv_w": dense(ks[13], (L, SSD_CONV, XBC_WIDTH), SSD_CONV),
        "ssd_conv_b": bias(ks[14], (L, XBC_WIDTH)),
        "ssd_a_log": jnp.log(jax.random.uniform(ks[16], (L, 2, N_SSD_HEADS), f32, 1.0, 16.0)),
        "ssd_dt_bias": dt0 + jnp.log(-jnp.expm1(-dt0)),
        "ssd_d": gain(ks[17], (L, N_SSD_HEADS)),
        "ssd_norm": gain(ks[18], (L, D_INNER)),
        "w_out": dense(ks[19], (L, MIX_WIDTH, D_MODEL), MIX_WIDTH),
        "ffn_pre_norm": gain(ks[20], (L, D_MODEL)),
        "ffn_post_norm": gain(ks[21], (L, D_MODEL)),
        "w_up": dense(ks[22], (L, D_MODEL, 2 * D_FF), D_MODEL),
        "ffn_conv_w": dense(ks[23], (L, FFN_CONV, D_FF), FFN_CONV),
        "ffn_conv_b": bias(ks[24], (L, D_FF)),
        "w_down": dense(ks[25], (L, D_FF, D_MODEL), D_FF),
    }

def second_block(x, c, ctx, c_ctx, w_mod, b_mod, mix_pre_norm, mix_post_norm, w_in, q_norm, w_q_up,
              kv_norm, w_kv_up, ssd_conv_w, ssd_conv_b, ssd_a_log, ssd_dt_bias, ssd_d, ssd_norm, w_out,
              ffn_pre_norm, ffn_post_norm, w_up, ffn_conv_w, ffn_conv_b, w_down):
    bsz, seq, _ = x.shape
    cos, sin = axial_rope_tables(seq)
    cos_q, sin_q = cos[:, None, :], sin[:, None, :]

    def flip(t):
        return jnp.flip(t, axis=1)

    for l in range(DEPTH_2):
        last = l == DEPTH_2 - 1
        mod_x = jnp.split((jax.nn.silu(c) @ w_mod[l] + b_mod[l])[:, None, :], N_MOD_2, axis=-1)
        mod_c = jnp.split((jax.nn.silu(c_ctx) @ w_mod[l] + b_mod[l])[None, None, :], N_MOD_2, axis=-1)

        cq_x, ckv_x, kr_x, z_x, xbc_x, dt_x = in_split(
            modulate(rms_norm(x, mix_pre_norm[l]), mod_x[0], mod_x[1]) @ w_in[l])
        cq_c, ckv_c, kr_c, z_c, xbc_c, dt_c = in_split(
            modulate(rms_norm(ctx, mix_pre_norm[l]), mod_c[0], mod_c[1]) @ w_in[l])

        q_nope_x, q_rope_x = mla_queries(cq_x, q_norm[l], w_q_up[l])
        q_rope_x = apply_rope(q_rope_x, cos_q, sin_q)
        k_nope_x, v_x = mla_keys_values(ckv_x, kv_norm[l], w_kv_up[l])
        k_rope_x = apply_rope(kr_x, cos, sin)
        k_nope_c, v_c = mla_keys_values(ckv_c, kv_norm[l], w_kv_up[l])
        attn_x = latent_attention(q_nope_x, q_rope_x,
                                  jnp.concatenate([k_nope_c, k_nope_x], axis=1),
                                  jnp.concatenate([kr_c, k_rope_x], axis=1),
                                  jnp.concatenate([v_c, v_x], axis=1))

        A = -jnp.exp(ssd_a_log[l].astype(jnp.float32)).reshape(2, SSD_GROUPS, HEADS_PER_GROUP)
        xs_x, b_x, c_x, dtv_x = ssd_prepare(xbc_x, dt_x, ssd_conv_w[l], ssd_conv_b[l], ssd_dt_bias[l])
        xs_c, b_c, c_c, dtv_c = ssd_prepare(xbc_c, dt_c, ssd_conv_w[l], ssd_conv_b[l], ssd_dt_bias[l])
        zero_state = jnp.zeros((bsz, SSD_GROUPS, HEADS_PER_GROUP, SSD_HEAD_DIM, SSD_STATE), xs_x.dtype)
        st_cf = ssd_states(xs_c, dtv_c[:, :, 0], A[0], b_c, c_c, zero_state)
        st_cb = ssd_states(flip(xs_c), flip(dtv_c[:, :, 1]), A[1], flip(b_c), flip(c_c), zero_state)
        st_xf = ssd_states(xs_x, dtv_x[:, :, 0], A[0], b_x, c_x, st_cf[2])
        st_xb = ssd_states(flip(xs_x), flip(dtv_x[:, :, 1]), A[1], flip(b_x), flip(c_x), st_cb[2])
        y_x = ssd_output(st_xf[0], st_xf[1]) + flip(ssd_output(st_xb[0], st_xb[1]))
        ssd_x = ssd_finish(y_x, xs_x, z_x, ssd_d[l], ssd_norm[l])

        mix_x = jnp.concatenate([attn_x, ssd_x], axis=-1) @ w_out[l]
        x = x + mod_x[2] * rms_norm(mix_x, mix_post_norm[l])

        if not last:
            q_nope_c, q_rope_c = mla_queries(cq_c, q_norm[l], w_q_up[l])
            attn_c = attend(q_nope_c, q_rope_c, k_nope_c, kr_c, v_c).reshape(bsz, -1, ATTN_WIDTH)
            y_c = ssd_output(st_cf[0], st_cf[1]) + flip(ssd_output(st_cb[0], st_cb[1]))
            ssd_c = ssd_finish(y_c, xs_c, z_c, ssd_d[l], ssd_norm[l])
            mix_c = jnp.concatenate([attn_c, ssd_c], axis=-1) @ w_out[l]
            ctx = ctx + mod_c[2] * rms_norm(mix_c, mix_post_norm[l])
            ffn_c = conv_glu(modulate(rms_norm(ctx, ffn_pre_norm[l]), mod_c[3], mod_c[4]),
                             w_up[l], ffn_conv_w[l], ffn_conv_b[l], w_down[l])
            ctx = ctx + mod_c[5] * rms_norm(ffn_c, ffn_post_norm[l])

        ffn_x = conv_glu(modulate(rms_norm(x, ffn_pre_norm[l]), mod_x[3], mod_x[4]),
                         w_up[l], ffn_conv_w[l], ffn_conv_b[l], w_down[l])
        x = x + mod_x[5] * rms_norm(ffn_x, ffn_post_norm[l])
    return x


def setup_inputs(seed=0):
    out = dict(first_inputs(seed))
    for name, value in second_inputs(seed + 1).items():
        if name != "x":
            out[name + "_2"] = value
    return out


def reference(
    x, c, ctx, c_ctx, ada_w, ada_b, ffn_w_in, ffn_w_out, even_w_in, even_w_out, mlstm_conv,
    mlstm_gate_b, mlstm_norm, sgu_norm, sgu_ws, sgu_b, odd_w_qkv, odd_w_out, attn_sink,
    final_norm, c_2, ctx_2, c_ctx_2, w_mod_2, b_mod_2, mix_pre_norm_2, mix_post_norm_2, w_in_2,
    q_norm_2, w_q_up_2, kv_norm_2, w_kv_up_2, ssd_conv_w_2, ssd_conv_b_2, ssd_a_log_2,
    ssd_dt_bias_2, ssd_d_2, ssd_norm_2, w_out_2, ffn_pre_norm_2, ffn_post_norm_2, w_up_2,
    ffn_conv_w_2, ffn_conv_b_2, w_down_2,
):
    x = first_block(
        x, c, ctx, c_ctx, ada_w, ada_b, ffn_w_in, ffn_w_out, even_w_in, even_w_out, mlstm_conv,
        mlstm_gate_b, mlstm_norm, sgu_norm, sgu_ws, sgu_b, odd_w_qkv, odd_w_out, attn_sink,
        final_norm,
    )
    return second_block(
        x, c_2, ctx_2, c_ctx_2, w_mod_2, b_mod_2, mix_pre_norm_2, mix_post_norm_2, w_in_2,
        q_norm_2, w_q_up_2, kv_norm_2, w_kv_up_2, ssd_conv_w_2, ssd_conv_b_2, ssd_a_log_2,
        ssd_dt_bias_2, ssd_d_2, ssd_norm_2, w_out_2, ffn_pre_norm_2, ffn_post_norm_2, w_up_2,
        ffn_conv_w_2, ffn_conv_b_2, w_down_2,
    )


_drawn_inputs = setup_inputs


def setup_inputs(seed=0):
    import zlib

    import numpy as np

    out = dict(_drawn_inputs(seed))
    spreads = {}
    factors = {'mlstm_norm': 8.0,
     'sgu_norm': 6.77,
     'sgu_b': 3.428,
     'attn_sink': 25.867,
     'q_norm_2': 8.0,
     'ssd_conv_b_2': 5.676,
     'ssd_d_2': 7.098,
     'ffn_conv_b_2': 8.0}
    for name, (base, spread) in spreads.items():
        noise = np.random.default_rng([zlib.crc32(name.encode()), seed]).standard_normal(out[name].shape)
        drawn = base * np.exp(spread * noise) if base else spread * noise
        out[name] = __import__('jax').numpy.asarray(drawn.astype(out[name].dtype))
    for name, factor in factors.items():
        out[name] = (out[name] * factor).astype(out[name].dtype)
    return out
```

```python
from contextlib import ExitStack

import numpy as np

import concourse.bass as bass
from concourse import mybir

ALU = mybir.AluOpType
ACT = mybir.ActivationFunctionType
AX = mybir.AxisListType
F32 = mybir.dt.float32
F32R = mybir.dt.float32r

P = 128
D = 1024
KD = D // P
SEQ = 256
TOK = 2 * SEQ
TT = TOK // P
X_TILES = SEQ // P
EPS = 1e-6
F = 2816
KF = F // P
N_MOD = 9
N_MOD_2 = 6

HEADS = 4
HEAD = 128
W_A = HEADS * HEAD
GROUPS_B = 4
W_B = GROUPS_B * P

C_HEADS = 16
C_KV = 4
C_DIM = 64
ROPE_BASE = 10000.0
GRID_W = 64

M_HEADS = 16
NOPE = 64
ROPE = 32
QD = NOPE + ROPE
V_DIM = 64
Q_RANK = 384
KV_RANK = 256
HEADS_AT_ONCE = 4

S_HEADS = 16
S_DIM = 64
S_GROUPS = 2
S_STATE = 128
S_PER = S_HEADS // S_GROUPS
D_INNER = S_HEADS * S_DIM
S_CONV = 5

MASKED = -1e30
CHUNK = 2048
RAW_SLOTS = 4
SPLIT_SLOTS = 3
A_SLOTS = 12
TEMPS = 6

VECTORS = {}
N_VECTORS = 0
for _name, _n in (("ada_b", 2 * N_MOD * KD), ("b_mod", N_MOD_2 * KD), ("conv", 3 * 8), ("mnorm", 4),
                  ("sgu", 4), ("final", KD), ("mix_pre", KD), ("mix_post", KD), ("q_norm", 3),
                  ("kv_norm", 2), ("sconv_w", S_CONV * 12), ("sconv_b", 12), ("ssd_norm", KD),
                  ("ssd_d", KD), ("ffn_pre", KD), ("ffn_post", KD), ("fconv_w", 3 * KF), ("fconv_b", KF),
                  ("c", 4 * KD), ("gate_b", 16), ("sink", 16), ("dt_b", 32), ("a_log", 32)):
    VECTORS[_name] = (N_VECTORS, _n)
    N_VECTORS += _n

MATRICES = ["ident", "tri_f", "tri_b", "mask_f", "mask_b", "ones", "swap", "turn", "sum_groups"]


def shape_constants():
    i = np.arange(P)
    le = (i[:, None] <= i[None, :]).astype(np.float32)
    swap = np.zeros((P, P), np.float32)
    swap[i[1::2], i[0::2]] = -1.0
    swap[i[0::2], i[1::2]] = 1.0
    turn = np.zeros((P, P), np.float32)
    for base in (NOPE, NOPE + 16):
        for j in range(8):
            turn[base + 8 + j, base + j] = -1.0
            turn[base + j, base + 8 + j] = 1.0
    sum_groups = np.zeros((P, P), np.float32)
    for g in range(4):
        sum_groups[32 * g, 0] = sum_groups[32 * g + 1, 1] = 1.0
    mats = {"ident": np.eye(P, dtype=np.float32), "tri_f": le, "tri_b": le.T,
            "mask_f": np.where(le > 0, 0, MASKED), "mask_b": np.where(le.T > 0, 0, MASKED),
            "ones": np.ones((P, P)), "swap": swap, "turn": turn, "sum_groups": sum_groups}
    square = np.concatenate([mats[m] for m in MATRICES], axis=1).astype(np.float32)

    row = (np.arange(SEQ) // GRID_W).astype(np.float32)
    col = (np.arange(SEQ) % GRID_W).astype(np.float32)
    n_freq = C_DIM // 4
    inv = np.float32(ROPE_BASE) ** (-np.arange(n_freq, dtype=np.float32) / np.float32(n_freq))
    ang = np.concatenate([row[:, None] * inv, col[:, None] * inv], axis=1)
    ang = np.repeat(ang, 2, axis=1).T
    ang = np.concatenate([ang, ang], axis=0)
    q = np.arange(SEQ)
    near = np.where(np.abs(q[:, None] - q[None, :]) <= P, 0.0, MASKED)
    odd = np.concatenate([np.cos(ang), np.sin(ang), near[:P], near[P:]], axis=1).astype(np.float32)

    axis = ROPE // 2
    inv = np.float32(ROPE_BASE) ** (-np.arange(0, axis, 2, dtype=np.float32) / np.float32(axis))
    ar, ac = row[:, None] * inv, col[:, None] * inv
    ang = np.concatenate([ar, ar, ac, ac], axis=1).T
    mla = np.zeros((P, 2 * SEQ), np.float32)
    mla[:NOPE, :SEQ] = 1.0
    mla[NOPE:QD, :SEQ] = np.cos(ang)
    mla[NOPE:QD, SEQ:] = np.sin(ang)
    return square, odd, mla


class Mark:

    def __init__(self, semaphore, value):
        self.semaphore, self.value = semaphore, value


class Line:

    def __init__(self, semaphore):
        self.semaphore, self.count, self.steps, self.passed = semaphore, 0, [], {}

    def wait(self, *marks):
        for m in marks:
            if m is None:
                continue
            if isinstance(m, (list, tuple)):
                self.wait(*m)
                continue
            if self.passed.get(id(m.semaphore), 0) < m.value:
                self.passed[id(m.semaphore)] = m.value
                self.steps.append((None, m.semaphore, m.value))

    def do(self, emit, *after, counted=True):
        self.wait(*after)
        if counted:
            self.count += 1
            self.steps.append((emit, self.semaphore, 1))
        else:
            self.steps.append((emit, None, 0))
        return Mark(self.semaphore, self.count)

    def load(self, out, in_, semaphore, value, *after):
        self.wait(*after)
        self.steps.append((lambda e: e.dma_start(out, in_), semaphore, 16))
        return Mark(semaphore, value)

    def last(self):
        return Mark(self.semaphore, self.count)

    def run(self, engine):
        for emit, semaphore, n in self.steps:
            if emit is None:
                engine.wait_ge(semaphore, n)
            elif semaphore is None:
                emit(engine)
            else:
                emit(engine).then_inc(semaphore, n)


class Buffers:

    def __init__(self, buffers):
        self.free = [(b, ()) for b in buffers]

    def take(self):
        return self.free.pop(0)

    def give(self, buffer, *marks):
        self.free.append((buffer, marks))


class Chunk:
    pass


class Program:
    def __init__(self, nc, dram, mem, sems, order):
        self.nc, self.dram, self.mem, self.sems = nc, dram, mem, sems
        self.PE, self.ACT, self.DVE, self.SP, self.POOL = (Line(sems[n]) for n in ("pe", "act", "dve", "sp", "pool"))
        self.banks = Buffers(mem["banks"])
        self.temps = Buffers(mem["temps"])
        self.order = order
        self.asked = []
        self.loaded = self.prepared = self.finished = 0
        self.chunks = {}
        self.raw_free = [None] * RAW_SLOTS
        self.split_free = [None] * SPLIT_SLOTS
        self.n_split = 0
        self.split_done = 0
        self.a_free = [None] * A_SLOTS
        self.a_next = 0
        self.side = []

    def tt(self, out, a, b, op, *after, line=None):
        return (line or self.DVE).do(lambda e: e.tensor_tensor(out, a, b, op), *after)

    def copy(self, out, a, *after):
        return self.DVE.do(lambda e: e.tensor_copy(out, a), *after)

    def ts(self, out, a, s1, s2, op0, op1, *after):
        if op1 is None:
            return self.DVE.do(lambda e: e.tensor_scalar(out, a, s1, None, op0), *after)
        return self.DVE.do(lambda e: e.tensor_scalar(out, a, s1, s2, op0, op1), *after)

    def stt(self, out, a, s, b, op0, op1, *after):
        return self.DVE.do(lambda e: e.scalar_tensor_tensor(out=out, in0=a, scalar=s, in1=b, op0=op0, op1=op1),
                           *after)

    def act(self, out, in_, func, *after, **kw):
        return self.ACT.do(lambda e: e.activation(out, in_, func, **kw), *after)

    def mm(self, out, lhs, rhs, start, stop, *after, counted=False):
        return self.PE.do(lambda e: e.matmul(out, lhs, rhs, start=start, stop=stop, skip_group_check=True),
                          *after, counted=counted)

    def turn(self, out, in_, *after, counted=False):
        ident = self.mat("ident")[0:in_.shape[0], 0:in_.shape[0]]
        return self.PE.do(lambda e: e.transpose(out, in_, ident), *after, counted=counted)

    def mm3(self, out, w, x, start, stop, *after, counted=False):
        (wh, wl), (xh, xl) = w, x
        self.mm(out, wh, xh, start, False, *after)
        self.mm(out, wh, xl, False, False)
        return self.mm(out, wl, xh, False, stop, counted=counted)

    def split(self, hi, lo, value, *after):
        m = self.act(hi, value, ACT.Copy, *after)
        return self.tt(lo, value, hi.bitcast(F32), ALU.subtract, m, *after)

    def vec(self, name, i=0, n=1):
        at = VECTORS[name][0] + i
        return self.mem["vectors"][:, at:at + n]

    def mat(self, name):
        at = MATRICES.index(name) * P
        return self.mem["matrices"][:, at:at + P]

    def barrier(self):
        marks = [x.last() for x in (self.PE, self.ACT, self.DVE, self.POOL) if x.count]
        for x in (self.PE, self.ACT, self.DVE, self.POOL, self.SP):
            x.wait(*marks)
        return marks

    def load_ahead(self):
        while self.loaded < len(self.order):
            i = self.loaded
            name, at, width, _ = self.order[i]
            slot = i % RAW_SLOTS
            if i >= RAW_SLOTS and self.raw_free[slot] is None:
                return
            free = self.raw_free[slot]
            self.raw_free[slot] = None
            raw = self.mem["raw"][slot][:, 0:width]
            c = Chunk()
            c.index, c.raw = i, raw
            c.landed = self.SP.load(raw, self.dram[name][at, :, 0:width], self.sems["raw"][slot],
                                    16 * (i // RAW_SLOTS + 1), free)
            self.chunks[i] = c
            self.loaded += 1

    def prepare(self, i):
        name, at, width, parts = self.order[i]
        c = self.chunks[i]
        slot = i % RAW_SLOTS
        if not parts:
            c.ready = c.landed
            return
        s = self.n_split % SPLIT_SLOTS
        self.n_split += 1
        c.split_slot = s
        c.hi, c.lo = self.mem["w_hi"][s][:, 0:width], self.mem["w_lo"][s][:, 0:width]
        c.ready = self.split(c.hi, c.lo, c.raw, c.landed, self.split_free[s])
        self.raw_free[slot] = c.ready

    def next_chunk(self, name, at, width, parts=True):
        i = len(self.asked)
        self.asked.append((name, at, width, parts))
        if self.order is None:
            c = Chunk()
            c.hi = c.lo = None
            c.raw = self.mem["raw"][0][:, 0:width]
            c.hi, c.lo = self.mem["w_hi"][0][:, 0:width], self.mem["w_lo"][0][:, 0:width]
            c.ready = None
            c.index = i
            return c
        assert self.order[i] == (name, at, width, parts)
        self.load_ahead()
        while self.prepared < len(self.order) and self.prepared <= i + 2:
            if self.prepared >= self.loaded:
                break
            if self.order[self.prepared][3]:
                if self.n_split - self.split_done >= SPLIT_SLOTS:
                    break
            self.prepare(self.prepared)
            self.prepared += 1
            self.load_ahead()
        assert self.prepared > i, "chunk is not ready"
        return self.chunks[i]

    def done_with(self, c, mark):
        if self.order is None:
            return
        if self.order[c.index][3]:
            self.split_free[c.split_slot] = mark
            self.split_done += 1
        else:
            self.raw_free[c.index % RAW_SLOTS] = mark

    def modulation(self, name, k, pair, dest, bias, sections):
        per = D // 256
        self.side += [(name, k, sec, q, pair, dest, bias, sections) for sec in sections for q in range(per)]

    def side_step(self, n=1):
        for _ in range(n):
            if not self.side:
                return
            name, k, sec, q, pair, dest, bias, _ = self.side.pop(0)
            chunk = self.next_chunk(name, k + sec * 4 + q, CHUNK, parts=False)
            w = chunk.raw.rearrange("p (k n) -> p k n", k=KD)
            bank, free = self.banks.take()
            for kt in range(KD):
                g = kt % 4
                m = self.mm(bank[32 * g:32 * g + 32, 0:256], self.mem["silu_c"][:, pair, kt, :], w[:, kt, :],
                            kt < 4, kt >= 4, chunk.ready, free, self.silu_c_ready, counted=kt == KD - 1)
            self.done_with(chunk, m)
            row, row_free = self.temps.take()
            m = self.act(row[:, 0:256], bank[:, 0:256], ACT.Copy, m, row_free)
            self.banks.give(bank, m)
            self.end_side()
            self.side_open = (row, m, dest, bias, sec * KD + 2 * q)

    side_open = None

    def end_side(self):
        if self.side_open is None:
            return
        row, ready, dest, bias, at = self.side_open
        self.side_open = None
        bank, free = self.banks.take()
        for j in range(2):
            m = self.mm(bank[:, 2 * j:2 * j + 2], row[:, j * P:(j + 1) * P], self.mat("sum_groups")[:, 0:2],
                        True, True, ready, free, counted=j == 1)
        self.temps.give(row, m)
        m = self.tt(dest[:, at:at + 2, :], bank[:, 0:4].rearrange("p (j s) -> p j s", j=2),
                    self.vec(bias[0], bias[1] + at, 2).unsqueeze(2).broadcast_to((P, 2, 2)), ALU.add, m)
        self.banks.give(bank, m)

    def section(self, dest, sec, op, value):
        view = dest[:, sec * KD:(sec + 1) * KD, :]
        return self.ts(view, view, value, None, op, None, self.DVE.last())

    def finish_side(self):
        while self.side:
            self.side_step()
        self.end_side()

    def square_sum(self, tiles, n, *after):
        bank, free = self.banks.take()
        for i, t in enumerate(tiles):
            sq, sq_free = self.temps.take()
            m = self.act(sq[0:t.shape[0], 0:n], t, ACT.Square, sq_free, *after)
            m = self.mm(bank[:, 0:n], self.mat("ones")[0:t.shape[0], :], sq[0:t.shape[0], 0:n], i == 0,
                        i == len(tiles) - 1, m, free, counted=True)
            self.temps.give(sq, m)
        return bank, m

    def rstd(self, out, total, width, *after):
        eps = self.mem["eps"][0:out.shape[0], 0:1]
        m = self.act(out, total, ACT.Sqrt, *after, scale=1.0 / width, bias=eps)
        return self.DVE.do(lambda e: e.reciprocal(out, out), m)

    def norm(self, scale, shift, n, *after):
        h, n_hi, n_lo = self.mem["h"], self.mem["n_hi"], self.mem["n_lo"]
        bank, m = self.square_sum([h[:, k, 0:n] for k in range(KD)], n, *after)
        inv, free = self.temps.take()
        m = self.rstd(inv[:, 0:n], bank[:, 0:n], D, m, free)
        self.banks.give(bank, m)
        ready = []
        for k in range(KD):
            t, free = self.temps.take()
            for s in range(n // SEQ):
                at = slice(s * SEQ, (s + 1) * SEQ)
                a = self.stt(t[:, at], h[:, k, at], scale(k, s), inv[:, at], ALU.mult, ALU.mult, m, free)
                b = self.act(n_hi[:, k, at], t[:, at], ACT.Identity, a, bias=shift(k, s))
                c = self.stt(n_lo[:, k, at], t[:, at], shift(k, s), n_hi[:, k, at].bitcast(F32), ALU.add,
                             ALU.subtract, b)
            self.temps.give(t, c)
            ready.append(c)
        self.temps.give(inv, c)
        return ready

    def mod_scale(self, dest, sec):
        return lambda k, s: dest[:, sec * KD + k, s:s + 1]

    def project(self, name, at, ktiles, cols, n, sources, ready, finish, first=True, last=True,
                banks=None, tokens=False, col0=0):
        chunk = self.next_chunk(name, at, ktiles * cols)
        hi = chunk.hi.rearrange("p (k n) -> p k n", k=ktiles)
        lo = chunk.lo.rearrange("p (k n) -> p k n", k=ktiles)
        out = []
        for t in range(cols // P):
            bank, free = self.banks.take() if banks is None else banks[t]
            for k in range(ktiles):
                c = slice(t * P, (t + 1) * P)
                xh, xl = sources(k)
                m = self.mm3(bank[:, 0:n], (hi[:, k, c], lo[:, k, c]), (xh, xl), first and k == 0,
                             last and k == ktiles - 1, chunk.ready, free, ready[k] if ready else None,
                             counted=k == ktiles - 1)
            out.append((bank, m))
        self.done_with(chunk, m)
        if last:
            for t, (bank, m) in enumerate(out):
                finish(t, bank, m)
        return out

    def project_tokens(self, name, at, ktiles, cols, tiles, sources, ready, finish, view=None):
        chunk = self.next_chunk(name, at, ktiles * cols) if view is None else view
        hi = chunk.hi.rearrange("p (k n) -> p k n", k=ktiles)
        lo = chunk.lo.rearrange("p (k n) -> p k n", k=ktiles)
        for pair in range(len(tiles) // 2):
            bank, free = self.banks.take()
            for j in range(2):
                tt = tiles[2 * pair + j]
                for k in range(ktiles):
                    xh, xl = sources(k, tt)
                    m = self.mm3(bank[:, j * cols:(j + 1) * cols], (xh, xl), (hi[:, k, :], lo[:, k, :]), k == 0,
                                 k == ktiles - 1, chunk.ready, free, ready[k] if ready else None,
                                 counted=k == ktiles - 1)
            if pair == len(tiles) // 2 - 1:
                self.done_with(chunk, m)
            finish(pair, bank, m)

    def n_parts(self, k, n=TOK):
        return self.mem["n_hi"][:, k, 0:n], self.mem["n_lo"][:, k, 0:n]

    def add_gated(self, bank, m, k, gate, n):
        h = self.mem["h"]
        for s in range(n // SEQ):
            at = slice(s * SEQ, (s + 1) * SEQ)
            e = self.stt(h[:, k, at], bank[:, at], gate(k, s), h[:, k, at], ALU.mult, ALU.add, m)
        self.banks.give(bank, e)
        self.h_ready[k] = e

    def ffn(self, w_in, w_out, dest, secs, n):
        ready = self.norm(self.mod_scale(dest, secs[1]), self.mod_scale(dest, secs[0]), n, self.h_ready)
        self.hidden(w_in, w_out, n, ready, self.silu_gate,
                    lambda k, bank, m: self.add_gated(bank, m, k, self.mod_scale(dest, secs[2]), n))

    def silu_gate(self, j, n, g_bank, g_mark, u_bank, u_mark):
        t, free = self.temps.take()
        m = self.act(t[:, 0:n], g_bank[:, 0:n], ACT.Silu, g_mark, free)
        self.banks.give(g_bank, m)
        m = self.tt(t[:, 0:n], t[:, 0:n], u_bank[:, 0:n], ALU.mult, m, u_mark)
        self.banks.give(u_bank, m)
        return t, m

    def hidden(self, w_in, w_out, n, ready, gate, finish):
        a_hi, a_lo = self.mem["a_hi"], self.mem["a_lo"]
        placed = {}

        def inward(j):
            found = {}
            self.side_step()
            self.project(w_in[0], w_in[1] + j, KD, 2 * P, n, lambda k: self.n_parts(k, n), ready,
                         lambda t, bank, m: found.__setitem__(t, (bank, m)))
            t, m = gate(j, n, *found[0], *found[1])
            slot = self.a_next % A_SLOTS
            self.a_next += 1
            e = self.split(a_hi[:, slot, 0:n], a_lo[:, slot, 0:n], t[:, 0:n], m, self.a_free[slot])
            self.temps.give(t, e)
            placed[j] = (slot, e)

        def outward(half):
            tiles = list(range(half * (KF // 2), (half + 1) * (KF // 2)))
            parts = [tiles[0:6], tiles[6:11]]
            for q in range(D // 256):
                banks = None
                for i, part in enumerate(parts):
                    at = w_out[1] + (half * (D // 256) + q) * 2 + i
                    banks = self.project(w_out[0], at, len(part), 256, n,
                                         lambda k: (a_hi[:, placed[part[k]][0], 0:n], a_lo[:, placed[part[k]][0], 0:n]),
                                         [placed[j][1] for j in part],
                                         lambda t, bank, m: finish(2 * q + t, bank, m),
                                         first=i == 0, last=i == 1,
                                         banks=None if banks is None else [(b, mk) for b, mk in banks])
            for j in tiles:
                self.a_free[placed[j][0]] = self.PE.last()

        half = KF // 2
        for j in range(half + 1):
            inward(j)
        outward(0)
        for j in range(half + 1, KF):
            inward(j)
        outward(1)

    def even_mixer(self, dest):
        mem = self.mem
        n = TOK
        ready = self.norm(self.mod_scale(dest, 4), self.mod_scale(dest, 3), n, self.h_ready)
        self.finish_side()
        self.barrier()
        q_t, k_t, v, o_t, u_t, vb = (mem[x] for x in ("e_q", "e_k", "e_v", "e_o", "e_u", "e_vb"))
        tables = self.SP.load(mem["stage"][:, :], self.dram["even_tables"], self.sems["stage"], 16)
        ws_t = mem["stage"][:, 0:4 * P].rearrange("q (g p) -> q g p", g=GROUPS_B)
        sb = mem["stage"][:, 4 * P:8 * P].rearrange("c (g p) -> c g p", g=GROUPS_B)
        src = lambda k: self.n_parts(k)
        src_t = lambda k, tt: (mem["n_hi"][:, k, tt * P:(tt + 1) * P], mem["n_lo"][:, k, tt * P:(tt + 1) * P])

        def conv(base, out):
            def finish(t, bank, m):
                tile = base + t
                x, free = self.temps.take()
                xv = x[:, :].rearrange("p (s t) -> p s t", s=2)
                bv = bank[:, :].rearrange("p (s t) -> p s t", s=2)
                w = lambda tap: self.vec("conv", tap * 8 + tile)
                m = self.act(x[:, :], bank[:, :], ACT.Copy, m, free, scale=w(1))
                m = self.stt(xv[:, :, 1:SEQ], bv[:, :, 0:SEQ - 1], w(0), xv[:, :, 1:SEQ], ALU.mult, ALU.add, m)
                m = self.stt(xv[:, :, 0:SEQ - 1], bv[:, :, 1:SEQ], w(2), xv[:, :, 0:SEQ - 1], ALU.mult, ALU.add, m)
                self.banks.give(bank, m)
                m = self.act(out[:, tile % 4, :], x[:, :], ACT.Silu, m)
                self.temps.give(x, m)
            return finish

        for c in range(4):
            self.project("even_in", c, KD, 256, n, src, ready, conv(2 * c, q_t if c < 2 else k_t))
        for c in range(2):
            def store_v(pair, bank, m, c=c):
                m = self.act(v[:, 2 * pair:2 * pair + 2, c * 256:(c + 1) * 256],
                             bank[:, :].rearrange("p (t n) -> p t n", t=2), ACT.Copy, m)
                self.banks.give(bank, m)
            self.project_tokens("even_in", 4 + c, KD, 256, range(TT), src_t, ready, store_v)
        for c in range(2):
            def store_o(t, bank, m, c=c):
                self.banks.give(bank, self.act(o_t[:, 2 * c + t, :], bank[:, :], ACT.Sigmoid, m))
            self.project("even_in", 6 + c, KD, 256, n, src, ready, store_o)
        small = mem["small"]
        gates = small[:, 0:TT * 16].rearrange("p (t g) -> p t g", t=TT)
        gate_marks = []

        def store_gates(pair, bank, m):
            e = self.tt(gates[:, 2 * pair:2 * pair + 2, :], bank[:, 0:32].rearrange("p (t g) -> p t g", t=2),
                        self.vec("gate_b", 0, 16).unsqueeze(1).broadcast_to((P, 2, 16)), ALU.add, m)
            self.banks.give(bank, e)
            gate_marks.append(e)
        self.project_tokens("even_gates", 0, KD, 16, range(TT), src_t, ready, store_gates)
        for c in range(2):
            def store_u(t, bank, m, c=c):
                self.banks.give(bank, self.act(u_t[:, 2 * c + t, :], bank[:, :], ACT.Gelu_apprx_tanh, m))
            self.project("even_in", 8 + c, KD, 256, n, src, ready, store_u)
        for c in range(2):
            def store_vb(pair, bank, m, c=c):
                m = self.act(vb[:, 2 * pair:2 * pair + 2, c * 256:(c + 1) * 256],
                             bank[:, :].rearrange("p (t n) -> p t n", t=2), ACT.Gelu_apprx_tanh, m)
                self.banks.give(bank, m)
            self.project_tokens("even_in", 10 + c, KD, 256, range(TT), src_t, ready, store_vb)

        ss = small[:, 64:64 + TT]
        for tt in range(TT):
            sq, free = self.temps.take()
            m = self.act(sq[:, :], vb[:, tt, :], ACT.Square, free, self.ACT.last(), accum_out=ss[:, tt:tt + 1])
            self.temps.give(sq, m)
        m = self.rstd(ss, ss, W_B, m)
        for tt in range(TT):
            m2 = self.ts(vb[:, tt, :], vb[:, tt, :], ss[:, tt:tt + 1], None, ALU.mult, None, m)
        b_done = []
        n_read = self.PE.last()
        for g in range(GROUPS_B):
            bank, free = self.banks.take()
            for tt in range(TT):
                m = self.mm(bank[:, tt * P:(tt + 1) * P], vb[:, tt, g * P:(g + 1) * P], ws_t[:, g, :], True, True,
                            m2, tables, free, counted=tt == TT - 1)
            t, free = self.temps.take()
            m = self.stt(t[:, :].rearrange("p (t c) -> p t c", t=TT), bank[:, :].rearrange("p (t c) -> p t c", t=TT),
                         self.vec("sgu", g), sb[:, g, :].unsqueeze(1).broadcast_to((P, TT, P)), ALU.mult, ALU.add,
                         m, free)
            self.banks.give(bank, m)
            m = self.tt(t[:, :], t[:, :], u_t[:, g, :], ALU.mult, m, self.ACT.last())
            m = self.split(mem["n_hi"][:, 4 + g, :], mem["n_lo"][:, 4 + g, :], t[:, :], m, n_read)
            self.temps.give(t, m)
            b_done.append(m)

        self.barrier()
        gv = gates.rearrange("p t (d w h) -> p t d w h", d=2, w=2)
        lf = small[:, 96:96 + 8 * TT].rearrange("p (t d h) -> p t d h", t=TT, d=2)
        e1 = small[:, 128:128 + 8 * TT].rearrange("p (t d h) -> p t d h", t=TT, d=2)
        c_col = small[:, 160:160 + 8 * TT].rearrange("p (t d h) -> p t d h", t=TT, d=2)
        for tt in range(TT):
            m = self.log_one_plus_exp(lf[:, tt], e1[:, tt], gv[:, tt, :, 1, :], -1.0, gate_marks,
                                      small[:, 192:200].rearrange("p (d h) -> p d h", d=2))
        m = self.ts(lf, lf, -1.0, None, ALU.mult, None, m)
        bank, free = self.banks.take()
        bv = bank[:, 0:8 * TT].rearrange("p (t d h) -> p t d h", t=TT, d=2)
        for tt in range(TT):
            for d in range(2):
                tri = self.mat(("tri_f", "tri_b")[d])
                m2 = self.mm(bv[:, tt, d, :], tri, lf[:, tt, d, :], True, True, m, free, counted=True)
        m = self.tt(c_col, gv[:, :, :, 0, :], bv, ALU.subtract, m2)
        self.banks.give(bank, m)
        self.mlstm(q_t, k_t, v, lf, c_col, m)

        h_sum = mem["e_vb"][:, :, :]
        for h in range(HEADS):
            bank, m = self.square_sum([h_sum[:, h, :]], n, self.DVE.last())
            inv, free = self.temps.take()
            m = self.rstd(inv[:, :], bank[:, :], HEAD, m, free)
            self.banks.give(bank, m)
            m = self.tt(inv[:, :], inv[:, :], h_sum[:, h, :], ALU.mult, m)
            m = self.stt(inv[:, :], inv[:, :], self.vec("mnorm", h), o_t[:, h, :], ALU.mult, ALU.mult, m)
            m = self.split(mem["n_hi"][:, h, :], mem["n_lo"][:, h, :], inv[:, :], m, self.PE.last())
            self.temps.give(inv, m)
        for c in range(4):
            self.project("even_out", c, KD, 256, n, src, [m] * KD,
                         lambda t, bank, mk, c=c: self.add_gated(bank, mk, 2 * c + t, self.mod_scale(dest, 5), n))
        self.barrier()

    def log_one_plus_exp(self, out, e1, x, sign, after, tmp):
        m = self.ts(tmp, x, -1.0, None, ALU.mult, None, *after, self.DVE.last())
        m = self.tt(e1, tmp, x, ALU.min, m)
        m = self.act(e1, e1, ACT.Exp, m)
        m = self.ts(tmp, e1, 1.0, None, ALU.add, None, m)
        ln = self.act(out, tmp, ACT.Ln, m)
        m = self.stt(e1, tmp, 1.0, e1, ALU.subtract, ALU.subtract, m)
        r = self.DVE.do(lambda e: e.reciprocal(tmp, tmp), m, ln)
        m = self.tt(e1, e1, tmp, ALU.mult, r)
        m = self.tt(out, out, e1, ALU.subtract, m, ln)
        m = self.ts(tmp, x, sign, 0.0, ALU.mult, ALU.max, m)
        return self.tt(out, out, tmp, ALU.add, m)

    def mlstm(self, q_t, k_t, v, lf, c_col, m_cols):
        mem, small = self.mem, self.mem["small"]
        h_sum = mem["e_vb"]
        scale = HEAD ** -0.5
        order = ([2, 3, 0, 1], [3, 2, 1, 0])
        state = [mem["e_c0"], mem["e_c1"]]
        n_state = [small[:, 200 + 4 * d:204 + 4 * d] for d in range(2)]
        m_state = [small[:, 208 + 4 * d:212 + 4 * d] for d in range(2)]
        wide = lambda ap: ap.rearrange("p (h t) -> p h t", h=HEADS)
        ones = self.mat("ones")
        extra = Buffers(mem["e_extra"])
        m_ready = [self.DVE.do(lambda e, d=d: e.memset(m_state[d], 0.0), m_cols) for d in range(2)]
        s_ready = [None, None]
        h_written = {}
        for step in range(TT):
            for d in range(2):
                tt = order[d][step]
                cols = slice(tt * P, (tt + 1) * P)
                tri, mask = self.mat(("tri_f", "tri_b")[d]), self.mat(("mask_f", "mask_b")[d])
                end = P - 1 if d == 0 else 0
                b_bank, b_free = self.banks.take()
                c_bank, c_free = self.banks.take()
                for h in range(HEADS):
                    at = slice(h * P, (h + 1) * P)
                    mb = self.mm(b_bank[:, at], lf[:, tt, d, h:h + 1].broadcast_to((P, P)), tri, True, True,
                                 b_free, m_cols)
                    mc = self.mm(c_bank[:, at], c_col[:, tt, d, h:h + 1].broadcast_to((P, P)), self.mat("ident"),
                                 True, True, c_free, m_cols, counted=h == HEADS - 1)
                big_m, free = self.temps.take()
                for h in range(HEADS):
                    o, i = big_m[:, h * P:(h + 1) * P], c_bank[:, h * P:(h + 1) * P]
                    if d == 1:
                        o, i = o[:, ::-1], i[:, ::-1]
                    mM = self.running_max(o, i, m_state[d][:, h:h + 1], mc, free, m_ready[d])
                self.banks.give(c_bank, mM)
                dec, free = extra.take()
                m = self.tt(wide(dec[:, :]), mask.unsqueeze(1).broadcast_to((P, HEADS, P)), wide(big_m[:, :]),
                            ALU.subtract, mM, free)
                for h in range(HEADS):
                    at = slice(h * P, (h + 1) * P)
                    m_dec = self.act(dec[:, at], dec[:, at], ACT.Exp, m, bias=c_col[:, tt, d, h:h + 1])
                inter, free = self.temps.take()
                for h in range(HEADS):
                    at = slice(h * P, (h + 1) * P)
                    m_int = self.act(inter[:, at], big_m[:, at], ACT.Exp, mM, free, m_ready[d], scale=-1.0,
                                     bias=m_state[d][:, h:h + 1])
                floor, free = extra.take()
                m = self.tt(floor[:, :], b_bank[:, :], big_m[:, :], ALU.add, mM, free)
                m_floor = self.act(floor[:, :], floor[:, :], ACT.Exp, m, scale=-1.0)
                s_bank, free = self.banks.take()
                for h in range(HEADS):
                    m_s = self.mm(s_bank[:, h * P:(h + 1) * P], k_t[:, h, cols], q_t[:, h, cols], True, True, free,
                                  counted=h == HEADS - 1)
                s, free = self.temps.take()
                m_sc = self.stt(s[:, :], s_bank[:, :], scale, dec[:, :], ALU.mult, ALU.mult, m_s, m_dec, free)
                self.banks.give(s_bank, m_sc)
                extra.give(dec, m_sc)
                m_qi = None
                if step:
                    qi, free = self.temps.take()
                    m_qi = self.tt(wide(qi[:, :]), q_t[:, :, cols], wide(inter[:, :]), ALU.mult, m_int, free)
                num, nfree = self.banks.take()
                den, dfree = self.banks.take()
                m_d = self.mm(den[:, :], ones, s[:, :], True, step == 0, m_sc, dfree)
                for h in range(HEADS):
                    at = slice(h * P, (h + 1) * P)
                    m_d = self.mm(num[:, at], v[:, tt, at], s[:, at], True, step == 0, nfree, m_sc,
                                  counted=h == HEADS - 1)
                    if step:
                        self.mm(num[:, at], state[d][:, h, :], qi[:, at], False, True, m_qi, s_ready[d])
                        m_d = self.mm(den[:, at], n_state[d][:, h:h + 1].broadcast_to((P, P)), qi[:, at], False,
                                      True, counted=h == HEADS - 1)
                self.temps.give(s, m_d)
                if step:
                    self.temps.give(qi, m_d)
                r, free = self.temps.take()
                m = self.act(r[:, :], den[:, :], ACT.Abs, m_d, free)
                self.banks.give(den, m)
                m = self.tt(r[:, :], r[:, :], floor[:, :], ALU.max, m, m_floor)
                extra.give(floor, m)
                m = self.DVE.do(lambda e, r=r: e.reciprocal(r[:, :], r[:, :]), m)
                if tt in h_written:
                    m = self.tt(wide(r[:, :]), wide(r[:, :]), wide(num[:, :]), ALU.mult, m)
                    m = self.tt(h_sum[:, :, cols], h_sum[:, :, cols], wide(r[:, :]), ALU.add, m, h_written[tt])
                else:
                    m = self.tt(h_sum[:, :, cols], wide(r[:, :]), wide(num[:, :]), ALU.mult, m)
                h_written[tt] = m
                self.banks.give(num, m)
                self.temps.give(r, m)
                if step == TT - 1:
                    self.banks.give(b_bank, m)
                    self.temps.give(big_m, m)
                    self.temps.give(inter, m_int, m)
                    continue
                w = small[:, 216 + 4 * d:220 + 4 * d]
                m_end = wide(big_m[:, :])[:, :, end]
                m = self.tt(w, c_col[:, tt, d, :], m_end, ALU.subtract, self.DVE.last())
                m = self.act(w, w, ACT.Exp, m)
                m = self.ts(w, w, scale, None, ALU.mult, None, m)
                m_w = m
                kt_bank, free = self.banks.take()
                for h in range(HEADS):
                    m_k = self.turn(kt_bank[:, h * P:(h + 1) * P], k_t[:, h, cols], free, counted=h == HEADS - 1)
                kw, free = self.temps.take()
                m_kw = self.tt(wide(kw[:, :]), wide(kt_bank[:, :]), w.unsqueeze(2).broadcast_to((P, HEADS, P)),
                               ALU.mult, m_k, m_w, free)
                self.banks.give(kt_bank, m_kw)
                c_loc, free = self.banks.take()
                n_loc, free2 = self.banks.take()
                for h in range(HEADS):
                    at = slice(h * P, (h + 1) * P)
                    self.mm(c_loc[:, at], kw[:, at], v[:, tt, at], True, True, m_kw, free)
                    m_c = self.mm(n_loc[:, h:h + 1], kw[:, at], ones[:, 0:1], True, True, free2,
                                  counted=h == HEADS - 1)
                self.temps.give(kw, m_c)
                fade = wide(inter[:, :])[:, :, end]
                st = state[d]
                if step == 0:
                    m = self.copy(st[:, :, :], wide(c_loc[:, :]), m_c)
                    m = self.copy(n_state[d], n_loc[:, 0:HEADS], m_c)
                else:
                    m = self.tt(st[:, :, :], st[:, :, :], fade.unsqueeze(2).broadcast_to((P, HEADS, P)), ALU.mult,
                                m_d, m_int)
                    m = self.tt(st[:, :, :], st[:, :, :], wide(c_loc[:, :]), ALU.add, m, m_c)
                    m = self.tt(n_state[d], n_state[d], fade, ALU.mult)
                    m = self.tt(n_state[d], n_state[d], n_loc[:, 0:HEADS], ALU.add, m)
                s_ready[d] = m
                self.banks.give(c_loc, m)
                self.banks.give(n_loc, m)
                m = self.tt(m_state[d], wide(b_bank[:, :])[:, :, end], m_end, ALU.add, m_int)
                m_ready[d] = m
                self.banks.give(b_bank, m)
                self.temps.give(big_m, m, m_int)
                self.temps.give(inter, m)

    def running_max(self, out, in_, start, *after):
        zeros = self.mem["zeros"][:, 0:1].broadcast_to((P, P))
        return self.DVE.do(lambda e: e.tensor_tensor_scan(out, zeros, in_, start, ALU.add, ALU.max), *after)

    def rope(self, out, bank, m, rows, cos, sin, turn, *after):
        x, free = self.temps.take()
        m = self.act(x[0:rows, 0:SEQ], bank[0:rows, 0:SEQ], ACT.Copy, m, free)
        self.banks.give(bank, m)
        self.rope_from(out, x, m, rows, cos, sin, turn, *after)

    def rope_from(self, out, x, m, rows, cos, sin, turn, *after):
        bank, free = self.banks.take()
        m = self.mm(bank[0:rows, 0:SEQ], turn[0:rows, 0:rows], x[0:rows, 0:SEQ], True, True, m, free, counted=True)
        m = self.tt(x[0:rows, SEQ:TOK], bank[0:rows, 0:SEQ], sin[0:rows, :], ALU.mult, m, *after)
        self.banks.give(bank, m)
        m = self.tt(x[0:rows, 0:SEQ], x[0:rows, 0:SEQ], cos[0:rows, :], ALU.mult, m)
        m = self.tt(out, x[0:rows, 0:SEQ], x[0:rows, SEQ:TOK], ALU.add, m)
        self.temps.give(x, m)
        return m

    def softmax(self, bank, m, scale, sink, out, out_free):
        slot = self.soft_n % 8
        self.soft_n += 1
        small, at = self.mem["small"], 8 * slot
        top, total = small[:, at:at + 1], small[:, at + 1:at + 2]
        m = self.DVE.do(lambda e: e.tensor_reduce(top, bank[:, :], AX.X, ALU.max), m, self.soft_free[slot])
        if sink is None:
            m = self.ts(top, top, -scale, None, ALU.mult, None, m)
        else:
            m = self.ts(top, top, -scale, sink[1], ALU.mult, ALU.min, m)
        p, free = self.temps.take()
        m = self.act(p[:, :], bank[:, :], ACT.Exp, m, free, scale=scale, bias=top, accum_out=total)
        self.banks.give(bank, m)
        if sink is not None:
            extra = small[:, at + 2:at + 3]
            m = self.act(extra, sink[0], ACT.Exp, m, bias=top)
            m = self.tt(total, total, extra, ALU.add, m)
        m = self.DVE.do(lambda e: e.reciprocal(total, total), m)
        m = self.ts(p[:, :], p[:, :], total, None, ALU.mult, None, m)
        self.soft_free[slot] = m
        t_bank, free = self.banks.take()
        for k in range(TT):
            m2 = self.turn(t_bank[:, k * P:(k + 1) * P], p[:, k * P:(k + 1) * P], m, free, counted=k == TT - 1)
        self.temps.give(p, m2)
        m = self.act(out, t_bank[:, :].rearrange("p (k q) -> p k q", k=TT), ACT.Copy, m2, out_free)
        self.banks.give(t_bank, m)
        return m

    def odd_mixer(self, dest):
        mem = self.mem
        ready = self.norm(self.mod_scale(dest, 4), self.mod_scale(dest, 3), TOK, self.h_ready)
        self.finish_side()
        self.barrier()
        q_t, k_t, v = mem["o_q"], mem["o_k"], mem["o_v"]
        tables = self.SP.load(mem["stage"][:, :], self.dram["odd_tables"], self.sems["stage"], 32)
        cos, sin = mem["stage"][:, 0:SEQ], mem["stage"][:, SEQ:2 * SEQ]
        near = mem["stage"][:, 2 * SEQ:4 * SEQ].rearrange("q (b k) -> q b k", b=X_TILES)
        src_t = lambda k, tt: (mem["n_hi"][:, k, tt * P:(tt + 1) * P], mem["n_lo"][:, k, tt * P:(tt + 1) * P])
        swap = self.mat("swap")
        def store_k(t, bank, m):
            e = self.act(k_t[:, t, SEQ:TOK], bank[:, SEQ:TOK], ACT.Copy, m)
            self.rope(k_t[:, t, 0:SEQ], bank, e, P, cos, sin, swap, tables)
        self.project("odd_kv", 0, KD, 256, TOK, lambda k: self.n_parts(k), ready, store_k)

        def store_v(pair, bank, m):
            e = self.act(v[:, 2 * pair:2 * pair + 2, :], bank[:, :].rearrange("p (t n) -> p t n", t=2), ACT.Copy, m)
            self.banks.give(bank, e)
        self.project_tokens("odd_kv", 1, KD, 256, range(TT), src_t, ready, store_v)
        for c in range(4):
            self.project("odd_q", c, KD, 256, SEQ, lambda k: self.n_parts(k, SEQ), ready,
                         lambda t, bank, m, c=c: self.rope(q_t[:, 2 * c + t, :], bank, m, P, cos, sin, swap))
        n_read = self.PE.last()
        neg = mem["small"][:, 128:144]
        m_neg = self.ts(neg, self.vec("sink", 0, 16), -1.0, None, ALU.mult, None)
        p_t = mem["o_p"]
        p_free = [None, None]
        turn = 0
        m_in = [self.DVE.last(), self.ACT.last(), m_neg]
        ready = [None] * KD
        for kv in range(C_KV):
            low = (kv % 2) * C_DIM
            rows = slice(low, low + C_DIM)
            for qb in range(X_TILES):
                buf = p_t[turn % 2]
                done = []
                for j in range(4):
                    head = 4 * kv + j
                    tile = (kv // 2) * 4 + j
                    bank, free = self.banks.take()
                    self.mm(bank[:, :], q_t[rows, tile, qb * P:(qb + 1) * P], k_t[rows, kv // 2, :], True, False,
                            free, m_in)
                    m = self.mm(bank[:, 0:SEQ], self.mat("ident"), near[:, qb, :], False, True, counted=True)
                    m = self.softmax(bank, m, C_DIM ** -0.5, (self.vec("sink", head), neg[:, head:head + 1]),
                                     buf[:, :, j * P:(j + 1) * P], p_free[turn % 2])
                    done.append(m)
                out, free = self.banks.take()
                for k in range(TT):
                    m = self.mm(out[rows, :], v[:, k, kv * C_DIM:(kv + 1) * C_DIM], buf[:, k, :], k == 0,
                                k == TT - 1, done, free, counted=k == TT - 1)
                p_free[turn % 2] = m
                turn += 1
                t, free = self.temps.take()
                m = self.act(t[rows, :], out[rows, :], ACT.Copy, m, free)
                self.banks.give(out, m)
                tiles = slice((kv // 2) * 4, (kv // 2) * 4 + 4)
                at = slice(qb * P, (qb + 1) * P)
                m = self.split(mem["n_hi"][rows, tiles, at], mem["n_lo"][rows, tiles, at],
                               t[rows, :].rearrange("p (j q) -> p j q", j=4), m, n_read)
                self.temps.give(t, m)
        for c in range(4):
            self.project("odd_out", c, KD, 256, SEQ, lambda k: self.n_parts(k, SEQ), [m] * KD,
                         lambda t, bank, mk, c=c: self.add_gated(bank, mk, 2 * c + t, self.mod_scale(dest, 5), SEQ))
        self.barrier()

    def second_mixer(self, dest):
        mem, small = self.mem, self.mem["small"]
        wsc = small[:, 0:2 * KD].rearrange("p (k s) -> p k s", k=KD)
        m = self.tt(wsc, dest[:, KD:2 * KD, :], self.vec("mix_pre", 0, KD).unsqueeze(2).broadcast_to((P, KD, 2)),
                    ALU.mult, self.DVE.last())
        ready = self.norm(lambda k, s: wsc[:, k, s:s + 1], self.mod_scale(dest, 0), TOK, self.h_ready, m)
        self.finish_side()
        self.barrier()
        tables = self.SP.load(mem["stage"][:, 0:2 * SEQ], self.dram["mla_tables"], self.sems["stage"], 48)
        cos, sin = mem["stage"][:, 0:SEQ], mem["stage"][:, SEQ:2 * SEQ]
        src = lambda k: self.n_parts(k)
        src_x = lambda k: self.n_parts(k, SEQ)
        src_t = lambda k, tt: (mem["n_hi"][:, k, tt * P:(tt + 1) * P], mem["n_lo"][:, k, tt * P:(tt + 1) * P])
        cq, ckv, kr = (mem["m_cqh"], mem["m_cql"]), (mem["m_ckh"], mem["m_ckl"]), mem["m_kr"]
        z_t, xs_t, b_t, c_t = mem["m_z"], mem["m_xs"], mem["m_b"], mem["m_c"]

        def latent(banks, n, weight, width, parts):
            total, m = self.square_sum([b[:, 0:n] for b, _ in banks], n, [mk for _, mk in banks])
            inv, free = self.temps.take()
            m = self.rstd(inv[:, 0:n], total[:, 0:n], width, m, free)
            self.banks.give(total, m)
            for k, (bank, _) in enumerate(banks):
                t, free = self.temps.take()
                e = self.stt(t[:, 0:n], bank[:, 0:n], self.vec(weight, k), inv[:, 0:n], ALU.mult, ALU.mult, m, free)
                self.banks.give(bank, e)
                e = self.split(parts[0][:, k, 0:n], parts[1][:, k, 0:n], t[:, 0:n], e)
                self.temps.give(t, e)
            self.temps.give(inv, e)
            return e

        found = []
        for c in range(2):
            self.project("in_q", c, KD, (256, P)[c], SEQ, src_x, ready, lambda t, bank, m: found.append((bank, m)))
        m_cq = latent(found, SEQ, "q_norm", Q_RANK, cq)
        found = []
        self.project("in_kv", 0, KD, 256, TOK, src, ready, lambda t, bank, m: found.append((bank, m)))
        m_ckv = latent(found, TOK, "kv_norm", KV_RANK, ckv)

        def store_kr(t, bank, m):
            e = self.act(kr[:, :], bank[:, :], ACT.Copy, m)
            self.banks.give(bank, e)
            x, free = self.temps.take()
            e = self.act(x[0:QD, 0:SEQ], kr[0:QD, 0:SEQ], ACT.Copy, e, free)
            self.m_kr = self.rope_from(kr[0:QD, 0:SEQ], x, e, QD, cos, sin, self.mat("turn"), tables)
        self.project("in_kr", 0, KD, P, TOK, src, ready, store_kr)

        def store_z(c):
            def finish(t, bank, m):
                self.banks.give(bank, self.act(z_t[:, 2 * c + t, :], bank[:, 0:SEQ], ACT.Silu, m))
            return finish
        for c in range(4):
            self.project("in_z", c, KD, 256, SEQ, src_x, ready, store_z(c))

        def conv(base, n):
            def finish(t, bank, m):
                tile = base + t
                s = n // SEQ
                x, free = self.temps.take()
                xv = x[:, 0:n].rearrange("p (s t) -> p s t", s=s)
                bv = bank[:, 0:n].rearrange("p (s t) -> p s t", s=s)
                w = lambda tap: self.vec("sconv_w", tap * 12 + tile)
                m = self.act(x[:, 0:n], bank[:, 0:n], ACT.Identity, m, free, scale=w(2),
                             bias=self.vec("sconv_b", tile))
                for tap in (0, 1, 3, 4):
                    off = tap - 2
                    o = slice(max(0, -off), SEQ - max(0, off))
                    i = slice(max(0, off), SEQ - max(0, -off))
                    m = self.stt(xv[:, :, o], bv[:, :, i], w(tap), xv[:, :, o], ALU.mult, ALU.add, m)
                self.banks.give(bank, m)
                out = xs_t[:, tile, 0:n] if tile < 8 else b_t[:, tile - 8, 0:n] if tile < 10 else c_t[:, tile - 10, :]
                m = self.act(out, x[:, 0:n], ACT.Silu, m)
                self.temps.give(x, m)
            return finish
        for c in range(6):
            n = TOK if c < 5 else SEQ
            self.project("in_xbc", c, KD, 256, n, src if c < 5 else src_x, ready, conv(2 * c, n))
        dt = small[:, 64:64 + 32 * TT].rearrange("p (t g) -> p t g", t=TT)

        def store_dt(pair, bank, m):
            e = self.tt(dt[:, 2 * pair:2 * pair + 2, :], bank[:, 0:64].rearrange("p (t g) -> p t g", t=2),
                        self.vec("dt_b", 0, 32).unsqueeze(1).broadcast_to((P, 2, 32)), ALU.add, m)
            self.banks.give(bank, e)
        self.project_tokens("in_dt", 0, KD, 32, range(TT), src_t, ready, store_dt)
        self.barrier()
        self.ssd(dt)
        self.barrier()
        self.latent_attention(cq, ckv, kr, cos, sin)
        self.barrier()
        mix = mem["m_mix"]
        parts = lambda k: (mem["y_hi"][:, k, :], mem["y_lo"][:, k, :])
        for q in range(4):
            banks = None
            for i in range(2):
                banks = self.project("mix_out", 2 * q + i, KD, 256, SEQ, lambda k, i=i: parts(8 * i + k), None,
                                     lambda t, bank, m, q=q: self.banks.give(
                                         bank, self.act(mix[:, 2 * q + t, :], bank[:, 0:SEQ], ACT.Copy, m)),
                                     first=i == 0, last=i == 1, banks=banks)
        self.post_norm(mix, dest, 2, "mix_post")

    def post_norm(self, mix, dest, sec, weight):
        small = self.mem["small"]
        gw = small[:, 0:KD]
        m0 = self.tt(gw, dest[:, sec * KD:(sec + 1) * KD, 0], self.vec(weight, 0, KD), ALU.mult, self.DVE.last())
        bank, m = self.square_sum([mix[:, k, :] for k in range(KD)], SEQ, self.ACT.last(), self.DVE.last())
        inv, free = self.temps.take()
        m = self.rstd(inv[:, 0:SEQ], bank[:, 0:SEQ], D, m, free)
        self.banks.give(bank, m)
        h = self.mem["h"]
        for k in range(KD):
            e = self.stt(mix[:, k, :], mix[:, k, :], gw[:, k:k + 1], inv[:, 0:SEQ], ALU.mult, ALU.mult, m, m0)
            self.h_ready[k] = self.tt(h[:, k, 0:SEQ], h[:, k, 0:SEQ], mix[:, k, :], ALU.add, e)
        self.temps.give(inv, e)

    def ssd(self, dt):
        mem, small = self.mem, self.mem["small"]
        xs_t, b_t, c_t, z_t = mem["m_xs"], mem["m_b"], mem["m_c"], mem["m_z"]
        xs, bt, y, state = mem["s_xs"], mem["s_b"], mem["s_y"], mem["s_state"]
        cb = mem["s_cb"]
        at = 64 + 32 * TT
        da = small[:, at:at + 32 * TT].rearrange("p (t g) -> p t g", t=TT)
        col = small[:, at + 128:at + 256].rearrange("p (t g) -> p t g", t=TT)
        e1 = small[:, at + 256:at + 288]
        tmp = small[:, at + 288:at + 320]
        neg_a = small[:, at + 320:at + 352]
        m = None
        for tt in range(TT):
            m = self.log_one_plus_exp(da[:, tt, :], e1, dt[:, tt, :], 1.0, [m], tmp)
        m = self.DVE.do(lambda e: e.tensor_copy(dt, da), m)
        m2 = self.act(neg_a, self.vec("a_log", 0, 32), ACT.Exp)
        m2 = self.ts(neg_a, neg_a, -1.0, None, ALU.mult, None, m2)
        m_da = self.tt(da, dt, neg_a.unsqueeze(1).broadcast_to((P, TT, 32)), ALU.mult, m, m2)
        bank, free = self.banks.take()
        for tt in range(TT):
            for d in range(2):
                g = slice(tt * 32 + d * 16, tt * 32 + d * 16 + 16)
                m = self.mm(bank[:, g], self.mat(("tri_f", "tri_b")[d]), da[:, tt, d * 16:d * 16 + 16], True, True,
                            m_da, free, counted=tt == TT - 1 and d == 1)
        m_col = self.ts(col, bank[:, 0:32 * TT].rearrange("p (t g) -> p t g", t=TT), -1.0, None, ALU.mult, None, m)
        self.banks.give(bank, m_col)
        for tt in range(TT):
            for half in range(2):
                bank, free = self.banks.take()
                for j in range(4):
                    m = self.turn(bank[:, j * P:(j + 1) * P], xs_t[:, 4 * half + j, tt * P:(tt + 1) * P], free,
                                  counted=j == 3)
                m = self.act(xs[:, tt, half * 512:(half + 1) * 512], bank[:, :], ACT.Copy, m)
                self.banks.give(bank, m)
            bank, free = self.banks.take()
            for j in range(2):
                m = self.turn(bank[:, j * P:(j + 1) * P], b_t[:, j, tt * P:(tt + 1) * P], free, counted=j == 1)
            m_xs = self.act(bt[:, tt, :], bank[:, 0:256], ACT.Copy, m)
            self.banks.give(bank, m_xs)
        bank, free = self.banks.take()
        for tt in range(X_TILES):
            for g in range(S_GROUPS):
                o = (tt * S_GROUPS + g) * P
                m = self.mm(bank[:, o:o + P], b_t[:, g, tt * P:(tt + 1) * P], c_t[:, g, tt * P:(tt + 1) * P], True,
                            True, free, counted=True)
        m_cb = self.act(cb[:, :], bank[:, :], ACT.Copy, m)
        self.banks.give(bank, m_cb)
        cbv = cb[:, :].rearrange("p (t g l) -> p t g l", t=X_TILES, g=S_GROUPS)

        heads = lambda ap: ap.rearrange("p (h e) -> p h e", h=S_PER)
        wide = lambda ap: ap.rearrange("p (h l) -> p h l", h=4)
        w = small[:, at + 352:at + 368]
        fade = small[:, at + 368:at + 384]
        y_written = set()
        for d in range(2):
            order = ([2, 3, 0, 1], [3, 2, 1, 0])[d]
            tri, mask = self.mat(("tri_f", "tri_b")[d]), self.mat(("mask_f", "mask_b")[d])
            m_state = None
            for step, tt in enumerate(order):
                g16 = slice(d * 16, d * 16 + 16)
                xd = []
                for g in range(S_GROUPS):
                    part, free = self.temps.take()
                    xd.append(part)
                    scale = dt[:, tt, d * 16 + g * S_PER:d * 16 + (g + 1) * S_PER]
                    m_xd = self.tt(heads(part[:, :]), heads(xs[:, tt, g * 512:(g + 1) * 512]),
                                   scale.unsqueeze(2).broadcast_to((P, S_PER, S_DIM)), ALU.mult, m_xs, free)
                if tt < X_TILES:
                    cols = slice(tt * P, (tt + 1) * P)
                    for quad in range(4):
                        g = quad // 2
                        a_bank, free = self.banks.take()
                        for j in range(4):
                            h = 4 * quad + j
                            m = self.mm(a_bank[:, j * P:(j + 1) * P],
                                        da[:, tt, d * 16 + h:d * 16 + h + 1].broadcast_to((P, P)), tri, True, True,
                                        free, counted=j == 3)
                        dec, free = self.temps.take()
                        m2 = self.tt(wide(dec[:, :]), wide(a_bank[:, :]), mask.unsqueeze(1).broadcast_to((P, 4, P)),
                                     ALU.add, m, free)
                        for j in range(4):
                            h = 4 * quad + j
                            o = slice(j * P, (j + 1) * P)
                            m2 = self.act(dec[:, o], dec[:, o], ACT.Exp, m2, m_col,
                                          bias=col[:, tt, d * 16 + h:d * 16 + h + 1])
                        ce, free = self.temps.take()
                        m3 = self.act(ce[:, :], a_bank[:, :], ACT.Exp, m, free)
                        self.banks.give(a_bank, m2, m3)
                        m2 = self.tt(wide(dec[:, :]), wide(dec[:, :]),
                                     cbv[:, tt, g, :].unsqueeze(1).broadcast_to((P, 4, P)), ALU.mult, m2, m_cb)
                        m3 = self.tt(wide(ce[:, :]), wide(ce[:, :]),
                                     c_t[:, g, cols].unsqueeze(1).broadcast_to((P, 4, P)), ALU.mult, m3)
                        y_bank, free = self.banks.take()
                        for j in range(4):
                            h = 4 * quad + j
                            out = y_bank[(h % 2) * 64:(h % 2) * 64 + 64, (j // 2) * P:(j // 2 + 1) * P]
                            self.mm(out, xd[g][:, (h % S_PER) * S_DIM:(h % S_PER + 1) * S_DIM], dec[:, j * P:(j + 1) * P], True, False,
                                    m_xd, m2, free)
                            m = self.mm(out, state[:, h * S_DIM:(h + 1) * S_DIM], ce[:, j * P:(j + 1) * P], False,
                                        True, m_state, m3, counted=j == 3)
                        self.temps.give(dec, m)
                        self.temps.give(ce, m)
                        yv = y[:, 2 * quad:2 * quad + 2, cols]
                        bv = y_bank[:, 0:256].rearrange("p (j l) -> p j l", j=2)
                        if (tt, quad) in y_written:
                            e = self.tt(yv, yv, bv, ALU.add, m, self.DVE.last())
                        else:
                            e = self.copy(yv, bv, m)
                        y_written.add((tt, quad))
                        self.banks.give(y_bank, e)
                if step == TT - 1:
                    for part in xd:
                        self.temps.give(part, m)
                    continue
                bank, free = self.banks.take()
                m = self.mm(bank[:, 0:16], self.mat("ones"), da[:, tt, g16], True, True, free, counted=True)
                m1 = self.tt(w, bank[:, 0:16], col[:, tt, g16], ALU.add, m, self.DVE.last())
                m1 = self.act(w, w, ACT.Exp, m1)
                m2 = self.act(fade, bank[:, 0:16], ACT.Exp, m, self.DVE.last(), self.ACT.last())
                self.banks.give(bank, m1, m2)
                for g in range(S_GROUPS):
                    m = self.tt(heads(xd[g][:, :]), heads(xd[g][:, :]),
                                w[:, g * S_PER:(g + 1) * S_PER].unsqueeze(2).broadcast_to((P, S_PER, S_DIM)),
                                ALU.mult, m1, m_xd, self.PE.last())
                    bank, free = self.banks.take()
                    gc = slice(g * 512, (g + 1) * 512)
                    m4 = self.mm(bank[:, :], bt[:, tt, g * P:(g + 1) * P], xd[g][:, :], True, True, m, free,
                                 counted=True)
                    if step == 0:
                        m5 = self.copy(state[:, gc], bank[:, :], m4)
                    else:
                        sv = state[:, gc].rearrange("p (h e) -> p h e", h=S_PER)
                        m5 = self.tt(sv, sv, fade[:, g * S_PER:(g + 1) * S_PER].unsqueeze(2).broadcast_to(
                            (P, S_PER, S_DIM)), ALU.mult, m4, m2, self.DVE.last())
                        m5 = self.tt(state[:, gc], state[:, gc], bank[:, :], ALU.add, m5)
                    self.banks.give(bank, m5)
                    self.temps.give(xd[g], m4)
                m_state = m5
        for k in range(KD):
            m = self.stt(y[:, k, :], xs_t[:, k, 0:SEQ], self.vec("ssd_d", k), y[:, k, :], ALU.mult, ALU.add,
                         self.DVE.last())
            m = self.tt(y[:, k, :], y[:, k, :], z_t[:, k, :], ALU.mult, m)
        bank, m = self.square_sum([y[:, k, :] for k in range(KD)], SEQ, m)
        inv, free = self.temps.take()
        m = self.rstd(inv[:, 0:SEQ], bank[:, 0:SEQ], D_INNER, m, free)
        self.banks.give(bank, m)
        for k in range(KD):
            t, free = self.temps.take()
            e = self.stt(t[:, 0:SEQ], y[:, k, :], self.vec("ssd_norm", k), inv[:, 0:SEQ], ALU.mult, ALU.mult, m,
                         free, self.PE.last())
            e = self.split(mem["y_hi"][:, 8 + k, :], mem["y_lo"][:, 8 + k, :], t[:, 0:SEQ], e)
            self.temps.give(t, e)
        self.temps.give(inv, e)

    def latent_attention(self, cq, ckv, kr, cos, sin):
        mem = self.mem
        p_free = [None, None]
        n = 0
        free_g = None
        for g in range(M_HEADS // HEADS_AT_ONCE):
            q_g, k_g, v_g = mem["l_q"], mem["l_k"], mem["l_v"]
            chunk = self.next_chunk("q_up", g, 3 * HEADS_AT_ONCE * QD)
            hi, lo = (x.rearrange("p (k h c) -> p k h c", k=3, h=HEADS_AT_ONCE) for x in (chunk.hi, chunk.lo))
            q_ready = []
            for h in range(HEADS_AT_ONCE):
                bank, free = self.banks.take()
                for k in range(3):
                    m = self.mm3(bank[0:QD, 0:SEQ], (hi[:, k, h, :], lo[:, k, h, :]),
                                 (cq[0][:, k, :], cq[1][:, k, :]), k == 0, k == 2, chunk.ready, free, counted=k == 2)
                if h == HEADS_AT_ONCE - 1:
                    self.done_with(chunk, m)
                x, free = self.temps.take()
                m = self.act(x[0:QD, 0:SEQ], bank[0:QD, 0:SEQ], ACT.Copy, m, free)
                self.banks.give(bank, m)
                q_ready.append(self.rope_from(q_g[0:QD, h, :], x, m, QD, cos, sin, self.mat("turn"), free_g))
            chunk = self.next_chunk("kv_up", g, 2 * HEADS_AT_ONCE * P)
            hi, lo = (x.rearrange("p (k h c) -> p k h c", k=2, h=HEADS_AT_ONCE) for x in (chunk.hi, chunk.lo))
            k_ready = []
            for h in range(HEADS_AT_ONCE):
                bank, free = self.banks.take()
                for k in range(2):
                    m = self.mm3(bank[:, :], (hi[:, k, h, :], lo[:, k, h, :]), (ckv[0][:, k, :], ckv[1][:, k, :]),
                                 k == 0, k == 1, chunk.ready, free, counted=k == 1)
                m = self.act(k_g[0:NOPE, h, :], bank[0:NOPE, :], ACT.Copy, m, free_g)
                self.banks.give(bank, m)
                m2 = self.act(k_g[NOPE:QD, h, :], kr[NOPE:QD, :], ACT.Copy, free_g)
                k_ready.append(m2)
            for pair in range(2):
                bank, free = self.banks.take()
                for j in range(2):
                    tt = 2 * pair + j
                    c = slice(tt * P, (tt + 1) * P)
                    for k in range(2):
                        m = self.mm3(bank[:, j * 256:(j + 1) * 256].rearrange("p (h c) -> p h c", h=HEADS_AT_ONCE),
                                     (ckv[0][:, k, c], ckv[1][:, k, c]),
                                     (hi[:, k, :, NOPE:P], lo[:, k, :, NOPE:P]), k == 0, k == 1, free,
                                     counted=k == 1)
                v_ready = self.act(v_g[:, 2 * pair:2 * pair + 2, :], bank[:, :].rearrange("p (t c) -> p t c", t=2),
                                   ACT.Copy, m, free_g)
                self.banks.give(bank, v_ready)
            self.done_with(chunk, m)
            for h in range(HEADS_AT_ONCE):
                buf = mem["l_p"][n % 2]
                done = []
                for qb in range(X_TILES):
                    bank, free = self.banks.take()
                    m = self.mm(bank[:, :], q_g[0:QD, h, qb * P:(qb + 1) * P], k_g[0:QD, h, :], True, True, free,
                                q_ready[h], k_ready[h], counted=True)
                    done.append(self.softmax(bank, m, QD ** -0.5, None, buf[:, :, qb * P:(qb + 1) * P],
                                             p_free[n % 2]))
                rows = slice((h % 2) * V_DIM, (h % 2) * V_DIM + V_DIM)
                out, free = self.banks.take()
                for k in range(TT):
                    m = self.mm(out[rows, 0:SEQ], v_g[:, k, h * V_DIM:(h + 1) * V_DIM], buf[:, k, :], k == 0,
                                k == TT - 1, done, v_ready, free, counted=k == TT - 1)
                p_free[n % 2] = m
                n += 1
                t, free = self.temps.take()
                m = self.act(t[rows, 0:SEQ], out[rows, 0:SEQ], ACT.Copy, m, free)
                self.banks.give(out, m)
                tile = (g * HEADS_AT_ONCE + h) // 2
                m = self.split(mem["y_hi"][rows, tile, :], mem["y_lo"][rows, tile, :], t[rows, 0:SEQ], m)
                self.temps.give(t, m)
            free_g = self.PE.last()

    def second_ffn(self, dest):
        mem, small = self.mem, self.mem["small"]
        wsc = small[:, 16:16 + KD]
        m = self.tt(wsc, dest[:, 4 * KD:5 * KD, 0], self.vec("ffn_pre", 0, KD), ALU.mult, self.DVE.last())
        ready = self.norm(lambda k, s: wsc[:, k:k + 1], self.mod_scale(dest, 3), SEQ, self.h_ready, m)
        acc = mem["f_out"]

        def gate(j, n, g_bank, g_mark, u_bank, u_mark):
            t, free = self.temps.take()
            w = lambda tap: self.vec("fconv_w", tap * KF + j)
            m = self.act(t[:, 0:n], g_bank[:, 0:n], ACT.Identity, g_mark, free, scale=w(1),
                         bias=self.vec("fconv_b", j))
            m = self.stt(t[:, 1:n], g_bank[:, 0:n - 1], w(0), t[:, 1:n], ALU.mult, ALU.add, m)
            m = self.stt(t[:, 0:n - 1], g_bank[:, 1:n], w(2), t[:, 0:n - 1], ALU.mult, ALU.add, m)
            self.banks.give(g_bank, m)
            m = self.act(t[:, 0:n], t[:, 0:n], ACT.Gelu, m)
            m = self.tt(t[:, 0:n], t[:, 0:n], u_bank[:, 0:n], ALU.mult, m, u_mark)
            self.banks.give(u_bank, m)
            return t, m

        seen = set()

        def finish(k, bank, m):
            if k in seen:
                e = self.tt(acc[:, k, :], acc[:, k, :], bank[:, 0:SEQ], ALU.add, m, self.DVE.last())
            else:
                e = self.copy(acc[:, k, :], bank[:, 0:SEQ], m)
            seen.add(k)
            self.banks.give(bank, e)
        self.hidden(("up", 0), ("down", 0), SEQ, ready, gate, finish)
        self.post_norm(acc, dest, 5, "ffn_post")

    def compose(self):
        mem, dram, sems = self.mem, self.dram, self.sems
        self.soft_n, self.soft_free = 0, [None] * 8
        mats = self.SP.load(mem["matrices"][:, :], dram["matrices"], sems["matrices"], 16)
        vecs = self.SP.load(mem["vectors"][:, :], dram["vectors"], sems["vectors"], 16)
        h_in = [self.SP.load(mem["h"][:, :, :], dram["tokens"], sems["h"], 16)]
        zero = self.DVE.do(lambda e: e.memset(mem["silu_c"][:, :, :, :], 0.0))
        zero = self.DVE.do(lambda e: e.memset(mem["zeros"][:, :], 0.0))
        zero = self.DVE.do(lambda e: e.memset(mem["eps"][:, :], EPS))
        self.DVE.wait(zero)
        cv = self.vec("c", 0, 4 * KD).rearrange("p (b s k) -> p b s k", b=2, s=2)
        for b in range(2):
            for s in range(2):
                m = self.act(mem["silu_c"][:, b, :, s], cv[:, b, s, :], ACT.Silu, vecs, zero)
        self.silu_c_ready = m
        for line in (self.PE, self.DVE, self.ACT):
            line.wait(mats, vecs)

        mods, mod_2 = mem["mods"], mem["mod_2"]
        half = 0.5
        self.modulation("ada", 0, 0, mods[0], ("ada_b", 0), [1, 0])
        self.finish_side()
        self.section(mods[0], 1, ALU.add, 1.0)
        self.modulation("ada", 0, 0, mods[0], ("ada_b", 0), [2, 3, 4, 5, 6, 7, 8])
        self.h_ready = [h_in[0]] * KD

        def scales(dest, ones_, halves):
            for s in ones_:
                self.section(dest, s, ALU.add, 1.0)
            for s in halves:
                self.section(dest, s, ALU.mult, half)

        self.ffn_with_gate("ffn_in", 0, "ffn_out", 0, mods[0], (0, 1, 2), TOK)
        self.finish_side()
        scales(mods[0], [4, 7], [8])
        self.even_mixer(mods[0])
        self.modulation("ada", 36, 0, mods[1], ("ada_b", N_MOD * KD), [1, 0, 2, 3, 4, 5, 6, 7, 8])
        self.ffn(("ffn_in", KF), ("ffn_out", 16), mods[0], (6, 7, 8), TOK)
        self.finish_side()
        scales(mods[1], [1, 4, 7], [2, 8])
        self.modulation("mod_2", 0, 1, mod_2, ("b_mod", 0), [0, 1, 2, 3, 4, 5])
        self.ffn(("ffn_in", 2 * KF), ("ffn_out", 32), mods[1], (0, 1, 2), TOK)
        self.odd_mixer(mods[1])
        scales(mod_2, [1, 4], [])
        self.ffn(("ffn_in", 3 * KF), ("ffn_out", 48), mods[1], (6, 7, 8), SEQ)
        h = mem["h"]
        bank, m = self.square_sum([h[:, k, 0:SEQ] for k in range(KD)], SEQ, self.h_ready)
        inv, free = self.temps.take()
        m = self.rstd(inv[:, 0:SEQ], bank[:, 0:SEQ], D, m, free)
        self.banks.give(bank, m)
        ctx_in = self.SP.load(h[:, :, SEQ:TOK], dram["ctx_2"], sems["h"], 32, self.barrier())
        for k in range(KD):
            e = self.stt(h[:, k, 0:SEQ], h[:, k, 0:SEQ], self.vec("final", k), inv[:, 0:SEQ], ALU.mult, ALU.mult, m)
            self.h_ready[k] = [e, ctx_in]
        self.temps.give(inv, e)
        self.barrier()
        self.second_mixer(mod_2)
        self.barrier()
        self.second_ffn(mod_2)
        out = self.SP.load(dram["out"], h[:, :, 0:SEQ], sems["out"], 16, self.h_ready)
        self.SP.wait(out)

    def ffn_with_gate(self, w_in, i, w_out, o, dest, secs, n):
        ready = self.norm(self.mod_scale(dest, secs[1]), self.mod_scale(dest, secs[0]), n, self.h_ready)
        state = {"halved": False}

        def finish(k, bank, m):
            if not state["halved"]:
                state["halved"] = True
                self.section(dest, secs[2], ALU.mult, 0.5)
                self.DVE.wait(self.DVE.last())
            self.add_gated(bank, m, k, self.mod_scale(dest, secs[2]), n)
        self.hidden((w_in, i), (w_out, o), n, ready, self.silu_gate, finish)


def build(nc, dram):
    base = [16512]
    mem = {}

    def place(name, shape, dtype=F32, at=None):
        width = 4
        for s in shape[1:]:
            width *= s
        offset = base[0] if at is None else at
        t = nc.alloc_sbuf_tensor_at(name, shape, dtype, offset=offset)
        if at is None:
            base[0] += (width + 31) // 32 * 32
        return t

    mem["h"] = place("h", [P, KD, TOK])
    n_at = base[0]
    mem["n_hi"] = place("n_hi", [P, KD, TOK], F32R)
    mem["n_lo"] = place("n_lo", [P, KD, TOK], F32R)
    a_at = base[0]
    mem["a_hi"] = place("a_hi", [P, A_SLOTS, TOK], F32R)
    mem["a_lo"] = place("a_lo", [P, A_SLOTS, TOK], F32R)
    mem["raw"] = [place(f"raw{i}", [P, CHUNK]) for i in range(RAW_SLOTS)]
    mem["w_hi"] = [place(f"w_hi{i}", [P, CHUNK], F32R) for i in range(SPLIT_SLOTS)]
    mem["w_lo"] = [place(f"w_lo{i}", [P, CHUNK], F32R) for i in range(SPLIT_SLOTS)]
    mem["temps"] = [place(f"temp{i}", [P, TOK]) for i in range(TEMPS)]
    mem["matrices"] = place("matrices", [P, len(MATRICES) * P])
    mem["vectors"] = place("vectors", [P, N_VECTORS])
    mem["stage"] = place("stage", [P, 8 * P])
    mem["mods"] = [place(f"mod{i}", [P, N_MOD * KD, 2]) for i in range(2)]
    mem["mod_2"] = place("mod_2", [P, N_MOD_2 * KD, 2])
    mem["silu_c"] = place("silu_c", [P, 2, KD, 32])
    mem["small"] = place("small", [P, 768])
    mem["zeros"] = place("zeros", [P, 8])
    mem["eps"] = place("eps", [P, 8])
    assert base[0] <= 229368, base[0]
    K = 1024
    for i, x in enumerate(("e_q", "e_k", "e_v", "e_o", "e_u", "e_vb")):
        mem[x] = place(x, [P, 4, TOK], at=a_at + i * 8 * K)
    mem["e_c0"] = place("e_c0", [P, HEADS, HEAD], at=n_at)
    mem["e_c1"] = place("e_c1", [P, HEADS, HEAD], at=n_at + 2 * K)
    mem["e_extra"] = [place(f"e_extra{i}", [P, TOK], at=n_at + 16 * K + i * 2 * K) for i in range(4)]
    mem["o_q"] = place("o_q", [P, KD, SEQ], at=a_at)
    mem["o_k"] = place("o_k", [P, 2, TOK], at=a_at + 8 * K)
    mem["o_v"] = place("o_v", [P, TT, 256], at=a_at + 12 * K)
    mem["o_p"] = [place(f"o_p{i}", [P, TT, 512], at=a_at + (16 + 8 * i) * K) for i in range(2)]
    mem["m_cqh"] = place("m_cqh", [P, 3, SEQ], F32R, at=a_at)
    mem["m_cql"] = place("m_cql", [P, 3, SEQ], F32R, at=a_at + 3 * K)
    mem["m_ckh"] = place("m_ckh", [P, 2, TOK], F32R, at=a_at + 6 * K)
    mem["m_ckl"] = place("m_ckl", [P, 2, TOK], F32R, at=a_at + 10 * K)
    mem["m_kr"] = place("m_kr", [P, TOK], at=a_at + 14 * K)
    b = a_at + 16 * K
    mem["m_z"] = place("m_z", [P, KD, SEQ], at=b)
    mem["m_xs"] = place("m_xs", [P, KD, TOK], at=b + 8 * K)
    mem["m_b"] = place("m_b", [P, 2, TOK], at=b + 24 * K)
    mem["m_c"] = place("m_c", [P, 2, SEQ], at=b + 28 * K)
    mem["s_cb"] = place("s_cb", [P, TOK], at=b + 30 * K)
    mem["s_y"] = place("s_y", [P, KD, SEQ], at=n_at)
    mem["s_xs"] = place("s_xs", [P, TT, D_INNER], at=n_at + 8 * K)
    mem["s_b"] = place("s_b", [P, TT, 256], at=n_at + 24 * K)
    mem["s_state"] = place("s_state", [P, D_INNER], at=n_at + 28 * K)
    mem["y_hi"] = place("y_hi", [P, 16, SEQ], F32R, at=n_at)
    mem["y_lo"] = place("y_lo", [P, 16, SEQ], F32R, at=n_at + 16 * K)
    mem["l_q"] = place("l_q", [P, HEADS_AT_ONCE, SEQ], at=b)
    mem["l_k"] = place("l_k", [P, HEADS_AT_ONCE, TOK], at=b + 4 * K)
    mem["l_v"] = place("l_v", [P, TT, HEADS_AT_ONCE * V_DIM], at=b + 12 * K)
    mem["l_p"] = [place(f"l_p{i}", [P, TT, SEQ], at=b + (16 + 4 * i) * K) for i in range(2)]
    mem["m_mix"] = place("m_mix", [P, KD, SEQ], at=a_at)
    mem["f_out"] = place("f_out", [P, KD, TOK], at=n_at)[:, :, SEQ:TOK]
    mem["banks"] = [nc.alloc_psum_tensor(f"bank{i}", [P, 512], F32) for i in range(8)]

    with ExitStack() as stack:
        def semaphore(name):
            return stack.enter_context(nc.semaphore(name))
        sems = {x: semaphore(f"s_{x}") for x in ("pe", "act", "dve", "sp", "pool", "matrices", "vectors", "h",
                                                 "stage", "out")}
        sems["raw"] = [semaphore(f"s_raw{i}") for i in range(RAW_SLOTS)]
        first = Program(nc, dram, mem, sems, None)
        first.compose()
        program = Program(nc, dram, mem, sems, first.asked)
        program.compose()
        assert program.asked == first.asked
        block = stack.enter_context(nc.Block())

        @block.sync
        def _(engine):
            program.SP.run(engine)

        @block.tensor
        def _(engine):
            program.PE.run(engine)

        @block.scalar
        def _(engine):
            program.ACT.run(engine)

        @block.vector
        def _(engine):
            program.DVE.run(engine)


def chunks(w, cols, width=None):
    kt, n = w.shape[0] // P, w.shape[1] // cols
    out = w.reshape(kt, P, n, cols).transpose(2, 1, 0, 3).reshape(n, P, kt * cols)
    if width and width > kt * cols:
        out = np.pad(out, ((0, 0), (0, 0), (0, width - kt * cols)))
    return out


def inward_chunks(w):
    g, u = w[:, :F].reshape(D, KF, P), w[:, F:].reshape(D, KF, P)
    return chunks(np.stack([g, u], axis=2).reshape(D, 2 * F), 2 * P)


def outward_chunks(w):
    out = []
    for half in range(2):
        rows = w[half * F // 2:(half + 1) * F // 2]
        for q in range(D // 256):
            part = rows[:, q * 256:(q + 1) * 256]
            out += [chunks(part[:6 * P], 256, 6 * 256), chunks(part[6 * P:], 256, 6 * 256)]
    return np.concatenate(out)


def features(v):
    return v.reshape(-1, P).T


def kernel(**inputs):
    import concourse.bacc as bacc
    from concourse.bass_utils import run_bass_kernel_spmd

    a = {k: np.asarray(v) for k, v in inputs.items()}
    square, odd, mla = shape_constants()
    on_all = lambda v: np.broadcast_to(v.reshape(1, -1), (P, v.size))
    vectors = {
        "ada_b": features(a["ada_b"]), "b_mod": features(a["b_mod_2"]), "conv": features(a["mlstm_conv"]),
        "mnorm": features(a["mlstm_norm"]), "sgu": features(a["sgu_norm"]), "final": features(a["final_norm"]),
        "mix_pre": features(a["mix_pre_norm_2"]), "mix_post": features(a["mix_post_norm_2"]),
        "q_norm": features(a["q_norm_2"]), "kv_norm": features(a["kv_norm_2"]),
        "sconv_w": features(a["ssd_conv_w_2"]), "sconv_b": features(a["ssd_conv_b_2"]),
        "ssd_norm": features(a["ssd_norm_2"]), "ssd_d": features(np.repeat(a["ssd_d_2"].reshape(-1), S_DIM)),
        "ffn_pre": features(a["ffn_pre_norm_2"]), "ffn_post": features(a["ffn_post_norm_2"]),
        "fconv_w": features(a["ffn_conv_w_2"]), "fconv_b": features(a["ffn_conv_b_2"]),
        "c": np.concatenate([features(a[x]) for x in ("c", "c_ctx", "c_2", "c_ctx_2")], axis=1),
        "gate_b": on_all(a["mlstm_gate_b"]), "sink": on_all(a["attn_sink"]), "dt_b": on_all(a["ssd_dt_bias_2"]),
        "a_log": on_all(a["ssd_a_log_2"]),
    }
    vectors = np.concatenate([vectors[x] for x in VECTORS], axis=1)
    stream = lambda x: x[0].T.reshape(KD, P, SEQ).transpose(1, 0, 2)
    heads = [4 * kv + j for g in range(2) for j in range(4) for kv in (2 * g, 2 * g + 1)]
    qkv, q_cols = a["odd_w_qkv"][0], C_HEADS * C_DIM
    odd_q = qkv[:, :q_cols].reshape(D, C_HEADS, C_DIM)[:, heads].reshape(D, q_cols)
    odd_out = a["odd_w_out"][0].reshape(C_HEADS, C_DIM, D)[heads].reshape(q_cols, D)
    w_in, even = a["w_in_2"][0], a["even_w_in"][0]
    z_at = Q_RANK + KV_RANK + ROPE
    x_at = z_at + D_INNER
    dt_at = x_at + D_INNER + 2 * S_GROUPS * S_STATE
    kr_at = Q_RANK + KV_RANK - NOPE
    gates_at = 4 * W_A
    arrays = {
        "matrices": square, "vectors": vectors, "odd_tables": odd, "mla_tables": mla,
        "tokens": np.concatenate([stream(a["x"]), stream(a["ctx"])], axis=2), "ctx_2": stream(a["ctx_2"]),
        "even_tables": np.concatenate([a["sgu_ws"][0].transpose(2, 0, 1).reshape(P, 4 * P),
                                       on_all(a["sgu_b"])], axis=1),
        "ada": np.concatenate([chunks(w, 256) for w in a["ada_w"]]),
        "mod_2": chunks(a["w_mod_2"][0], 256),
        "ffn_in": np.concatenate([inward_chunks(w) for w in a["ffn_w_in"].reshape(4, D, 2 * F)]),
        "ffn_out": np.concatenate([outward_chunks(w) for w in a["ffn_w_out"].reshape(4, F, D)]),
        "even_in": chunks(np.concatenate([even[:, :gates_at], even[:, gates_at + 16:]], axis=1), 256),
        "even_gates": chunks(even[:, gates_at:gates_at + 16], 16),
        "even_out": chunks(a["even_w_out"][0], 256),
        "odd_q": chunks(odd_q, 256), "odd_kv": chunks(qkv[:, q_cols:], 256), "odd_out": chunks(odd_out, 256),
        "in_q": np.concatenate([chunks(w_in[:, :256], 256), chunks(w_in[:, 256:Q_RANK], P, CHUNK)]),
        "in_kv": chunks(w_in[:, Q_RANK:Q_RANK + KV_RANK], 256),
        "in_kr": chunks(w_in[:, kr_at:kr_at + P], P),
        "in_z": chunks(w_in[:, z_at:x_at], 256), "in_xbc": chunks(w_in[:, x_at:dt_at], 256),
        "in_dt": chunks(w_in[:, dt_at:], 32),
        "q_up": chunks(a["w_q_up_2"][0], HEADS_AT_ONCE * QD),
        "kv_up": chunks(a["w_kv_up_2"][0], HEADS_AT_ONCE * P),
        "mix_out": np.stack([chunks(a["w_out_2"][0][i * D:(i + 1) * D], 256) for i in range(2)],
                            axis=1).reshape(8, P, CHUNK),
        "up": inward_chunks(a["w_up_2"][0]), "down": outward_chunks(a["w_down_2"][0]),
    }
    arrays = {k: np.ascontiguousarray(v) for k, v in arrays.items()}
    nc = bacc.Bacc("TRN2", target_bir_lowering=False, num_devices=1)
    dram = {k: nc.dram_tensor(k, v.shape, F32, kind="ExternalInput").ap() for k, v in arrays.items()}
    dram["out"] = nc.dram_tensor("out", (P, KD, SEQ), F32, kind="ExternalOutput").ap()
    build(nc, dram)
    got = run_bass_kernel_spmd(nc, [arrays], core_ids=[0]).results[0]["out"]
    return got.transpose(2, 1, 0).reshape(1, SEQ, D)
```

```python
from contextlib import ExitStack
from itertools import count

import numpy as np

import concourse.bass as bass
from concourse import mybir

ALU = mybir.AluOpType
ACT = mybir.ActivationFunctionType
AX = mybir.AxisListType
F32 = mybir.dt.float32
F32R = mybir.dt.float32r

P = 128
D = 1024
KD = D // P
SEQ = 256
TOK = 2 * SEQ
TT = TOK // P
X_TILES = SEQ // P
EPS = 1e-6
F = 2816
KF = F // P
N_MOD = 9
N_MOD_2 = 6

HEADS = 4
HEAD = 128
W_A = HEADS * HEAD
GROUPS_B = 4
W_B = GROUPS_B * P

C_HEADS = 16
C_KV = 4
C_DIM = 64
ROPE_BASE = 10000.0
GRID_W = 64

M_HEADS = 16
NOPE = 64
ROPE = 32
QD = NOPE + ROPE
V_DIM = 64
Q_RANK = 384
KV_RANK = 256
HEADS_AT_ONCE = 4

S_HEADS = 16
S_DIM = 64
S_GROUPS = 2
S_STATE = 128
S_PER = S_HEADS // S_GROUPS
D_INNER = S_HEADS * S_DIM
S_CONV = 5

MASKED = -1e30
CHUNK = 2048
RAW_SLOTS = 4
SPLIT_SLOTS = 3
A_SLOTS = 12
TEMPS = 6

VECTORS = {}
N_VECTORS = 0
for _name, _n in (("ada_b", 2 * N_MOD * KD), ("b_mod", N_MOD_2 * KD), ("conv", 3 * 8), ("mnorm", 4),
                  ("sgu", 4), ("final", KD), ("mix_pre", KD), ("mix_post", KD), ("q_norm", 3),
                  ("kv_norm", 2), ("sconv_w", S_CONV * 12), ("sconv_b", 12), ("ssd_norm", KD),
                  ("ssd_d", KD), ("ffn_pre", KD), ("ffn_post", KD), ("fconv_w", 3 * KF), ("fconv_b", KF),
                  ("c", 4 * KD), ("gate_b", 16), ("sink", 16), ("dt_b", 32), ("a_log", 32)):
    VECTORS[_name] = (N_VECTORS, _n)
    N_VECTORS += _n

MATRICES = ["ident", "tri_f", "tri_b", "mask_f", "mask_b", "ones", "swap", "turn", "sum_groups"]


def shape_constants():
    i = np.arange(P)
    le = (i[:, None] <= i[None, :]).astype(np.float32)
    swap = np.zeros((P, P), np.float32)
    swap[i[1::2], i[0::2]] = -1.0
    swap[i[0::2], i[1::2]] = 1.0
    turn = np.zeros((P, P), np.float32)
    for base in (NOPE, NOPE + 16):
        for j in range(8):
            turn[base + 8 + j, base + j] = -1.0
            turn[base + j, base + 8 + j] = 1.0
    sum_groups = np.zeros((P, P), np.float32)
    for g in range(4):
        sum_groups[32 * g, 0] = sum_groups[32 * g + 1, 1] = 1.0
    mats = {"ident": np.eye(P, dtype=np.float32), "tri_f": le, "tri_b": le.T,
            "mask_f": np.where(le > 0, 0, MASKED), "mask_b": np.where(le.T > 0, 0, MASKED),
            "ones": np.ones((P, P)), "swap": swap, "turn": turn, "sum_groups": sum_groups}
    square = np.concatenate([mats[m] for m in MATRICES], axis=1).astype(np.float32)

    row = (np.arange(SEQ) // GRID_W).astype(np.float32)
    col = (np.arange(SEQ) % GRID_W).astype(np.float32)
    n_freq = C_DIM // 4
    inv = np.float32(ROPE_BASE) ** (-np.arange(n_freq, dtype=np.float32) / np.float32(n_freq))
    ang = np.concatenate([row[:, None] * inv, col[:, None] * inv], axis=1)
    ang = np.repeat(ang, 2, axis=1).T
    ang = np.concatenate([ang, ang], axis=0)
    q = np.arange(SEQ)
    near = np.where(np.abs(q[:, None] - q[None, :]) <= P, 0.0, MASKED)
    odd = np.concatenate([np.cos(ang), np.sin(ang), near[:P], near[P:]], axis=1).astype(np.float32)

    axis = ROPE // 2
    inv = np.float32(ROPE_BASE) ** (-np.arange(0, axis, 2, dtype=np.float32) / np.float32(axis))
    ar, ac = row[:, None] * inv, col[:, None] * inv
    ang = np.concatenate([ar, ar, ac, ac], axis=1).T
    mla = np.zeros((P, 2 * SEQ), np.float32)
    mla[:NOPE, :SEQ] = 1.0
    mla[NOPE:QD, :SEQ] = np.cos(ang)
    mla[NOPE:QD, SEQ:] = np.sin(ang)
    return square, odd, mla




class Mark:

    def __init__(self, semaphore, value):
        self.semaphore, self.value = semaphore, value


class Line:

    def __init__(self, semaphore):
        self.semaphore, self.count, self.steps, self.passed = semaphore, 0, [], {}

    def wait(self, *marks):
        for m in marks:
            if m is None:
                continue
            if isinstance(m, (list, tuple)):
                self.wait(*m)
                continue
            if self.passed.get(id(m.semaphore), 0) < m.value:
                self.passed[id(m.semaphore)] = m.value
                self.steps.append((None, m.semaphore, m.value))

    def do(self, emit, *after, counted=True):
        self.wait(*after)
        if counted:
            self.count += 1
            self.steps.append((emit, self.semaphore, 1))
        else:
            self.steps.append((emit, None, 0))
        return Mark(self.semaphore, self.count)

    def load(self, out, in_, semaphore, value, *after):
        self.wait(*after)
        self.steps.append((lambda e: e.dma_start(out, in_), semaphore, 16))
        return Mark(semaphore, value)

    def last(self):
        return Mark(self.semaphore, self.count)

    def run(self, engine):
        for emit, semaphore, n in self.steps:
            if emit is None:
                engine.wait_ge(semaphore, n)
            elif semaphore is None:
                emit(engine)
            else:
                emit(engine).then_inc(semaphore, n)


class Buffers:

    def __init__(self, buffers):
        self.free = [(b, ()) for b in buffers]

    def take(self):
        return self.free.pop(0)

    def give(self, buffer, *last_use):
        self.free.append((buffer, last_use))


class Chunk:
    pass


class Program:

    def __init__(self, nc, dram, mem, sems, order):
        self.nc, self.dram, self.mem, self.sems = nc, dram, mem, sems
        self.PE, self.ACT, self.DVE, self.SP, self.POOL = (Line(sems[n]) for n in ("pe", "act", "dve", "sp", "pool"))
        self.banks = Buffers(mem["banks"])
        self.temps = Buffers(mem["temps"])
        self.columns = Buffers(mem["columns"])
        self.order = order
        self.asked = []
        self.loaded = self.prepared = self.finished = 0
        self.chunks = {}
        self.raw_free = [None] * RAW_SLOTS
        self.split_free = [None] * SPLIT_SLOTS
        self.n_split = 0
        self.split_done = 0
        self.a_free = [None] * A_SLOTS
        self.a_next = 0
        self.side = []

    def tt(self, out, a, b, op, *after, line=None):
        return (line or self.DVE).do(lambda e: e.tensor_tensor(out, a, b, op), *after)

    def copy(self, out, a, *after):
        return self.DVE.do(lambda e: e.tensor_copy(out, a), *after)

    def ts(self, out, a, s1, s2, op0, op1, *after):
        if op1 is None:
            return self.DVE.do(lambda e: e.tensor_scalar(out, a, s1, None, op0), *after)
        return self.DVE.do(lambda e: e.tensor_scalar(out, a, s1, s2, op0, op1), *after)

    def stt(self, out, a, s, b, op0, op1, *after):
        return self.DVE.do(lambda e: e.scalar_tensor_tensor(out=out, in0=a, scalar=s, in1=b, op0=op0, op1=op1),
                           *after)

    def act(self, out, in_, func, *after, **kw):
        return self.ACT.do(lambda e: e.activation(out, in_, func, **kw), *after)

    def mm(self, out, lhs, rhs, start, stop, *after, counted=False):
        return self.PE.do(lambda e: e.matmul(out, lhs, rhs, start=start, stop=stop, skip_group_check=True),
                          *after, counted=counted)

    def turn(self, out, in_, *after, counted=False):
        ident = self.mat("ident")[0:in_.shape[0], 0:in_.shape[0]]
        return self.PE.do(lambda e: e.transpose(out, in_, ident), *after, counted=counted)

    def mm3(self, out, w, x, start, stop, *after, counted=False):
        (wh, wl), (xh, xl) = w, x
        self.mm(out, wh, xh, start, False, *after)
        self.mm(out, wh, xl, False, False)
        return self.mm(out, wl, xh, False, stop, counted=counted)

    def split(self, hi, lo, value, *after):
        m = self.act(hi, value, ACT.Copy, *after)
        return self.tt(lo, value, hi.bitcast(F32), ALU.subtract, m, *after)

    def vec(self, name, i=0, n=1):
        at = VECTORS[name][0] + i
        return self.mem["vectors"][:, at:at + n]

    def mat(self, name):
        at = MATRICES.index(name) * P
        return self.mem["matrices"][:, at:at + P]

    def barrier(self):
        marks = [x.last() for x in (self.PE, self.ACT, self.DVE, self.POOL) if x.count]
        for x in (self.PE, self.ACT, self.DVE, self.POOL, self.SP):
            x.wait(*marks)
        return marks

    def load_ahead(self):
        while self.loaded < len(self.order):
            i = self.loaded
            name, at, width, _ = self.order[i]
            slot = i % RAW_SLOTS
            if i >= RAW_SLOTS and self.raw_free[slot] is None:
                return
            free = self.raw_free[slot]
            self.raw_free[slot] = None
            raw = self.mem["raw"][slot][:, 0:width]
            c = Chunk()
            c.index, c.raw = i, raw
            c.landed = self.SP.load(raw, self.dram[name][at, :, 0:width], self.sems["raw"][slot],
                                    16 * (i // RAW_SLOTS + 1), free)
            self.chunks[i] = c
            self.loaded += 1

    def prepare(self, i):
        name, at, width, parts = self.order[i]
        c = self.chunks[i]
        slot = i % RAW_SLOTS
        if not parts:
            c.ready = c.landed
            return
        s = self.n_split % SPLIT_SLOTS
        self.n_split += 1
        c.split_slot = s
        c.hi, c.lo = self.mem["w_hi"][s][:, 0:width], self.mem["w_lo"][s][:, 0:width]
        c.ready = self.split(c.hi, c.lo, c.raw, c.landed, self.split_free[s])
        self.raw_free[slot] = c.ready

    def next_chunk(self, name, at, width, parts=True):
        i = len(self.asked)
        self.asked.append((name, at, width, parts))
        if self.order is None:
            c = Chunk()
            c.hi = c.lo = None
            c.raw = self.mem["raw"][0][:, 0:width]
            c.hi, c.lo = self.mem["w_hi"][0][:, 0:width], self.mem["w_lo"][0][:, 0:width]
            c.ready = None
            c.index = i
            return c
        assert self.order[i] == (name, at, width, parts)
        self.load_ahead()
        while self.prepared < len(self.order):
            if self.prepared >= self.loaded:
                break
            if self.order[self.prepared][3]:
                if self.n_split - self.split_done >= SPLIT_SLOTS:
                    break
            self.prepare(self.prepared)
            self.prepared += 1
            self.load_ahead()
        assert self.prepared > i, "chunk is not ready"
        return self.chunks[i]

    def done_with(self, c, mark):
        if self.order is None:
            return
        if self.order[c.index][3]:
            self.split_free[c.split_slot] = mark
            self.split_done += 1
        else:
            self.raw_free[c.index % RAW_SLOTS] = mark

    def modulation(self, name, k, pair, dest, bias, sections):
        per = D // 256
        self.side += [(name, k, sec, q, pair, dest, bias, sections) for sec in sections for q in range(per)]

    def side_step(self, n=1):
        for _ in range(n):
            if not self.side:
                return
            name, k, sec, q, pair, dest, bias, _ = self.side.pop(0)
            chunk = self.next_chunk(name, k + sec * 4 + q, CHUNK, parts=False)
            w = chunk.raw.rearrange("p (k n) -> p k n", k=KD)
            bank, free = self.banks.take()
            for kt in range(KD):
                g = kt % 4
                m = self.mm(bank[32 * g:32 * g + 32, 0:256], self.mem["silu_c"][:, pair, kt, :], w[:, kt, :],
                            kt < 4, kt >= 4, chunk.ready, free, self.silu_c_ready, counted=kt == KD - 1)
            self.done_with(chunk, m)
            row, row_free = self.temps.take()
            m = self.act(row[:, 0:256], bank[:, 0:256], ACT.Copy, m, row_free)
            self.banks.give(bank, m)
            self.end_side()
            self.side_open = (row, m, dest, bias, sec * KD + 2 * q)

    side_open = None

    def end_side(self):
        if self.side_open is None:
            return
        row, ready, dest, bias, at = self.side_open
        self.side_open = None
        bank, free = self.banks.take()
        for j in range(2):
            m = self.mm(bank[:, 2 * j:2 * j + 2], row[:, j * P:(j + 1) * P], self.mat("sum_groups")[:, 0:2],
                        True, True, ready, free, counted=j == 1)
        self.temps.give(row, m)
        m = self.tt(dest[:, at:at + 2, :], bank[:, 0:4].rearrange("p (j s) -> p j s", j=2),
                    self.vec(bias[0], bias[1] + at, 2).unsqueeze(2).broadcast_to((P, 2, 2)), ALU.add, m)
        self.banks.give(bank, m)

    def section(self, dest, sec, op, value):
        view = dest[:, sec * KD:(sec + 1) * KD, :]
        return self.ts(view, view, value, None, op, None, self.DVE.last())

    def finish_side(self):
        while self.side:
            self.side_step()
        self.end_side()

    def add_squares(self, bank, i, count, squares, *after):
        rows = slice(32 * (i % 4), 32 * (i % 4) + 32)
        return self.mm(bank[rows, 0:squares.shape[1]], self.mat("ones")[:, 0:32], squares, i < 4,
                       i + 4 >= count, *after, counted=True)

    def rstd(self, bank, count, n, width, *after):
        rows = 32 * min(count, 4)
        sums, free = self.temps.take()
        m = self.act(sums[0:rows, 0:n], bank[0:rows, 0:n], ACT.Copy, *after, free)
        self.banks.give(bank, m)
        total, free = self.banks.take()
        tiles = n // P
        for tt in range(tiles):
            m = self.mm(total[:, tt:tt + 1], sums[0:rows, tt * P:(tt + 1) * P], self.mat("sum_groups")[0:rows, 0:1],
                        True, True, m, free, counted=tt == tiles - 1)
        self.temps.give(sums, m)
        col, free = self.columns.take()
        inv = col[:, 0:tiles]
        m = self.act(inv, total[:, 0:tiles], ACT.Sqrt, m, free, scale=1.0 / width, bias=self.mem["eps"][:, 0:1])
        self.banks.give(total, m)
        m = self.DVE.do(lambda e: e.reciprocal(inv, inv), m)
        wide, free = self.banks.take()
        m = self.spread(wide, inv, tiles, m, free)
        self.columns.give(col, m)
        return wide, m

    def spread(self, bank, columns, tiles, *after):
        for tt in range(tiles):
            m = self.mm(bank[:, tt * P:(tt + 1) * P], columns[:, tt:tt + 1].broadcast_to((P, P)),
                        self.mat("ident"), True, True, *after, counted=tt == tiles - 1)
        return m

    def norm_of(self, tiles, n, width, *after):
        bank, free = self.banks.take()
        for i, t in enumerate(tiles):
            sq, sq_free = self.temps.take()
            m = self.act(sq[:, 0:n], t, ACT.Square, sq_free, *after)
            m = self.add_squares(bank, i, len(tiles), sq[:, 0:n], m, free)
            self.temps.give(sq, m)
        return self.rstd(bank, len(tiles), n, width, m)

    def load_root_table(self):
        self.act(self.mem["eps"][:, 1:2], self.mem["eps"][:, 0:1], ACT.Sqrt, self.ACT.last())

    def add_square(self, k, n):
        if not self.squares:
            self.square_bank, self.square_free = self.banks.take()
            self.square_count = 0
            self.load_root_table()
        sq, free = self.temps.take()
        m = self.act(sq[:, 0:n], self.mem["h"][:, k, 0:n], ACT.Square, free, self.h_ready[k])
        self.squares.append((sq, m, n))
        if self.square_count < len(self.squares) - 2:
            self.sum_square()

    def sum_square(self):
        sq, m, n = self.squares[self.square_count]
        m = self.add_squares(self.square_bank, self.square_count, KD, sq[:, 0:n], m, self.square_free)
        self.temps.give(sq, m)
        self.square_count += 1
        return m

    def h_rstd(self, n):
        while self.square_count < KD:
            m = self.sum_square()
        self.squares = []
        return self.rstd(self.square_bank, KD, n, D, m)

    squares = ()

    def norm(self, scale, shift, n, *after):
        h, n_hi, n_lo = self.mem["h"], self.mem["n_hi"], self.mem["n_lo"]
        inv, m = self.h_rstd(n)
        ready, scaled = [], []
        parts = [(s, slice(s * SEQ, (s + 1) * SEQ)) for s in range(n // SEQ)]

        def finish():
            k, t, marks = scaled.pop(0)
            for (s, at), a in zip(parts, marks):
                b = self.act(n_hi[:, k, at], t[:, at], ACT.Identity, a, bias=shift(k, s))
                c = self.stt(n_lo[:, k, at], t[:, at], shift(k, s), n_hi[:, k, at].bitcast(F32), ALU.add,
                             ALU.subtract, b)
            self.temps.give(t, c)
            ready.append(c)

        for k in range(KD):
            t, free = self.temps.take()
            scaled.append((k, t, [self.stt(t[:, at], h[:, k, at], scale(k, s), inv[:, at], ALU.mult, ALU.mult, m,
                                           free, after) for s, at in parts]))
            if k:
                finish()
        finish()
        self.banks.give(inv, self.DVE.last())
        return ready

    def mod_scale(self, dest, sec):
        return lambda k, s: dest[:, sec * KD + k, s:s + 1]

    def project(self, name, at, ktiles, cols, n, sources, ready, finish, first=True, last=True,
                banks=None, tokens=False, col0=0):
        chunk = self.next_chunk(name, at, ktiles * cols)
        hi = chunk.hi.rearrange("p (k n) -> p k n", k=ktiles)
        lo = chunk.lo.rearrange("p (k n) -> p k n", k=ktiles)
        out = []
        for t in range(cols // P):
            bank, free = self.banks.take() if banks is None else banks[t]
            for k in range(ktiles):
                c = slice(t * P, (t + 1) * P)
                xh, xl = sources(k)
                m = self.mm3(bank[:, 0:n], (hi[:, k, c], lo[:, k, c]), (xh, xl), first and k == 0,
                             last and k == ktiles - 1, chunk.ready, free, ready[k] if ready else None,
                             counted=k == ktiles - 1)
            out.append((bank, m))
        self.done_with(chunk, m)
        if last:
            for t, (bank, m) in enumerate(out):
                finish(t, bank, m)
        return out

    def project_group(self, specs, n, sources, ready):
        opened = []
        for name, at, cols, finish in specs:
            chunk = self.next_chunk(name, at, KD * cols)
            parts = [x.rearrange("p (k n) -> p k n", k=KD) for x in (chunk.hi, chunk.lo)]
            opened.append((chunk, parts, [self.banks.take() for _ in range(cols // P)], finish))
        for k in range(KD):
            for chunk, (hi, lo), banks, finish in opened:
                for t, (bank, free) in enumerate(banks):
                    c = slice(t * P, (t + 1) * P)
                    m = self.mm3(bank[:, 0:n], (hi[:, k, c], lo[:, k, c]), sources(k), k == 0, k == KD - 1,
                                 chunk.ready, free, ready[k], counted=k == KD - 1)
                    if k == KD - 1:
                        banks[t] = (bank, m)
                if k == KD - 1:
                    self.done_with(chunk, m)
        for _, _, banks, finish in opened:
            for t, (bank, m) in enumerate(banks):
                finish(t, bank, m)

    def project_tokens(self, name, at, ktiles, cols, tiles, sources, ready, finish, view=None):
        chunk = self.next_chunk(name, at, ktiles * cols) if view is None else view
        hi = chunk.hi.rearrange("p (k n) -> p k n", k=ktiles)
        lo = chunk.lo.rearrange("p (k n) -> p k n", k=ktiles)
        for pair in range(len(tiles) // 2):
            bank, free = self.banks.take()
            for j in range(2):
                tt = tiles[2 * pair + j]
                for k in range(ktiles):
                    xh, xl = sources(k, tt)
                    m = self.mm3(bank[:, j * cols:(j + 1) * cols], (xh, xl), (hi[:, k, :], lo[:, k, :]), k == 0,
                                 k == ktiles - 1, chunk.ready, free, ready[k] if ready else None,
                                 counted=k == ktiles - 1)
            if pair == len(tiles) // 2 - 1:
                self.done_with(chunk, m)
            finish(pair, bank, m)

    def n_parts(self, k, n=TOK):
        return self.mem["n_hi"][:, k, 0:n], self.mem["n_lo"][:, k, 0:n]

    def add_gated(self, bank, m, k, gate, n, final=True):
        h = self.mem["h"]
        for s in range(n // SEQ):
            at = slice(s * SEQ, (s + 1) * SEQ)
            e = self.stt(h[:, k, at], bank[:, at], gate(k, s), h[:, k, at], ALU.mult, ALU.add, m)
        self.banks.give(bank, e)
        self.h_ready[k] = e
        if final:
            self.add_square(k, n)

    def ffn(self, w_in, w_out, dest, secs, n):
        ready = self.norm(self.mod_scale(dest, secs[1]), self.mod_scale(dest, secs[0]), n)
        self.hidden(w_in, w_out, n, ready, self.silu_gate,
                    lambda k, bank, m, final: self.add_gated(bank, m, k, self.mod_scale(dest, secs[2]), n, final))

    def silu_gate(self, j, n, g_bank, g_mark, u_bank, u_mark):
        t, free = self.temps.take()
        m = self.act(t[:, 0:n], g_bank[:, 0:n], ACT.Silu, g_mark, free)
        self.banks.give(g_bank, m)
        m = self.tt(t[:, 0:n], t[:, 0:n], u_bank[:, 0:n], ALU.mult, m, u_mark)
        self.banks.give(u_bank, m)
        return t, m

    def hidden(self, w_in, w_out, n, ready, gate, finish):
        a_hi, a_lo = self.mem["a_hi"], self.mem["a_lo"]
        placed = {}

        def inward(j):
            found = {}
            self.side_step()
            self.project(w_in[0], w_in[1] + j, KD, 2 * P, n, lambda k: self.n_parts(k, n), ready,
                         lambda t, bank, m: found.__setitem__(t, (bank, m)))
            gated(j, found)

        def gated(j, found):
            t, m = gate(j, n, *found[0], *found[1])
            slot = self.a_next % A_SLOTS
            self.a_next += 1
            e = self.split(a_hi[:, slot, 0:n], a_lo[:, slot, 0:n], t[:, 0:n], m, self.a_free[slot])
            self.temps.give(t, e)
            placed[j] = (slot, e)

        def outward(half):
            tiles = list(range(half * (KF // 2), (half + 1) * (KF // 2)))
            parts = [tiles[0:6], tiles[6:11]]
            for q in range(D // 256):
                banks = None
                for i, part in enumerate(parts):
                    self.side_step()
                    at = w_out[1] + (half * (D // 256) + q) * 2 + i
                    banks = self.project(w_out[0], at, len(part), 256, n,
                                         lambda k: (a_hi[:, placed[part[k]][0], 0:n], a_lo[:, placed[part[k]][0], 0:n]),
                                         [placed[j][1] for j in part],
                                         lambda t, bank, m: finish(2 * q + t, bank, m, half == 1),
                                         first=i == 0, last=i == 1,
                                         banks=None if banks is None else [(b, mk) for b, mk in banks])
            for j in tiles:
                self.a_free[placed[j][0]] = self.PE.last()

        half = KF // 2
        found = [{}, {}]
        self.side_step()
        self.project_group([(w_in[0], w_in[1] + j, 2 * P, lambda t, bank, m, j=j: found[j].__setitem__(t, (bank, m)))
                            for j in range(2)], n, lambda k: self.n_parts(k, n), ready)
        for j in range(2):
            gated(j, found[j])
        for j in range(2, half + 1):
            inward(j)
        outward(0)
        for j in range(half + 1, KF):
            inward(j)
        outward(1)

    def even_mixer(self, dest):
        mem = self.mem
        n = TOK
        self.barrier()
        ready = self.norm(self.mod_scale(dest, 4), self.mod_scale(dest, 3), n)
        q_t, k_t, v, o_t, u_t, vb = (mem[x] for x in ("e_q", "e_k", "e_v", "e_o", "e_u", "e_vb"))
        tables = self.SP.load(mem["stage"][:, :], self.dram["even_tables"], self.sems["stage"], 16)
        ws_t = mem["stage"][:, 0:4 * P].rearrange("q (g p) -> q g p", g=GROUPS_B)
        sb = mem["stage"][:, 4 * P:8 * P].rearrange("c (g p) -> c g p", g=GROUPS_B)
        src = lambda k: self.n_parts(k)
        src_t = lambda k, tt: (mem["n_hi"][:, k, tt * P:(tt + 1) * P], mem["n_lo"][:, k, tt * P:(tt + 1) * P])

        def conv(base, out):
            def finish(t, bank, m):
                tile = base + t
                x, free = self.temps.take()
                xv = x[:, :].rearrange("p (s t) -> p s t", s=2)
                bv = bank[:, :].rearrange("p (s t) -> p s t", s=2)
                w = lambda tap: self.vec("conv", tap * 8 + tile)
                m = self.act(x[:, :], bank[:, :], ACT.Copy, m, free, scale=w(1))
                m = self.stt(xv[:, :, 1:SEQ], bv[:, :, 0:SEQ - 1], w(0), xv[:, :, 1:SEQ], ALU.mult, ALU.add, m)
                m = self.stt(xv[:, :, 0:SEQ - 1], bv[:, :, 1:SEQ], w(2), xv[:, :, 0:SEQ - 1], ALU.mult, ALU.add, m)
                self.banks.give(bank, m)
                m = self.act(out[:, tile % 4, :], x[:, :], ACT.Silu, m)
                self.temps.give(x, m)
            return finish

        self.project_group([("even_in", c, 256, conv(2 * c, q_t)) for c in range(2)], n, src, ready)
        for c in range(2, 4):
            self.project("even_in", c, KD, 256, n, src, ready, conv(2 * c, k_t))
        for c in range(2):
            def store_v(pair, bank, m, c=c):
                m = self.act(v[:, 2 * pair:2 * pair + 2, c * 256:(c + 1) * 256],
                             bank[:, :].rearrange("p (t n) -> p t n", t=2), ACT.Copy, m)
                self.banks.give(bank, m)
            self.project_tokens("even_in", 4 + c, KD, 256, range(TT), src_t, ready, store_v)
        for c in range(2):
            def store_o(t, bank, m, c=c):
                self.banks.give(bank, self.act(o_t[:, 2 * c + t, :], bank[:, :], ACT.Sigmoid, m))
            self.project("even_in", 6 + c, KD, 256, n, src, ready, store_o)
        small = mem["small"]
        gates = small[:, 0:TT * 16].rearrange("p (t g) -> p t g", t=TT)
        gate_marks = []

        def store_gates(pair, bank, m):
            e = self.tt(gates[:, 2 * pair:2 * pair + 2, :], bank[:, 0:32].rearrange("p (t g) -> p t g", t=2),
                        self.vec("gate_b", 0, 16).unsqueeze(1).broadcast_to((P, 2, 16)), ALU.add, m)
            self.banks.give(bank, e)
            gate_marks.append(e)
        self.project_tokens("even_gates", 0, KD, 16, range(TT), src_t, ready, store_gates)
        for c in range(2):
            def store_u(t, bank, m, c=c):
                self.banks.give(bank, self.act(u_t[:, 2 * c + t, :], bank[:, :], ACT.Gelu_apprx_tanh, m))
            self.project("even_in", 8 + c, KD, 256, n, src, ready, store_u)
        for c in range(2):
            def store_vb(pair, bank, m, c=c):
                m = self.act(vb[:, 2 * pair:2 * pair + 2, c * 256:(c + 1) * 256],
                             bank[:, :].rearrange("p (t n) -> p t n", t=2), ACT.Gelu_apprx_tanh, m)
                self.banks.give(bank, m)
            self.project_tokens("even_in", 10 + c, KD, 256, range(TT), src_t, ready, store_vb)

        ss = small[:, 64:64 + TT]
        for tt in range(TT):
            sq, free = self.temps.take()
            m = self.act(sq[:, :], vb[:, tt, :], ACT.Square, free, self.ACT.last(), accum_out=ss[:, tt:tt + 1])
            self.temps.give(sq, m)
        m = self.act(ss, ss, ACT.Sqrt, m, scale=1.0 / W_B, bias=mem["eps"][:, 0:1])
        m = self.DVE.do(lambda e: e.reciprocal(ss, ss), m)
        for tt in range(TT):
            m2 = self.ts(vb[:, tt, :], vb[:, tt, :], ss[:, tt:tt + 1], None, ALU.mult, None, m)
        b_done = []
        n_read = self.PE.last()
        for g in range(GROUPS_B):
            bank, free = self.banks.take()
            for tt in range(TT):
                m = self.mm(bank[:, tt * P:(tt + 1) * P], vb[:, tt, g * P:(g + 1) * P], ws_t[:, g, :], True, True,
                            m2, tables, free, counted=tt == TT - 1)
            t, free = self.temps.take()
            m = self.stt(t[:, :].rearrange("p (t c) -> p t c", t=TT), bank[:, :].rearrange("p (t c) -> p t c", t=TT),
                         self.vec("sgu", g), sb[:, g, :].unsqueeze(1).broadcast_to((P, TT, P)), ALU.mult, ALU.add,
                         m, free)
            self.banks.give(bank, m)
            m = self.tt(t[:, :], t[:, :], u_t[:, g, :], ALU.mult, m, self.ACT.last())
            m = self.split(mem["n_hi"][:, 4 + g, :], mem["n_lo"][:, 4 + g, :], t[:, :], m, n_read)
            self.temps.give(t, m)
            b_done.append(m)

        self.barrier()
        gv = gates.rearrange("p t (d w h) -> p t d w h", d=2, w=2)
        lf = small[:, 96:96 + 8 * TT].rearrange("p (t d h) -> p t d h", t=TT, d=2)
        e1 = small[:, 128:128 + 8 * TT].rearrange("p (t d h) -> p t d h", t=TT, d=2)
        c_col = small[:, 160:160 + 8 * TT].rearrange("p (t d h) -> p t d h", t=TT, d=2)
        for tt in range(TT):
            m = self.log_one_plus_exp(lf[:, tt], e1[:, tt], gv[:, tt, :, 1, :], -1.0, gate_marks,
                                      small[:, 192:200].rearrange("p (d h) -> p d h", d=2))
        m = self.ts(lf, lf, -1.0, None, ALU.mult, None, m)
        bank, free = self.banks.take()
        bv = bank[:, 0:8 * TT].rearrange("p (t d h) -> p t d h", t=TT, d=2)
        for tt in range(TT):
            for d in range(2):
                tri = self.mat(("tri_f", "tri_b")[d])
                m2 = self.mm(bv[:, tt, d, :], tri, lf[:, tt, d, :], True, True, m, free, counted=True)
        m = self.tt(c_col, gv[:, :, :, 0, :], bv, ALU.subtract, m2)
        self.banks.give(bank, m)
        self.mlstm(q_t, k_t, v, lf, c_col, m)

        h_sum = mem["e_vb"][:, :, :]
        for h in range(HEADS):
            bank, m = self.norm_of([h_sum[:, h, :]], n, HEAD, self.DVE.last())
            inv, free = self.temps.take()
            m = self.tt(inv[:, :], bank[:, :], h_sum[:, h, :], ALU.mult, m, free)
            self.banks.give(bank, m)
            m = self.stt(inv[:, :], inv[:, :], self.vec("mnorm", h), o_t[:, h, :], ALU.mult, ALU.mult, m)
            m = self.split(mem["n_hi"][:, h, :], mem["n_lo"][:, h, :], inv[:, :], m, self.PE.last())
            self.temps.give(inv, m)
        for c in range(4):
            self.project("even_out", c, KD, 256, n, src, [m] * KD,
                         lambda t, bank, mk, c=c: self.add_gated(bank, mk, 2 * c + t, self.mod_scale(dest, 5), n))
        self.barrier()

    def log_one_plus_exp(self, out, e1, x, sign, after, tmp):
        m = self.ts(tmp, x, -1.0, None, ALU.mult, None, *after, self.DVE.last())
        m = self.tt(e1, tmp, x, ALU.min, m)
        m = self.act(e1, e1, ACT.Exp, m)
        m = self.ts(tmp, e1, 1.0, None, ALU.add, None, m)
        ln = self.act(out, tmp, ACT.Ln, m)
        m = self.stt(e1, tmp, 1.0, e1, ALU.subtract, ALU.subtract, m)
        r = self.DVE.do(lambda e: e.reciprocal(tmp, tmp), m, ln)
        m = self.tt(e1, e1, tmp, ALU.mult, r)
        m = self.tt(out, out, e1, ALU.subtract, m, ln)
        m = self.ts(tmp, x, sign, 0.0, ALU.mult, ALU.max, m)
        return self.tt(out, out, tmp, ALU.add, m)

    def mlstm(self, q_t, k_t, v, lf, c_col, m_cols):
        mem, small = self.mem, self.mem["small"]
        h_sum = mem["e_vb"]
        scale = HEAD ** -0.5
        order = ([2, 3, 0, 1], [3, 2, 1, 0])
        state = [mem["e_c0"], mem["e_c1"]]
        n_state = [small[:, 200 + 4 * d:204 + 4 * d] for d in range(2)]
        m_state = [[small[:, 208 + 4 * (2 * d + i):212 + 4 * (2 * d + i)] for i in range(2)] for d in range(2)]
        wide = lambda ap: ap.rearrange("p (h t) -> p h t", h=HEADS)
        ones, ident = self.mat("ones"), self.mat("ident")
        tiles = Buffers(mem["e_tiles"])
        tiles.free += self.temps.free
        m_ready = [self.DVE.do(lambda e, d=d: e.memset(m_state[d][0], 0.0), m_cols) for d in range(2)]
        s_ready = [None, None]
        h_first = [None] * TT
        m_prev_used = [[None] * (TT + 2) for d in range(2)]
        w_used = [[None] * (TT + 2) for d in range(2)]

        def each_head(emit):
            for h in range(HEADS):
                m = emit(h, slice(h * P, (h + 1) * P), h == HEADS - 1)
            return m

        def item(d, step):
            tt = order[d][step]
            cols = slice(tt * P, (tt + 1) * P)
            tri, mask = self.mat(("tri_f", "tri_b")[d]), self.mat(("mask_f", "mask_b")[d])
            end = P - 1 if d == 0 else 0
            m_prev, m_next = m_state[d][step % 2], m_state[d][(step + 1) % 2]
            more = step < TT - 1
            b_bank, free = self.banks.take()
            each_head(lambda h, at, last: self.mm(b_bank[:, at], lf[:, tt, d, h:h + 1].broadcast_to((P, P)), tri,
                                                  True, True, free, m_cols))
            c_bank, free = self.banks.take()
            mc = each_head(lambda h, at, last: self.mm(c_bank[:, at], c_col[:, tt, d, h:h + 1].broadcast_to((P, P)),
                                                       ident, True, True, free, m_cols, counted=last))
            yield
            big_m, free = tiles.take()
            for h in range(HEADS):
                o, i = big_m[:, h * P:(h + 1) * P], c_bank[:, h * P:(h + 1) * P]
                if d == 1:
                    o, i = o[:, ::-1], i[:, ::-1]
                m_max = self.running_max(o, i, m_prev[:, h:h + 1], mc, free, m_ready[d])
            self.banks.give(c_bank, m_max)
            prev_ready = m_ready[d]
            m_end = wide(big_m[:, :])[:, :, end]
            m_ready[d] = self.tt(m_next, wide(b_bank[:, :])[:, :, end], m_end, ALU.add, m_max,
                                 m_prev_used[d][step])
            floor, free = tiles.take()
            m_floor = self.tt(floor[:, :], b_bank[:, :], big_m[:, :], ALU.add, m_max, free)
            self.banks.give(b_bank, m_floor, m_ready[d])
            dec, free = tiles.take()
            m_dec = self.tt(wide(dec[:, :]), mask.unsqueeze(1).broadcast_to((P, HEADS, P)), wide(big_m[:, :]),
                            ALU.subtract, m_max, free)
            w = small[:, 224 + 4 * (2 * d + step % 2):228 + 4 * (2 * d + step % 2)]
            m_w = self.tt(w, c_col[:, tt, d, :], m_end, ALU.subtract, m_max, w_used[d][step])
            s_bank, free = self.banks.take()
            m_s = each_head(lambda h, at, last: self.mm(s_bank[:, at], k_t[:, h, cols], q_t[:, h, cols], True, True,
                                                        free, counted=last))
            yield
            m_dec = each_head(lambda h, at, last: self.act(dec[:, at], dec[:, at], ACT.Exp, m_dec,
                                                           bias=c_col[:, tt, d, h:h + 1]))
            inter, free2 = tiles.take()
            m_int = each_head(lambda h, at, last: self.act(inter[:, at], big_m[:, at], ACT.Exp, m_max, free2,
                                                           prev_ready, scale=-1.0, bias=m_prev[:, h:h + 1]))
            m_prev_used[d][step + 1] = m_int
            m_w = self.act(w, w, ACT.Exp, m_w)
            m_floor = self.act(floor[0:1, :], floor[0:1, :], ACT.Exp, m_floor, scale=-1.0)
            tiles.give(big_m, m_int, m_w)
            if more:
                kt_bank, free3 = self.banks.take()
                m_k = each_head(lambda h, at, last: self.turn(kt_bank[:, at], k_t[:, h, cols], free3, counted=last))
            yield
            s, free4 = tiles.take()
            m_sc = self.stt(s[:, :], s_bank[:, :], scale, dec[:, :], ALU.mult, ALU.mult, m_s, m_dec, free4)
            self.banks.give(s_bank, m_sc)
            tiles.give(dec, m_sc)
            if step:
                qi, free5 = tiles.take()
                m_qi = self.tt(wide(qi[:, :]), q_t[:, :, cols], wide(inter[:, :]), ALU.mult, m_int, free5)
            if more:
                kw, free6 = tiles.take()
                m_w = self.ts(w, w, scale, None, ALU.mult, None, m_w)
                m_kw = self.tt(wide(kw[:, :]), wide(kt_bank[:, :]), w.unsqueeze(2).broadcast_to((P, HEADS, P)),
                               ALU.mult, m_k, m_w, free6)
                w_used[d][step + 2] = m_kw
                self.banks.give(kt_bank, m_kw)
            yield
            num, free7 = self.banks.take()
            den, free8 = self.banks.take()
            for h in range(HEADS):
                at = slice(h * P, (h + 1) * P)
                self.mm(num[:, at], v[:, tt, at], s[:, at], True, step == 0, free7, m_sc)
                if step:
                    self.mm(num[:, at], state[d][:, h, :], qi[:, at], False, True, m_qi, s_ready[d])
                m_d = self.mm(den[:, h:h + 1], s[:, at], ones[:, 0:1], True, step == 0, free8)
                if step:
                    m_d = self.mm(den[:, h:h + 1], qi[:, at], n_state[d][:, h:h + 1], False, True)
                m_d = self.mm(den[:, 4 + h:5 + h], floor[0:1, at], ones[0:1, 0:1], True, True, m_floor,
                              counted=h == HEADS - 1)
            tiles.give(s, m_d)
            tiles.give(floor, m_d)
            if step:
                tiles.give(qi, m_d)
            if more:
                c_loc, free9 = self.banks.take()
                n_loc = den[:, 8:12]
                for h in range(HEADS):
                    at = slice(h * P, (h + 1) * P)
                    self.mm(c_loc[:, at], kw[:, at], v[:, tt, at], True, True, m_kw, free9)
                    m_c = self.mm(n_loc[:, h:h + 1], kw[:, at], ones[:, 0:1], True, True,
                                  counted=h == HEADS - 1)
                tiles.give(kw, m_c)
                fade = wide(inter[:, :])[:, :, end]
                st = state[d]
                if step == 0:
                    m = self.copy(st[:, :, :], wide(c_loc[:, :]), m_c)
                    m = self.copy(n_state[d], n_loc[:, 0:HEADS], m_c)
                else:
                    m = self.tt(st[:, :, :], st[:, :, :], fade.unsqueeze(2).broadcast_to((P, HEADS, P)), ALU.mult,
                                m_d, m_int)
                    m2 = self.tt(n_state[d], n_state[d], fade, ALU.mult, m_d)
                    m = self.tt(st[:, :, :], st[:, :, :], wide(c_loc[:, :]), ALU.add, m, m_c)
                    m = self.tt(n_state[d], n_state[d], n_loc[:, 0:HEADS], ALU.add, m2)
                s_ready[d] = m
                self.banks.give(c_loc, m)
                tiles.give(inter, m)
            else:
                tiles.give(inter, m_int, self.DVE.last())
            col, free11 = self.columns.take()
            m = self.act(col[:, 0:8], den[:, 0:8], ACT.Abs, [m_c, s_ready[d]] if more else m_d, free11)
            self.banks.give(den, m, s_ready[d] if more else None)
            m = self.tt(col[:, 0:4], col[:, 0:4], col[:, 4:8], ALU.max, m)
            m = self.DVE.do(lambda e: e.reciprocal(col[:, 0:4], col[:, 0:4]), m)
            yield
            r_bank, free12 = self.banks.take()
            m = self.spread(r_bank, col, HEADS, m, free12)
            self.columns.give(col, m)
            r, free13 = tiles.take()
            m = self.act(r[:, :], r_bank[:, :], ACT.Copy, m, free13)
            self.banks.give(r_bank, m)
            yield
            if h_first[tt]:
                m = self.tt(wide(r[:, :]), wide(r[:, :]), wide(num[:, :]), ALU.mult, m)
                m = self.tt(h_sum[:, :, cols], h_sum[:, :, cols], wide(r[:, :]), ALU.add, m, h_first[tt])
            else:
                m = self.tt(h_sum[:, :, cols], wide(r[:, :]), wide(num[:, :]), ALU.mult, m)
            h_first[tt] = m
            self.banks.give(num, m)
            tiles.give(r, m)

        self.interleave([item(d, step) for step in range(TT) for d in range(2)], 2)
        done = (self.PE.last(), self.ACT.last(), self.DVE.last())
        self.temps.free = [(t, done) for t in mem["temps"]]

    def running_max(self, out, in_, start, *after):
        zeros = self.mem["zeros"][:, 0:1].broadcast_to((P, P))
        return self.DVE.do(lambda e: e.tensor_tensor_scan(out, zeros, in_, start, ALU.add, ALU.max), *after)

    def interleave(self, items, every=1):
        items, active = iter(items), []
        for n in count():
            if n % every == 0:
                new = next(items, None)
                if new is not None:
                    active.insert(0, new)
                elif not active:
                    return
            active = [x for x in active if next(x, "ended") != "ended"]

    def rope(self, out, bank, m, rows, cos, sin, turn, *after):
        x, free = self.temps.take()
        m = self.act(x[0:rows, 0:SEQ], bank[0:rows, 0:SEQ], ACT.Copy, m, free)
        self.banks.give(bank, m)
        self.rope_from(out, x, m, rows, cos, sin, turn, *after)

    def rope_from(self, out, x, m, rows, cos, sin, turn, *after):
        bank, free = self.banks.take()
        m = self.mm(bank[0:rows, 0:SEQ], turn[0:rows, 0:rows], x[0:rows, 0:SEQ], True, True, m, free, counted=True)
        m = self.tt(x[0:rows, SEQ:TOK], bank[0:rows, 0:SEQ], sin[0:rows, :], ALU.mult, m, *after)
        self.banks.give(bank, m)
        m = self.tt(x[0:rows, 0:SEQ], x[0:rows, 0:SEQ], cos[0:rows, :], ALU.mult, m)
        m = self.tt(out, x[0:rows, 0:SEQ], x[0:rows, SEQ:TOK], ALU.add, m)
        self.temps.give(x, m)
        return m

    def softmax(self, bank, m, scale, sink, out, out_free, done):
        col, free = self.columns.take()
        top, total = col[:, 0:1], col[:, 1:2]
        m = self.DVE.do(lambda e: e.tensor_reduce(top, bank[:, :], AX.X, ALU.max), m, free)
        if sink is None:
            m = self.ts(top, top, -scale, None, ALU.mult, None, m)
        else:
            m = self.ts(top, top, -scale, sink[1], ALU.mult, ALU.min, m)
        p, free = self.temps.take()
        m = self.act(p[:, :], bank[:, :], ACT.Exp, m, free, scale=scale, bias=top, accum_out=total)
        self.banks.give(bank, m)
        if sink is not None:
            m2 = self.act(col[:, 2:3], sink[0], ACT.Exp, bias=top)
        yield
        if sink is not None:
            m = self.tt(total, total, col[:, 2:3], ALU.add, m, m2)
        m = self.DVE.do(lambda e: e.reciprocal(total, total), m)
        m = self.ts(p[:, :], p[:, :], total, None, ALU.mult, None, m)
        self.columns.give(col, m)
        yield
        t_bank, free = self.banks.take()
        for k in range(TT):
            m2 = self.turn(t_bank[:, k * P:(k + 1) * P], p[:, k * P:(k + 1) * P], m, free, counted=k == TT - 1)
        self.temps.give(p, m2)
        m = self.act(out, t_bank[:, :].rearrange("p (k q) -> p k q", k=TT), ACT.Copy, m2, out_free)
        self.banks.give(t_bank, m)
        done.append(m)

    def odd_mixer(self, dest):
        mem = self.mem
        self.barrier()
        ready = self.norm(self.mod_scale(dest, 4), self.mod_scale(dest, 3), TOK)
        q_t, k_t, v = mem["o_q"], mem["o_k"], mem["o_v"]
        tables = self.SP.load(mem["stage"][:, :], self.dram["odd_tables"], self.sems["stage"], 32)
        cos, sin = mem["stage"][:, 0:SEQ], mem["stage"][:, SEQ:2 * SEQ]
        near = mem["stage"][:, 2 * SEQ:4 * SEQ].rearrange("q (b k) -> q b k", b=X_TILES)
        src_t = lambda k, tt: (mem["n_hi"][:, k, tt * P:(tt + 1) * P], mem["n_lo"][:, k, tt * P:(tt + 1) * P])
        swap = self.mat("swap")
        def store_k(t, bank, m):
            e = self.act(k_t[:, t, SEQ:TOK], bank[:, SEQ:TOK], ACT.Copy, m)
            self.rope(k_t[:, t, 0:SEQ], bank, e, P, cos, sin, swap, tables)
        self.project("odd_kv", 0, KD, 256, TOK, lambda k: self.n_parts(k), ready, store_k)

        def store_v(pair, bank, m):
            e = self.act(v[:, 2 * pair:2 * pair + 2, :], bank[:, :].rearrange("p (t n) -> p t n", t=2), ACT.Copy, m)
            self.banks.give(bank, e)
        self.project_tokens("odd_kv", 1, KD, 256, range(TT), src_t, ready, store_v)
        for c in range(4):
            self.project("odd_q", c, KD, 256, SEQ, lambda k: self.n_parts(k, SEQ), ready,
                         lambda t, bank, m, c=c: self.rope(q_t[:, 2 * c + t, :], bank, m, P, cos, sin, swap))
        n_read = self.PE.last()
        neg = mem["small"][:, 128:144]
        m_neg = self.ts(neg, self.vec("sink", 0, 16), -1.0, None, ALU.mult, None)
        buffers = Buffers(mem["o_p"])
        m_in = [self.DVE.last(), self.ACT.last(), m_neg]
        out_ready = []

        def head(kv, qb, j, shared):
            low = (kv % 2) * C_DIM
            rows = slice(low, low + C_DIM)
            if j == 0:
                shared.append(buffers.take())
                shared.append([])
            (buf, buf_free), done = shared
            tile = (kv // 2) * 4 + j
            bank, free = self.banks.take()
            self.mm(bank[:, :], q_t[rows, tile, qb * P:(qb + 1) * P], k_t[rows, kv // 2, :], True, False,
                    free, m_in)
            other = slice((1 - qb) * P, (2 - qb) * P)
            m = self.mm(bank[:, other], self.mat("ident"), near[:, qb, other], False, True, counted=True)
            yield
            h = 4 * kv + j
            yield from self.softmax(bank, m, C_DIM ** -0.5, (self.vec("sink", h), neg[:, h:h + 1]),
                                    buf[:, :, j * P:(j + 1) * P], buf_free, done)
            if j < 3:
                return
            yield
            out, free = self.banks.take()
            for k in range(TT):
                m = self.mm(out[rows, :], v[:, k, kv * C_DIM:(kv + 1) * C_DIM], buf[:, k, :], k == 0,
                            k == TT - 1, done, free, counted=k == TT - 1)
            buffers.give(buf, m)
            yield
            t, free = self.temps.take()
            m = self.act(t[rows, :], out[rows, :], ACT.Copy, m, free)
            self.banks.give(out, m)
            tiles = slice((kv // 2) * 4, (kv // 2) * 4 + 4)
            at = slice(qb * P, (qb + 1) * P)
            m = self.split(mem["n_hi"][rows, tiles, at], mem["n_lo"][rows, tiles, at],
                           t[rows, :].rearrange("p (j q) -> p j q", j=4), m, n_read)
            self.temps.give(t, m)
            out_ready.append(m)

        items = []
        for kv in range(C_KV):
            for qb in range(X_TILES):
                shared = []
                items += [head(kv, qb, j, shared) for j in range(4)]
        self.interleave(items)
        m = out_ready[-1]
        for c in range(4):
            self.project("odd_out", c, KD, 256, SEQ, lambda k: self.n_parts(k, SEQ), [m] * KD,
                         lambda t, bank, mk, c=c: self.add_gated(bank, mk, 2 * c + t, self.mod_scale(dest, 5), SEQ))
        self.barrier()

    def second_mixer(self, dest):
        mem, small = self.mem, self.mem["small"]
        wsc = small[:, 0:2 * KD].rearrange("p (k s) -> p k s", k=KD)
        m = self.tt(wsc, dest[:, KD:2 * KD, :], self.vec("mix_pre", 0, KD).unsqueeze(2).broadcast_to((P, KD, 2)),
                    ALU.mult, self.DVE.last())
        self.barrier()
        ready = self.norm(lambda k, s: wsc[:, k, s:s + 1], self.mod_scale(dest, 0), TOK, m)
        tables = self.SP.load(mem["stage"][:, 0:2 * SEQ], self.dram["mla_tables"], self.sems["stage"], 48)
        cos, sin = mem["stage"][:, 0:SEQ], mem["stage"][:, SEQ:2 * SEQ]
        src = lambda k: self.n_parts(k)
        src_x = lambda k: self.n_parts(k, SEQ)
        src_t = lambda k, tt: (mem["n_hi"][:, k, tt * P:(tt + 1) * P], mem["n_lo"][:, k, tt * P:(tt + 1) * P])
        cq, ckv, kr = (mem["m_cqh"], mem["m_cql"]), (mem["m_ckh"], mem["m_ckl"]), mem["m_kr"]
        z_t, xs_t, b_t, c_t = mem["m_z"], mem["m_xs"], mem["m_b"], mem["m_c"]

        def latent(banks, n, weight, width, parts):
            inv, m = self.norm_of([b[:, 0:n] for b, _ in banks], n, width, [mk for _, mk in banks])
            for k, (bank, _) in enumerate(banks):
                t, free = self.temps.take()
                e = self.ts(t[:, 0:n], bank[:, 0:n], self.vec(weight, k), None, ALU.mult, None, free)
                self.banks.give(bank, e)
                e = self.tt(t[:, 0:n], t[:, 0:n], inv[:, 0:n], ALU.mult, m, e)
                e = self.split(parts[0][:, k, 0:n], parts[1][:, k, 0:n], t[:, 0:n], e)
                self.temps.give(t, e)
            self.banks.give(inv, e)
            return e

        found = []
        for c in range(2):
            self.project("in_q", c, KD, (256, P)[c], SEQ, src_x, ready, lambda t, bank, m: found.append((bank, m)))
        m_cq = latent(found, SEQ, "q_norm", Q_RANK, cq)
        found = []
        self.project("in_kv", 0, KD, 256, TOK, src, ready, lambda t, bank, m: found.append((bank, m)))
        m_ckv = latent(found, TOK, "kv_norm", KV_RANK, ckv)

        def store_kr(t, bank, m):
            e = self.act(kr[:, :], bank[:, :], ACT.Copy, m)
            self.banks.give(bank, e)
            x, free = self.temps.take()
            e = self.act(x[0:QD, 0:SEQ], kr[0:QD, 0:SEQ], ACT.Copy, e, free)
            self.m_kr = self.rope_from(kr[0:QD, 0:SEQ], x, e, QD, cos, sin, self.mat("turn"), tables)
        self.project("in_kr", 0, KD, P, TOK, src, ready, store_kr)

        def store_z(c):
            def finish(t, bank, m):
                self.banks.give(bank, self.act(z_t[:, 2 * c + t, :], bank[:, 0:SEQ], ACT.Silu, m))
            return finish
        for c in range(4):
            self.project("in_z", c, KD, 256, SEQ, src_x, ready, store_z(c))

        def conv(base, n):
            def finish(t, bank, m):
                tile = base + t
                s = n // SEQ
                x, free = self.temps.take()
                xv = x[:, 0:n].rearrange("p (s t) -> p s t", s=s)
                bv = bank[:, 0:n].rearrange("p (s t) -> p s t", s=s)
                w = lambda tap: self.vec("sconv_w", tap * 12 + tile)
                m = self.act(x[:, 0:n], bank[:, 0:n], ACT.Identity, m, free, scale=w(2),
                             bias=self.vec("sconv_b", tile))
                for tap in (0, 1, 3, 4):
                    off = tap - 2
                    o = slice(max(0, -off), SEQ - max(0, off))
                    i = slice(max(0, off), SEQ - max(0, -off))
                    m = self.stt(xv[:, :, o], bv[:, :, i], w(tap), xv[:, :, o], ALU.mult, ALU.add, m)
                self.banks.give(bank, m)
                out = xs_t[:, tile, 0:n] if tile < 8 else b_t[:, tile - 8, 0:n] if tile < 10 else c_t[:, tile - 10, :]
                m = self.act(out, x[:, 0:n], ACT.Silu, m)
                self.temps.give(x, m)
            return finish
        for c in range(6):
            n = TOK if c < 5 else SEQ
            self.project("in_xbc", c, KD, 256, n, src if c < 5 else src_x, ready, conv(2 * c, n))
        dt = small[:, 64:64 + 32 * TT].rearrange("p (t g) -> p t g", t=TT)

        def store_dt(pair, bank, m):
            e = self.tt(dt[:, 2 * pair:2 * pair + 2, :], bank[:, 0:64].rearrange("p (t g) -> p t g", t=2),
                        self.vec("dt_b", 0, 32).unsqueeze(1).broadcast_to((P, 2, 32)), ALU.add, m)
            self.banks.give(bank, e)
        self.project_tokens("in_dt", 0, KD, 32, range(TT), src_t, ready, store_dt)
        self.barrier()
        self.ssd(dt)
        self.barrier()
        self.latent_attention(cq, ckv, kr, cos, sin)
        self.barrier()
        mix = mem["m_mix"]
        parts = lambda k: (mem["y_hi"][:, k, :], mem["y_lo"][:, k, :])
        for q in range(4):
            banks = None
            for i in range(2):
                banks = self.project("mix_out", 2 * q + i, KD, 256, SEQ, lambda k, i=i: parts(8 * i + k), None,
                                     lambda t, bank, m, q=q: self.banks.give(
                                         bank, self.act(mix[:, 2 * q + t, :], bank[:, 0:SEQ], ACT.Copy, m)),
                                     first=i == 0, last=i == 1, banks=banks)
        self.post_norm(mix, dest, 2, "mix_post")

    def post_norm(self, mix, dest, sec, weight, last=False):
        small = self.mem["small"]
        gw = small[:, 0:KD]
        m0 = self.tt(gw, dest[:, sec * KD:(sec + 1) * KD, 0], self.vec(weight, 0, KD), ALU.mult, self.DVE.last())
        inv, m = self.norm_of([mix[:, k, :] for k in range(KD)], SEQ, D, self.ACT.last(), self.DVE.last())
        h = self.mem["h"]
        for k in range(KD):
            e = self.stt(mix[:, k, :], mix[:, k, :], gw[:, k:k + 1], inv[:, 0:SEQ], ALU.mult, ALU.mult, m, m0)
            self.h_ready[k] = self.tt(h[:, k, 0:SEQ], h[:, k, 0:SEQ], mix[:, k, :], ALU.add, e)
            if not last:
                self.add_square(k, SEQ)
        self.banks.give(inv, e)

    def ssd(self, dt):
        mem, small = self.mem, self.mem["small"]
        xs_t, b_t, c_t, z_t = mem["m_xs"], mem["m_b"], mem["m_c"], mem["m_z"]
        xs, bt, y, state, xd = mem["s_xs"], mem["s_b"], mem["s_y"], mem["s_state"], mem["s_xd"]
        cb = mem["s_cb"]
        at = 64 + 32 * TT
        da = small[:, at:at + 32 * TT].rearrange("p (t g) -> p t g", t=TT)
        col = small[:, at + 128:at + 256].rearrange("p (t g) -> p t g", t=TT)
        e1 = small[:, at + 256:at + 288]
        tmp = small[:, at + 288:at + 320]
        neg_a = small[:, at + 320:at + 352]
        m = None
        for tt in range(TT):
            m = self.log_one_plus_exp(da[:, tt, :], e1, dt[:, tt, :], 1.0, [m], tmp)
        m = self.DVE.do(lambda e: e.tensor_copy(dt, da), m)
        m2 = self.act(neg_a, self.vec("a_log", 0, 32), ACT.Exp)
        m2 = self.ts(neg_a, neg_a, -1.0, None, ALU.mult, None, m2)
        m_da = self.tt(da, dt, neg_a.unsqueeze(1).broadcast_to((P, TT, 32)), ALU.mult, m, m2)
        bank, free = self.banks.take()
        for tt in range(TT):
            for d in range(2):
                g = slice(tt * 32 + d * 16, tt * 32 + d * 16 + 16)
                m = self.mm(bank[:, g], self.mat(("tri_f", "tri_b")[d]), da[:, tt, d * 16:d * 16 + 16], True, True,
                            m_da, free, counted=tt == TT - 1 and d == 1)
        m_col = self.ts(col, bank[:, 0:32 * TT].rearrange("p (t g) -> p t g", t=TT), -1.0, None, ALU.mult, None, m)
        self.banks.give(bank, m_col)
        for tt in range(TT):
            for half in range(2):
                bank, free = self.banks.take()
                for j in range(4):
                    m = self.turn(bank[:, j * P:(j + 1) * P], xs_t[:, 4 * half + j, tt * P:(tt + 1) * P], free,
                                  counted=j == 3)
                m = self.act(xs[:, tt, half * 512:(half + 1) * 512], bank[:, :], ACT.Copy, m)
                self.banks.give(bank, m)
            bank, free = self.banks.take()
            for j in range(2):
                m = self.turn(bank[:, j * P:(j + 1) * P], b_t[:, j, tt * P:(tt + 1) * P], free, counted=j == 1)
            m_xs = self.act(bt[:, tt, :], bank[:, 0:256], ACT.Copy, m)
            self.banks.give(bank, m_xs)
        bank, free = self.banks.take()
        for tt in range(X_TILES):
            for g in range(S_GROUPS):
                o = (tt * S_GROUPS + g) * P
                m = self.mm(bank[:, o:o + P], b_t[:, g, tt * P:(tt + 1) * P], c_t[:, g, tt * P:(tt + 1) * P], True,
                            True, free, counted=True)
        m_cb = self.act(cb[:, :], bank[:, :], ACT.Copy, m)
        self.banks.give(bank, m_cb)
        cbv = cb[:, :].rearrange("p (t g l) -> p t g l", t=X_TILES, g=S_GROUPS)
        w = small[:, at + 256:at + 384].rearrange("p (t g) -> p t g", t=TT)
        fade = mem["mods"][0][:, 0:64, :].rearrange("p a b -> p (a b)").rearrange("p (t g) -> p t g", t=TT)
        bank, free = self.banks.take()
        m = self.mm(bank[:, 0:32 * TT], self.mat("ones"), da.rearrange("p t g -> p (t g)"), True, True, free, m_da,
                    counted=True)
        total = bank[:, 0:32 * TT].rearrange("p (t g) -> p t g", t=TT)
        m_w = self.tt(w, total, col, ALU.add, m, m_col)
        m_fade = self.act(fade, total, ACT.Exp, m_w)
        self.banks.give(bank, m_fade)
        m_w = self.act(w, w, ACT.Exp)

        wide = lambda ap: ap.rearrange("p (h l) -> p h l", h=4)
        heads = lambda ap: ap.rearrange("p k (h e) -> p k h e", h=4)
        spread = lambda ap, k: ap.rearrange("p (k h) -> p k h", k=k).unsqueeze(3).broadcast_to((P, k, 4, S_DIM))
        head = lambda ap, h: ap[:, h // 4, (h % 4) * S_DIM:(h % 4 + 1) * S_DIM]
        order = ([2, 3, 0, 1], [3, 2, 1, 0])
        y_first = [[None] * 4 for tt in range(X_TILES)]
        m_state, m_xd, xd_used, state_used = [None, None], [None, None], [None, None], [None, None]

        def scale_inputs(d, step):
            tt = order[d][step]
            m_xd[d] = self.tt(heads(xd[d]), heads(xs[:, tt, :].rearrange("p (k n) -> p k n", k=4)),
                              spread(dt[:, tt, d * 16:(d + 1) * 16], 4), ALU.mult, m_xs, xd_used[d])
            yield

        def outputs(d, step, quad):
            tt = order[d][step]
            cols = slice(tt * P, (tt + 1) * P)
            tri, mask = self.mat(("tri_f", "tri_b")[d]), self.mat(("mask_f", "mask_b")[d])
            g = quad // 2
            a_bank, free = self.banks.take()
            for j in range(4):
                c = d * 16 + 4 * quad + j
                m = self.mm(a_bank[:, j * P:(j + 1) * P], da[:, tt, c:c + 1].broadcast_to((P, P)), tri, True, True,
                            free, m_da, counted=j == 3)
            yield
            ce, free = self.temps.take()
            m3 = self.act(ce[:, :], a_bank[:, :], ACT.Exp, m, free)
            dec, free = self.temps.take()
            m2 = self.tt(wide(dec[:, :]), wide(a_bank[:, :]), mask.unsqueeze(1).broadcast_to((P, 4, P)), ALU.add, m,
                         free, m3)
            self.banks.give(a_bank, m2)
            for j in range(4):
                o, c = slice(j * P, (j + 1) * P), d * 16 + 4 * quad + j
                m2 = self.act(dec[:, o], dec[:, o], ACT.Exp, m2, m_col, bias=col[:, tt, c:c + 1])
            yield
            m3 = self.tt(wide(ce[:, :]), wide(ce[:, :]), c_t[:, g, cols].unsqueeze(1).broadcast_to((P, 4, P)),
                         ALU.mult, m3)
            m2 = self.tt(wide(dec[:, :]), wide(dec[:, :]), cbv[:, tt, g, :].unsqueeze(1).broadcast_to((P, 4, P)),
                         ALU.mult, m2, m_cb)
            yield
            y_bank, free = self.banks.take()
            for j in range(4):
                h = 4 * quad + j
                out = y_bank[(h % 2) * 64:(h % 2) * 64 + 64, (j // 2) * P:(j // 2 + 1) * P]
                self.mm(out, head(xd[d], h), dec[:, j * P:(j + 1) * P], True, False, m_xd[d], m2, free)
                m = self.mm(out, head(state[d], h), ce[:, j * P:(j + 1) * P], False, True, m_state[d], m3,
                            counted=j == 3)
            self.temps.give(dec, m)
            self.temps.give(ce, m)
            xd_used[d] = state_used[d] = m
            yield
            yv = y[:, 2 * quad:2 * quad + 2, cols]
            bv = y_bank[:, 0:256].rearrange("p (j l) -> p j l", j=2)
            if y_first[tt][quad]:
                e = self.tt(yv, yv, bv, ALU.add, m, y_first[tt][quad])
            else:
                e = self.copy(yv, bv, m)
            y_first[tt][quad] = e
            self.banks.give(y_bank, e)

        def update(d, step):
            tt = order[d][step]
            yield
            yield
            yield
            yield
            m = self.tt(heads(xd[d]), heads(xd[d]), spread(w[:, tt, d * 16:(d + 1) * 16], 4), ALU.mult, m_w, m_xd[d],
                        xd_used[d])
            yield
            for g in range(S_GROUPS):
                bank, free = self.banks.take()
                m2 = self.mm(bank[:, :], bt[:, tt, g * P:(g + 1) * P], xd[d][:, 2 * g:2 * g + 2, :], True, True, m,
                             free, counted=True)
                part = state[d][:, 2 * g:2 * g + 2, :]
                new = bank[:, :].rearrange("p (k n) -> p k n", k=2)
                if step == 0:
                    e = self.copy(part, new, m2)
                else:
                    e = self.tt(heads(part), heads(part), spread(fade[:, tt, d * 16 + g * 8:d * 16 + (g + 1) * 8], 2),
                                ALU.mult, m_fade, state_used[d], m_state[d])
                    e = self.tt(part, part, new, ALU.add, e, m2)
                self.banks.give(bank, e)
            m_state[d], xd_used[d] = e, m2

        for step in range(TT):
            items = [scale_inputs(d, step) for d in range(2)]
            if step >= 2:
                items += [outputs(d, step, quad) for quad in range(4) for d in range(2)]
            if step < TT - 1:
                items += [update(d, step) for d in range(2)]
            self.interleave(items)
        for k in range(KD):
            m = self.stt(y[:, k, :], xs_t[:, k, 0:SEQ], self.vec("ssd_d", k), y[:, k, :], ALU.mult, ALU.add,
                         self.DVE.last())
            m = self.tt(y[:, k, :], y[:, k, :], z_t[:, k, :], ALU.mult, m)
        inv, m = self.norm_of([y[:, k, :] for k in range(KD)], SEQ, D_INNER, m)
        for k in range(KD):
            t, free = self.temps.take()
            e = self.stt(t[:, 0:SEQ], y[:, k, :], self.vec("ssd_norm", k), inv[:, 0:SEQ], ALU.mult, ALU.mult, m,
                         free, self.PE.last())
            e = self.split(mem["y_hi"][:, 8 + k, :], mem["y_lo"][:, 8 + k, :], t[:, 0:SEQ], e)
            self.temps.give(t, e)
        self.banks.give(inv, e)

    def latent_attention(self, cq, ckv, kr, cos, sin):
        mem = self.mem
        buffers = Buffers(mem["l_p"])
        turn = self.mat("turn")
        q_ready, k_ready, v_ready, ended = {}, {}, {}, {}
        opened = {}

        def group_free(g):
            return ended[g - 2] if g > 1 else None

        def queries(g, h):
            if h == 0:
                opened["q"] = self.next_chunk("q_up", g, 3 * HEADS_AT_ONCE * QD)
            chunk = opened["q"]
            hi, lo = (x.rearrange("p (k h c) -> p k h c", k=3, h=HEADS_AT_ONCE) for x in (chunk.hi, chunk.lo))
            bank, free = self.banks.take()
            for k in range(3):
                m = self.mm3(bank[0:QD, 0:SEQ], (hi[:, k, h, :], lo[:, k, h, :]), (cq[0][:, k, :], cq[1][:, k, :]),
                             k == 0, k == 2, chunk.ready, free, counted=k == 2)
            if h == HEADS_AT_ONCE - 1:
                self.done_with(chunk, m)
            yield
            x, free = self.temps.take()
            m = self.act(x[0:QD, 0:SEQ], bank[0:QD, 0:SEQ], ACT.Copy, m, free)
            self.banks.give(bank, m)
            yield
            q_ready[g, h] = self.rope_from(mem["l_q"][g % 2][0:QD, h, :], x, m, QD, cos, sin, turn, group_free(g))

        def keys(g, h):
            if h == 0:
                opened["kv"] = self.next_chunk("kv_up", g, 2 * HEADS_AT_ONCE * P)
            chunk = opened["kv"]
            hi, lo = (x.rearrange("p (k h c) -> p k h c", k=2, h=HEADS_AT_ONCE) for x in (chunk.hi, chunk.lo))
            bank, free = self.banks.take()
            for k in range(2):
                m = self.mm3(bank[:, :], (hi[:, k, h, :], lo[:, k, h, :]), (ckv[0][:, k, :], ckv[1][:, k, :]),
                             k == 0, k == 1, chunk.ready, free, counted=k == 1)
            yield
            k_g = mem["l_k"][g % 2]
            m = self.act(k_g[0:NOPE, h, :], bank[0:NOPE, :], ACT.Copy, m, group_free(g))
            self.banks.give(bank, m)
            m2 = self.copy(k_g[NOPE:QD, h, :], kr[NOPE:QD, :], group_free(g))
            k_ready[g, h] = [m, m2]

        def values(g, pair):
            chunk = opened["kv"]
            hi, lo = (x.rearrange("p (k h c) -> p k h c", k=2, h=HEADS_AT_ONCE) for x in (chunk.hi, chunk.lo))
            bank, free = self.banks.take()
            for j in range(2):
                tt = 2 * pair + j
                c = slice(tt * P, (tt + 1) * P)
                for k in range(2):
                    m = self.mm3(bank[:, j * 256:(j + 1) * 256].rearrange("p (h c) -> p h c", h=HEADS_AT_ONCE),
                                 (ckv[0][:, k, c], ckv[1][:, k, c]),
                                 (hi[:, k, :, NOPE:P], lo[:, k, :, NOPE:P]), k == 0, k == 1, free, counted=k == 1)
            if pair == 1:
                self.done_with(chunk, m)
            yield
            m = self.act(mem["l_v"][g % 2][:, 2 * pair:2 * pair + 2, :],
                         bank[:, :].rearrange("p (t c) -> p t c", t=2), ACT.Copy, m, group_free(g))
            self.banks.give(bank, m)
            v_ready.setdefault(g, []).append(m)

        def head(g, h, qb):
            bank, free = self.banks.take()
            m = self.mm(bank[:, :], mem["l_q"][g % 2][0:QD, h, qb * P:(qb + 1) * P], mem["l_k"][g % 2][0:QD, h, :],
                        True, True, free, q_ready[g, h], k_ready[g, h], counted=True)
            yield
            buf, buf_free = buffers.take()
            done = []
            yield from self.softmax(bank, m, QD ** -0.5, None, buf, buf_free, done)
            yield
            rows = slice((h % 2) * V_DIM, (h % 2) * V_DIM + V_DIM)
            out, free = self.banks.take()
            for k in range(TT):
                m = self.mm(out[rows, 0:P], mem["l_v"][g % 2][:, k, h * V_DIM:(h + 1) * V_DIM], buf[:, k, :],
                            k == 0, k == TT - 1, done, v_ready[g], free, counted=k == TT - 1)
            buffers.give(buf, m)
            ended[g] = m
            yield
            t, free = self.temps.take()
            m = self.act(t[rows, 0:P], out[rows, 0:P], ACT.Copy, m, free)
            self.banks.give(out, m)
            tile, at = (g * HEADS_AT_ONCE + h) // 2, slice(qb * P, (qb + 1) * P)
            m = self.split(mem["y_hi"][rows, tile, at], mem["y_lo"][rows, tile, at], t[rows, 0:P], m)
            self.temps.give(t, m)

        def projections(g):
            return ([queries(g, h) for h in range(HEADS_AT_ONCE)] + [keys(g, h) for h in range(HEADS_AT_ONCE)]
                    + [values(g, pair) for pair in range(2)])

        items = projections(0)
        for g in range(M_HEADS // HEADS_AT_ONCE):
            ahead = projections(g + 1) if g + 1 < M_HEADS // HEADS_AT_ONCE else []
            for h in range(HEADS_AT_ONCE):
                for qb in range(X_TILES):
                    items.append(head(g, h, qb))
                    if h:
                        n = 2 if (h, qb) != (3, 1) else len(ahead)
                        items += ahead[:n]
                        ahead = ahead[n:]
        self.interleave(items)

    def second_ffn(self, dest):
        mem, small = self.mem, self.mem["small"]
        wsc = small[:, 16:16 + KD]
        m = self.tt(wsc, dest[:, 4 * KD:5 * KD, 0], self.vec("ffn_pre", 0, KD), ALU.mult, self.DVE.last())
        ready = self.norm(lambda k, s: wsc[:, k:k + 1], self.mod_scale(dest, 3), SEQ, m)
        acc = mem["f_out"]

        def gate(j, n, g_bank, g_mark, u_bank, u_mark):
            t, free = self.temps.take()
            w = lambda tap: self.vec("fconv_w", tap * KF + j)
            m = self.act(t[:, 0:n], g_bank[:, 0:n], ACT.Identity, g_mark, free, scale=w(1),
                         bias=self.vec("fconv_b", j))
            m = self.stt(t[:, 1:n], g_bank[:, 0:n - 1], w(0), t[:, 1:n], ALU.mult, ALU.add, m)
            m = self.stt(t[:, 0:n - 1], g_bank[:, 1:n], w(2), t[:, 0:n - 1], ALU.mult, ALU.add, m)
            self.banks.give(g_bank, m)
            m = self.act(t[:, 0:n], t[:, 0:n], ACT.Gelu, m)
            m = self.tt(t[:, 0:n], t[:, 0:n], u_bank[:, 0:n], ALU.mult, m, u_mark)
            self.banks.give(u_bank, m)
            return t, m

        seen = set()

        def finish(k, bank, m, final):
            if k in seen:
                e = self.tt(acc[:, k, :], acc[:, k, :], bank[:, 0:SEQ], ALU.add, m, self.DVE.last())
            else:
                e = self.copy(acc[:, k, :], bank[:, 0:SEQ], m)
            seen.add(k)
            self.banks.give(bank, e)
        self.hidden(("up", 0), ("down", 0), SEQ, ready, gate, finish)
        self.post_norm(acc, dest, 5, "ffn_post", last=True)

    def compose(self):
        mem, dram, sems = self.mem, self.dram, self.sems
        mats = self.SP.load(mem["matrices"][:, :], dram["matrices"], sems["matrices"], 16)
        vecs = self.SP.load(mem["vectors"][:, :], dram["vectors"], sems["vectors"], 16)
        self.h_ready = [self.SP.load(mem["h"][:, :, :], dram["tokens"], sems["h"], 16)] * KD
        zero = self.DVE.do(lambda e: e.memset(mem["silu_c"][:, :, :, :], 0.0))
        zero = self.DVE.do(lambda e: e.memset(mem["zeros"][:, :], 0.0))
        zero = self.DVE.do(lambda e: e.memset(mem["eps"][:, :], EPS))
        self.DVE.wait(zero)
        cv = self.vec("c", 0, 4 * KD).rearrange("p (b s k) -> p b s k", b=2, s=2)
        for b in range(2):
            for s in range(2):
                m = self.act(mem["silu_c"][:, b, :, s], cv[:, b, s, :], ACT.Silu, vecs, zero)
        self.silu_c_ready = m
        for line in (self.PE, self.DVE, self.ACT):
            line.wait(mats, vecs)

        self.squares = []
        for k in range(KD):
            self.add_square(k, TOK)
        mods, mod_2 = mem["mods"], mem["mod_2"]
        half = 0.5
        self.modulation("ada", 0, 0, mods[0], ("ada_b", 0), [1, 0])
        self.finish_side()
        self.section(mods[0], 1, ALU.add, 1.0)
        self.modulation("ada", 0, 0, mods[0], ("ada_b", 0), [2, 3, 4, 5, 6, 7, 8])

        def scales(dest, ones_, halves):
            for s in ones_:
                self.section(dest, s, ALU.add, 1.0)
            for s in halves:
                self.section(dest, s, ALU.mult, half)

        self.ffn_with_gate("ffn_in", 0, "ffn_out", 0, mods[0], (0, 1, 2), TOK)
        self.finish_side()
        scales(mods[0], [4, 7], [8])
        self.even_mixer(mods[0])
        self.modulation("ada", 36, 0, mods[1], ("ada_b", N_MOD * KD), [1, 0, 2, 3, 4, 5, 6, 7, 8])
        self.ffn(("ffn_in", KF), ("ffn_out", 16), mods[0], (6, 7, 8), TOK)
        self.finish_side()
        scales(mods[1], [1, 4, 7], [2, 8])
        self.modulation("mod_2", 0, 1, mod_2, ("b_mod", 0), [0, 1, 2, 3, 4, 5])
        self.ffn(("ffn_in", 2 * KF), ("ffn_out", 32), mods[1], (0, 1, 2), TOK)
        self.finish_side()
        self.odd_mixer(mods[1])
        scales(mod_2, [1, 4], [])
        self.ffn(("ffn_in", 3 * KF), ("ffn_out", 48), mods[1], (6, 7, 8), SEQ)
        h = mem["h"]
        inv, m = self.h_rstd(SEQ)
        ctx_in = self.SP.load(h[:, :, SEQ:TOK], dram["ctx_2"], sems["h"], 32, self.barrier())
        for k in range(KD):
            e = self.stt(h[:, k, 0:SEQ], h[:, k, 0:SEQ], self.vec("final", k), inv[:, 0:SEQ], ALU.mult, ALU.mult, m)
            self.h_ready[k] = [e, ctx_in]
            self.add_square(k, TOK)
        self.banks.give(inv, e)
        self.barrier()
        self.second_mixer(mod_2)
        self.barrier()
        self.second_ffn(mod_2)
        out = self.SP.load(dram["out"], h[:, :, 0:SEQ], sems["out"], 16, self.h_ready)
        self.SP.wait(out)

    def ffn_with_gate(self, w_in, i, w_out, o, dest, secs, n):
        ready = self.norm(self.mod_scale(dest, secs[1]), self.mod_scale(dest, secs[0]), n)
        state = {"halved": False}

        def finish(k, bank, m, final):
            if not state["halved"]:
                state["halved"] = True
                self.section(dest, secs[2], ALU.mult, 0.5)
                self.DVE.wait(self.DVE.last())
            self.add_gated(bank, m, k, self.mod_scale(dest, secs[2]), n, final)
        self.hidden((w_in, i), (w_out, o), n, ready, self.silu_gate, finish)


def build(nc, dram):
    base = [16512]
    mem = {}

    def place(name, shape, dtype=F32, at=None):
        width = 4
        for s in shape[1:]:
            width *= s
        offset = base[0] if at is None else at
        t = nc.alloc_sbuf_tensor_at(name, shape, dtype, offset=offset)
        if at is None:
            base[0] += (width + 31) // 32 * 32
        return t

    mem["h"] = place("h", [P, KD, TOK])
    n_at = base[0]
    mem["n_hi"] = place("n_hi", [P, KD, TOK], F32R)
    mem["n_lo"] = place("n_lo", [P, KD, TOK], F32R)
    a_at = base[0]
    mem["a_hi"] = place("a_hi", [P, A_SLOTS, TOK], F32R)
    mem["a_lo"] = place("a_lo", [P, A_SLOTS, TOK], F32R)
    mem["raw"] = [place(f"raw{i}", [P, CHUNK]) for i in range(RAW_SLOTS)]
    mem["w_hi"] = [place(f"w_hi{i}", [P, CHUNK], F32R) for i in range(SPLIT_SLOTS)]
    mem["w_lo"] = [place(f"w_lo{i}", [P, CHUNK], F32R) for i in range(SPLIT_SLOTS)]
    mem["temps"] = [place(f"temp{i}", [P, TOK]) for i in range(TEMPS)]
    mem["matrices"] = place("matrices", [P, len(MATRICES) * P])
    mem["vectors"] = place("vectors", [P, N_VECTORS])
    stage_at = base[0]
    mem["stage"] = place("stage", [P, 8 * P])
    mem["mods"] = [place(f"mod{i}", [P, N_MOD * KD, 2]) for i in range(2)]
    mem["mod_2"] = place("mod_2", [P, N_MOD_2 * KD, 2])
    mem["silu_c"] = place("silu_c", [P, 2, KD, 32])
    mem["small"] = place("small", [P, 640])
    mem["columns"] = [place(f"column{i}", [P, 8]) for i in range(8)]
    mem["zeros"] = place("zeros", [P, 8])
    mem["eps"] = place("eps", [P, 8])
    assert base[0] <= 229368, base[0]
    K = 1024
    for i, x in enumerate(("e_q", "e_k", "e_v", "e_o", "e_u", "e_vb")):
        mem[x] = place(x, [P, 4, TOK], at=a_at + i * 8 * K)
    mem["e_c0"] = place("e_c0", [P, HEADS, HEAD], at=n_at)
    mem["e_c1"] = place("e_c1", [P, HEADS, HEAD], at=n_at + 2 * K)
    places = ([n_at + i * 2 * K for i in (2, 3, 8, 9, 10, 11)] + [a_at + 32 * K + i * 2 * K for i in range(4)]
              + [stage_at, stage_at + 2 * K])
    mem["e_tiles"] = [place(f"e_tile{i}", [P, TOK], at=x) for i, x in enumerate(places)]
    mem["o_q"] = place("o_q", [P, KD, SEQ], at=a_at)
    mem["o_k"] = place("o_k", [P, 2, TOK], at=a_at + 8 * K)
    mem["o_v"] = place("o_v", [P, TT, 256], at=a_at + 12 * K)
    mem["o_p"] = [place(f"o_p{i}", [P, TT, 512], at=a_at + (16 + 8 * i) * K) for i in range(3)]
    mem["m_cqh"] = place("m_cqh", [P, 3, SEQ], F32R, at=a_at)
    mem["m_cql"] = place("m_cql", [P, 3, SEQ], F32R, at=a_at + 3 * K)
    mem["m_ckh"] = place("m_ckh", [P, 2, TOK], F32R, at=a_at + 6 * K)
    mem["m_ckl"] = place("m_ckl", [P, 2, TOK], F32R, at=a_at + 10 * K)
    mem["m_kr"] = place("m_kr", [P, TOK], at=a_at + 14 * K)
    b = a_at + 16 * K
    mem["m_z"] = place("m_z", [P, KD, SEQ], at=b)
    mem["m_xs"] = place("m_xs", [P, KD, TOK], at=b + 8 * K)
    mem["m_b"] = place("m_b", [P, 2, TOK], at=b + 24 * K)
    mem["m_c"] = place("m_c", [P, 2, SEQ], at=b + 28 * K)
    mem["s_cb"] = place("s_cb", [P, TOK], at=b + 30 * K)
    mem["s_y"] = place("s_y", [P, KD, SEQ], at=n_at)
    mem["s_xs"] = place("s_xs", [P, TT, D_INNER], at=n_at + 8 * K)
    mem["s_b"] = place("s_b", [P, TT, 256], at=n_at + 24 * K)
    mem["s_state"] = [place("s_state", [P, 4, SEQ], at=n_at + 28 * K)[:, :, :], mem["m_xs"][:, 0:4, SEQ:TOK]]
    mem["s_xd"] = [mem["h"][:, 4 * d:4 * d + 4, SEQ:TOK] for d in range(2)]
    mem["y_hi"] = place("y_hi", [P, 16, SEQ], F32R, at=n_at)
    mem["y_lo"] = place("y_lo", [P, 16, SEQ], F32R, at=n_at + 16 * K)
    mem["l_q"] = [place(f"l_q{i}", [P, HEADS_AT_ONCE, SEQ], at=b + 16 * i * K) for i in range(2)]
    mem["l_k"] = [place(f"l_k{i}", [P, HEADS_AT_ONCE, TOK], at=b + (16 * i + 4) * K) for i in range(2)]
    mem["l_v"] = [place(f"l_v{i}", [P, TT, HEADS_AT_ONCE * V_DIM], at=b + (16 * i + 12) * K) for i in range(2)]
    mem["l_p"] = [mem["h"][:, TT * i:TT * (i + 1), SEQ + P * j:SEQ + P * (j + 1)] for i in range(2) for j in range(2)]
    mem["m_mix"] = place("m_mix", [P, KD, SEQ], at=a_at)
    mem["f_out"] = place("f_out", [P, KD, TOK], at=n_at)[:, :, SEQ:TOK]
    mem["banks"] = [nc.alloc_psum_tensor(f"bank{i}", [P, 512], F32) for i in range(8)]

    with ExitStack() as stack:
        def semaphore(name):
            return stack.enter_context(nc.semaphore(name))
        sems = {x: semaphore(f"s_{x}") for x in ("pe", "act", "dve", "sp", "pool", "matrices", "vectors", "h",
                                                 "stage", "out")}
        sems["raw"] = [semaphore(f"s_raw{i}") for i in range(RAW_SLOTS)]
        first = Program(nc, dram, mem, sems, None)
        first.compose()
        program = Program(nc, dram, mem, sems, first.asked)
        program.compose()
        assert program.asked == first.asked
        block = stack.enter_context(nc.Block())

        @block.sync
        def _(engine):
            program.SP.run(engine)

        @block.tensor
        def _(engine):
            program.PE.run(engine)

        @block.scalar
        def _(engine):
            program.ACT.run(engine)

        @block.vector
        def _(engine):
            program.DVE.run(engine)


def chunks(w, cols, width=None):
    kt, n = w.shape[0] // P, w.shape[1] // cols
    out = w.reshape(kt, P, n, cols).transpose(2, 1, 0, 3).reshape(n, P, kt * cols)
    if width and width > kt * cols:
        out = np.pad(out, ((0, 0), (0, 0), (0, width - kt * cols)))
    return out


def inward_chunks(w):
    g, u = w[:, :F].reshape(D, KF, P), w[:, F:].reshape(D, KF, P)
    return chunks(np.stack([g, u], axis=2).reshape(D, 2 * F), 2 * P)


def outward_chunks(w):
    out = []
    for half in range(2):
        rows = w[half * F // 2:(half + 1) * F // 2]
        for q in range(D // 256):
            part = rows[:, q * 256:(q + 1) * 256]
            out += [chunks(part[:6 * P], 256, 6 * 256), chunks(part[6 * P:], 256, 6 * 256)]
    return np.concatenate(out)


def features(v):
    return v.reshape(-1, P).T


def kernel(**inputs):
    import concourse.bacc as bacc
    from concourse.bass_utils import run_bass_kernel_spmd

    a = {k: np.asarray(v) for k, v in inputs.items()}
    square, odd, mla = shape_constants()
    on_all = lambda v: np.broadcast_to(v.reshape(1, -1), (P, v.size))
    vectors = {
        "ada_b": features(a["ada_b"]), "b_mod": features(a["b_mod_2"]), "conv": features(a["mlstm_conv"]),
        "mnorm": features(a["mlstm_norm"]), "sgu": features(a["sgu_norm"]), "final": features(a["final_norm"]),
        "mix_pre": features(a["mix_pre_norm_2"]), "mix_post": features(a["mix_post_norm_2"]),
        "q_norm": features(a["q_norm_2"]), "kv_norm": features(a["kv_norm_2"]),
        "sconv_w": features(a["ssd_conv_w_2"]), "sconv_b": features(a["ssd_conv_b_2"]),
        "ssd_norm": features(a["ssd_norm_2"]), "ssd_d": features(np.repeat(a["ssd_d_2"].reshape(-1), S_DIM)),
        "ffn_pre": features(a["ffn_pre_norm_2"]), "ffn_post": features(a["ffn_post_norm_2"]),
        "fconv_w": features(a["ffn_conv_w_2"]), "fconv_b": features(a["ffn_conv_b_2"]),
        "c": np.concatenate([features(a[x]) for x in ("c", "c_ctx", "c_2", "c_ctx_2")], axis=1),
        "gate_b": on_all(a["mlstm_gate_b"]), "sink": on_all(a["attn_sink"]), "dt_b": on_all(a["ssd_dt_bias_2"]),
        "a_log": on_all(a["ssd_a_log_2"]),
    }
    vectors = np.concatenate([vectors[x] for x in VECTORS], axis=1)
    stream = lambda x: x[0].T.reshape(KD, P, SEQ).transpose(1, 0, 2)
    heads = [4 * kv + j for g in range(2) for j in range(4) for kv in (2 * g, 2 * g + 1)]
    qkv, q_cols = a["odd_w_qkv"][0], C_HEADS * C_DIM
    odd_q = qkv[:, :q_cols].reshape(D, C_HEADS, C_DIM)[:, heads].reshape(D, q_cols)
    odd_out = a["odd_w_out"][0].reshape(C_HEADS, C_DIM, D)[heads].reshape(q_cols, D)
    w_in, even = a["w_in_2"][0], a["even_w_in"][0]
    z_at = Q_RANK + KV_RANK + ROPE
    x_at = z_at + D_INNER
    dt_at = x_at + D_INNER + 2 * S_GROUPS * S_STATE
    kr_at = Q_RANK + KV_RANK - NOPE
    gates_at = 4 * W_A
    arrays = {
        "matrices": square, "vectors": vectors, "odd_tables": odd, "mla_tables": mla,
        "tokens": np.concatenate([stream(a["x"]), stream(a["ctx"])], axis=2), "ctx_2": stream(a["ctx_2"]),
        "even_tables": np.concatenate([a["sgu_ws"][0].transpose(2, 0, 1).reshape(P, 4 * P),
                                       on_all(a["sgu_b"])], axis=1),
        "ada": np.concatenate([chunks(w, 256) for w in a["ada_w"]]),
        "mod_2": chunks(a["w_mod_2"][0], 256),
        "ffn_in": np.concatenate([inward_chunks(w) for w in a["ffn_w_in"].reshape(4, D, 2 * F)]),
        "ffn_out": np.concatenate([outward_chunks(w) for w in a["ffn_w_out"].reshape(4, F, D)]),
        "even_in": chunks(np.concatenate([even[:, :gates_at], even[:, gates_at + 16:]], axis=1), 256),
        "even_gates": chunks(even[:, gates_at:gates_at + 16], 16),
        "even_out": chunks(a["even_w_out"][0], 256),
        "odd_q": chunks(odd_q, 256), "odd_kv": chunks(qkv[:, q_cols:], 256), "odd_out": chunks(odd_out, 256),
        "in_q": np.concatenate([chunks(w_in[:, :256], 256), chunks(w_in[:, 256:Q_RANK], P, CHUNK)]),
        "in_kv": chunks(w_in[:, Q_RANK:Q_RANK + KV_RANK], 256),
        "in_kr": chunks(w_in[:, kr_at:kr_at + P], P),
        "in_z": chunks(w_in[:, z_at:x_at], 256), "in_xbc": chunks(w_in[:, x_at:dt_at], 256),
        "in_dt": chunks(w_in[:, dt_at:], 32),
        "q_up": chunks(a["w_q_up_2"][0], HEADS_AT_ONCE * QD),
        "kv_up": chunks(a["w_kv_up_2"][0], HEADS_AT_ONCE * P),
        "mix_out": np.stack([chunks(a["w_out_2"][0][i * D:(i + 1) * D], 256) for i in range(2)],
                            axis=1).reshape(8, P, CHUNK),
        "up": inward_chunks(a["w_up_2"][0]), "down": outward_chunks(a["w_down_2"][0]),
    }
    arrays = {k: np.ascontiguousarray(v) for k, v in arrays.items()}
    nc = bacc.Bacc("TRN2", target_bir_lowering=False, num_devices=1)
    dram = {k: nc.dram_tensor(k, v.shape, F32, kind="ExternalInput").ap() for k, v in arrays.items()}
    dram["out"] = nc.dram_tensor("out", (P, KD, SEQ), F32, kind="ExternalOutput").ap()
    build(nc, dram)
    got = run_bass_kernel_spmd(nc, [arrays], core_ids=[0]).results[0]["out"]
    return got.transpose(2, 1, 0).reshape(1, SEQ, D)
```

```python
from contextlib import ExitStack
from itertools import count

import numpy as np

import concourse.bass as bass
from concourse import mybir

ALU = mybir.AluOpType
ACT = mybir.ActivationFunctionType
AX = mybir.AxisListType
F32 = mybir.dt.float32
F32R = mybir.dt.float32r

P = 128
D = 1024
KD = D // P
SEQ = 256
TOK = 2 * SEQ
TT = TOK // P
X_TILES = SEQ // P
EPS = 1e-6
F = 2816
KF = F // P
N_MOD = 9
N_MOD_2 = 6

HEADS = 4
HEAD = 128
W_A = HEADS * HEAD
GROUPS_B = 4
W_B = GROUPS_B * P

C_HEADS = 16
C_KV = 4
C_DIM = 64
ROPE_BASE = 10000.0
GRID_W = 64

M_HEADS = 16
NOPE = 64
ROPE = 32
QD = NOPE + ROPE
V_DIM = 64
Q_RANK = 384
KV_RANK = 256
HEADS_AT_ONCE = 4

S_HEADS = 16
S_DIM = 64
S_GROUPS = 2
S_STATE = 128
S_PER = S_HEADS // S_GROUPS
D_INNER = S_HEADS * S_DIM
S_CONV = 5

MASKED = -1e30
CHUNK = 2048
RAW_SLOTS = 4
SPLIT_SLOTS = 3
A_SLOTS = 12
TEMPS = 6

VECTORS = {}
N_VECTORS = 0
for _name, _n in (("ada_b", 2 * N_MOD * KD), ("b_mod", N_MOD_2 * KD), ("conv", 3 * 8), ("mnorm", 4),
                  ("sgu", 4), ("final", KD), ("mix_pre", KD), ("mix_post", KD), ("q_norm", 3),
                  ("kv_norm", 2), ("sconv_w", S_CONV * 12), ("sconv_b", 12), ("ssd_norm", KD),
                  ("ssd_d", KD), ("ffn_pre", KD), ("ffn_post", KD), ("fconv_w", 3 * KF), ("fconv_b", KF),
                  ("c", 4 * KD), ("gate_b", 16), ("sink", 16), ("dt_b", 32), ("a_log", 32)):
    VECTORS[_name] = (N_VECTORS, _n)
    N_VECTORS += _n

MATRICES = ["ident", "tri_f", "tri_b", "mask_f", "mask_b", "ones", "swap", "turn", "sum_groups"]


def shape_constants():
    i = np.arange(P)
    le = (i[:, None] <= i[None, :]).astype(np.float32)
    swap = np.zeros((P, P), np.float32)
    swap[i[1::2], i[0::2]] = -1.0
    swap[i[0::2], i[1::2]] = 1.0
    turn = np.zeros((P, P), np.float32)
    for base in (NOPE, NOPE + 16):
        for j in range(8):
            turn[base + 8 + j, base + j] = -1.0
            turn[base + j, base + 8 + j] = 1.0
    sum_groups = np.zeros((P, P), np.float32)
    for g in range(4):
        sum_groups[32 * g, 0] = 1.0
    mats = {"ident": np.eye(P, dtype=np.float32), "tri_f": le, "tri_b": le.T,
            "mask_f": np.where(le > 0, 0, MASKED), "mask_b": np.where(le.T > 0, 0, MASKED),
            "ones": np.ones((P, P)), "swap": swap, "turn": turn, "sum_groups": sum_groups}
    square = np.concatenate([mats[m] for m in MATRICES], axis=1).astype(np.float32)

    row = (np.arange(SEQ) // GRID_W).astype(np.float32)
    col = (np.arange(SEQ) % GRID_W).astype(np.float32)
    n_freq = C_DIM // 4
    inv = np.float32(ROPE_BASE) ** (-np.arange(n_freq, dtype=np.float32) / np.float32(n_freq))
    ang = np.concatenate([row[:, None] * inv, col[:, None] * inv], axis=1)
    ang = np.repeat(ang, 2, axis=1).T
    ang = np.concatenate([ang, ang], axis=0)
    q = np.arange(SEQ)
    near = np.where(np.abs(q[:, None] - q[None, :]) <= P, 0.0, MASKED)
    odd = np.concatenate([np.cos(ang), np.sin(ang), near[:P], near[P:]], axis=1).astype(np.float32)

    axis = ROPE // 2
    inv = np.float32(ROPE_BASE) ** (-np.arange(0, axis, 2, dtype=np.float32) / np.float32(axis))
    ar, ac = row[:, None] * inv, col[:, None] * inv
    ang = np.concatenate([ar, ar, ac, ac], axis=1).T
    mla = np.zeros((P, 2 * SEQ), np.float32)
    mla[:NOPE, :SEQ] = 1.0
    mla[NOPE:QD, :SEQ] = np.cos(ang)
    mla[NOPE:QD, SEQ:] = np.sin(ang)
    return square, odd, mla




class Mark:

    def __init__(self, semaphore, value):
        self.semaphore, self.value = semaphore, value


class Line:

    def __init__(self, semaphore):
        self.semaphore, self.count, self.steps, self.passed = semaphore, 0, [], {}

    def wait(self, *marks):
        for m in marks:
            if m is None:
                continue
            if isinstance(m, (list, tuple)):
                self.wait(*m)
                continue
            if self.passed.get(id(m.semaphore), 0) < m.value:
                self.passed[id(m.semaphore)] = m.value
                self.steps.append((None, m.semaphore, m.value))

    def do(self, emit, *after, counted=True):
        self.wait(*after)
        if counted:
            self.count += 1
            self.steps.append((emit, self.semaphore, 1))
        else:
            self.steps.append((emit, None, 0))
        return Mark(self.semaphore, self.count)

    def load(self, out, in_, semaphore, value, *after):
        self.wait(*after)
        self.steps.append((lambda e: e.dma_start(out, in_), semaphore, 16))
        return Mark(semaphore, value)

    def last(self):
        return Mark(self.semaphore, self.count)

    def run(self, engine):
        for emit, semaphore, n in self.steps:
            if emit is None:
                engine.wait_ge(semaphore, n)
            elif semaphore is None:
                emit(engine)
            else:
                emit(engine).then_inc(semaphore, n)


class Buffers:

    def __init__(self, buffers):
        self.free = [(b, ()) for b in buffers]

    def take(self):
        return self.free.pop(0)

    def give(self, buffer, *last_use):
        self.free.append((buffer, last_use))


class Chunk:
    pass


class Program:

    def __init__(self, nc, dram, mem, sems, order):
        self.nc, self.dram, self.mem, self.sems = nc, dram, mem, sems
        self.PE, self.ACT, self.DVE, self.SP, self.POOL = (Line(sems[n]) for n in ("pe", "act", "dve", "sp", "pool"))
        self.banks = Buffers(mem["banks"])
        self.temps = Buffers(mem["temps"])
        self.columns = Buffers(mem["columns"])
        self.order = order
        self.asked = []
        self.loaded = self.prepared = self.finished = 0
        self.chunks = {}
        self.raw_free = [None] * RAW_SLOTS
        self.split_free = [None] * SPLIT_SLOTS
        self.n_split = 0
        self.split_done = 0
        self.a_free = [None] * A_SLOTS
        self.a_next = 0
        self.side = []

    def tt(self, out, a, b, op, *after, line=None):
        return (line or self.DVE).do(lambda e: e.tensor_tensor(out, a, b, op), *after)

    def copy(self, out, a, *after):
        return self.DVE.do(lambda e: e.tensor_copy(out, a), *after)

    def ts(self, out, a, s1, s2, op0, op1, *after):
        if op1 is None:
            return self.DVE.do(lambda e: e.tensor_scalar(out, a, s1, None, op0), *after)
        return self.DVE.do(lambda e: e.tensor_scalar(out, a, s1, s2, op0, op1), *after)

    def stt(self, out, a, s, b, op0, op1, *after):
        return self.DVE.do(lambda e: e.scalar_tensor_tensor(out=out, in0=a, scalar=s, in1=b, op0=op0, op1=op1),
                           *after)

    def act(self, out, in_, func, *after, **kw):
        return self.ACT.do(lambda e: e.activation(out, in_, func, **kw), *after)

    def mm(self, out, lhs, rhs, start, stop, *after, counted=False):
        return self.PE.do(lambda e: e.matmul(out, lhs, rhs, start=start, stop=stop, skip_group_check=True),
                          *after, counted=counted)

    def turn(self, out, in_, *after, counted=False):
        ident = self.mat("ident")[0:in_.shape[0], 0:in_.shape[0]]
        return self.PE.do(lambda e: e.transpose(out, in_, ident), *after, counted=counted)

    def mm3(self, out, w, x, start, stop, *after, counted=False):
        (wh, wl), (xh, xl) = w, x
        self.mm(out, wh, xh, start, False, *after)
        self.mm(out, wh, xl, False, False)
        return self.mm(out, wl, xh, False, stop, counted=counted)

    def split(self, hi, lo, value, *after):
        m = self.act(hi, value, ACT.Copy, *after)
        return self.tt(lo, value, hi.bitcast(F32), ALU.subtract, m, *after)

    def vec(self, name, i=0, n=1):
        at = VECTORS[name][0] + i
        return self.mem["vectors"][:, at:at + n]

    def mat(self, name):
        at = MATRICES.index(name) * P
        return self.mem["matrices"][:, at:at + P]

    def barrier(self):
        marks = [x.last() for x in (self.PE, self.ACT, self.DVE, self.POOL) if x.count]
        for x in (self.PE, self.ACT, self.DVE, self.POOL):
            x.wait(*marks)
        return marks

    def load_ahead(self):
        while self.loaded < len(self.order):
            i = self.loaded
            name, at, width, _ = self.order[i]
            slot = i % RAW_SLOTS
            if i >= RAW_SLOTS and self.raw_free[slot] is None:
                return
            free = self.raw_free[slot]
            self.raw_free[slot] = None
            raw = self.mem["raw"][slot][:, 0:width]
            c = Chunk()
            c.index, c.raw = i, raw
            c.landed = self.SP.load(raw, self.dram[name][at, :, 0:width], self.sems["raw"][slot],
                                    16 * (i // RAW_SLOTS + 1), free)
            self.chunks[i] = c
            self.loaded += 1

    def prepare(self, i):
        name, at, width, parts = self.order[i]
        c = self.chunks[i]
        slot = i % RAW_SLOTS
        if not parts:
            c.ready = c.landed
            return
        s = self.n_split % SPLIT_SLOTS
        self.n_split += 1
        c.split_slot = s
        c.hi, c.lo = self.mem["w_hi"][s][:, 0:width], self.mem["w_lo"][s][:, 0:width]
        self.finish_split()
        c.high = self.act(c.hi, c.raw, ACT.Copy, c.landed, self.split_free[s])
        self.half_split = c
        if not self.low_later:
            self.finish_split()

    split_ahead = 4
    low_on_pool = False
    half_split = None
    low_later = False

    def finish_split(self):
        c, self.half_split = self.half_split, None
        if c is not None:
            c.ready = self.tt(c.lo, c.raw, c.hi.bitcast(F32), ALU.subtract, c.high,
                              line=self.POOL if self.low_on_pool else self.DVE)
            self.raw_free[c.index % RAW_SLOTS] = c.ready

    def next_chunk(self, name, at, width, parts=True):
        i = len(self.asked)
        self.asked.append((name, at, width, parts))
        if self.order is None:
            c = Chunk()
            c.hi = c.lo = None
            c.raw = self.mem["raw"][0][:, 0:width]
            c.hi, c.lo = self.mem["w_hi"][0][:, 0:width], self.mem["w_lo"][0][:, 0:width]
            c.ready = None
            c.index = i
            return c
        assert self.order[i] == (name, at, width, parts)
        self.prepare_ahead(i)
        assert self.prepared > i, "chunk is not ready"
        if self.chunks[i] is self.half_split:
            self.finish_split()
        return self.chunks[i]

    def prepare_ahead(self, i):
        if self.order is None:
            return
        self.load_ahead()
        while self.prepared < len(self.order) and self.prepared <= i + self.split_ahead:
            if self.prepared >= self.loaded:
                break
            if self.order[self.prepared][3]:
                if self.n_split - self.split_done >= SPLIT_SLOTS:
                    break
            self.prepare(self.prepared)
            self.prepared += 1
            self.load_ahead()

    def done_with(self, c, mark):
        if self.order is None:
            return
        if self.order[c.index][3]:
            self.split_free[c.split_slot] = mark
            self.split_done += 1
        else:
            self.raw_free[c.index % RAW_SLOTS] = mark

    def modulation(self, name, k, pair, dest, bias, sections):
        per = D // 256
        self.side += [(name, k, sec, q, pair, dest, bias, sections) for sec in sections for q in range(per)]

    def side_step(self, n=1):
        for _ in range(n):
            if not self.side:
                return
            name, k, sec, q, pair, dest, bias, _ = self.side.pop(0)
            chunk = self.next_chunk(name, k + sec * 4 + q, CHUNK, parts=False)
            w = chunk.raw.rearrange("p (k n) -> p k n", k=KD)
            bank, free = self.banks.take()
            for kt in range(KD):
                g = kt % 4
                m = self.mm(bank[32 * g:32 * g + 32, 0:256], self.mem["silu_c"][:, pair, kt, :], w[:, kt, :],
                            kt < 4, kt >= 4, chunk.ready, free, self.silu_c_ready, counted=kt == KD - 1)
            self.done_with(chunk, m)
            row, row_free = self.temps.take()
            m = self.act(row[:, 0:256], bank[:, 0:256], ACT.Copy, m, row_free)
            self.banks.give(bank, m)
            self.end_side()
            self.side_open = (row, m, dest, bias, sec * KD + 2 * q)

    side_open = None

    def end_side(self):
        if self.side_open is None:
            return
        row, ready, dest, bias, at = self.side_open
        self.side_open = None
        bank, free = self.banks.take()
        for j in range(2):
            m = self.turn(bank[:, j * P:(j + 1) * P], row[:, j * P:(j + 1) * P], ready, free, counted=j == 1)
        self.temps.give(row, m)
        groups = bank[:, 0:2 * P].rearrange("p (j g s) -> p j s g", j=2, g=4)[:, :, 0:2, :]
        out = dest[:, at:at + 2, :]
        m = self.DVE.do(lambda e: e.tensor_reduce(out, groups, AX.X, ALU.add), m)
        self.banks.give(bank, m)
        self.tt(out, out,
                self.vec(bias[0], bias[1] + at, 2).unsqueeze(2).broadcast_to((P, 2, 2)), ALU.add, m)

    def section(self, dest, sec, op, value):
        view = dest[:, sec * KD:(sec + 1) * KD, :]
        return self.ts(view, view, value, None, op, None, self.DVE.last())

    def finish_side(self):
        while self.side:
            self.side_step()
        self.end_side()

    def add_squares(self, bank, i, count, squares, *after):
        rows = slice(32 * (i % 4), 32 * (i % 4) + 32)
        return self.mm(bank[rows, 0:squares.shape[1]], self.mat("ones")[:, 0:32], squares, i < 4,
                       i + 4 >= count, *after, counted=True)

    def rstd(self, bank, count, n, width, *after):
        return self.drain(self.rstd_steps(bank, count, n, width, *after))

    def rstd_steps(self, bank, count, n, width, *after):
        rows = 32 * min(count, 4)
        sums, free = self.temps.take()
        m = self.act(sums[0:rows, 0:n], bank[0:rows, 0:n], ACT.Copy, *after, free)
        self.banks.give(bank, m)
        yield
        total, free = self.banks.take()
        tiles = n // P
        for tt in range(tiles):
            m = self.mm(total[:, tt:tt + 1], sums[0:rows, tt * P:(tt + 1) * P], self.mat("sum_groups")[0:rows, 0:1],
                        True, True, m, free, counted=tt == tiles - 1)
        self.temps.give(sums, m)
        col, free = self.columns.take()
        inv = col[:, 0:tiles]
        m = self.act(inv, total[:, 0:tiles], ACT.Sqrt, m, free, scale=1.0 / width, bias=self.mem["eps"][:, 0:1])
        self.banks.give(total, m)
        m = self.DVE.do(lambda e: e.reciprocal(inv, inv), m)
        yield
        wide, free = self.banks.take()
        m = self.spread(wide, inv, tiles, m, free)
        self.columns.give(col, m)
        return wide, m

    def drain(self, steps):
        while True:
            try:
                next(steps)
            except StopIteration as end:
                return end.value

    def spread(self, bank, columns, tiles, *after):
        for tt in range(tiles):
            m = self.mm(bank[:, tt * P:(tt + 1) * P], columns[:, tt:tt + 1].broadcast_to((P, P)),
                        self.mat("ident"), True, True, *after, counted=tt == tiles - 1)
        return m

    def load_root_table(self):
        self.act(self.mem["eps"][:, 1:2], self.mem["eps"][:, 0:1], ACT.Sqrt, self.ACT.last())

    def add_square(self, k, n, source=None, *ready):
        if not self.squares:
            self.square_bank, self.square_free = self.banks.take()
            self.square_count = 0
            self.load_root_table()
        sq, free = self.temps.take()
        if source is None:
            source, ready = self.mem["h"][:, k, 0:n], self.h_ready[k]
        m = self.act(sq[:, 0:n], source, ACT.Square, free, ready)
        self.squares.append((sq, m, n))
        if self.square_count < len(self.squares) - 2:
            self.sum_square()

    def sum_square(self):
        sq, m, n = self.squares[self.square_count]
        m = self.add_squares(self.square_bank, self.square_count, KD, sq[:, 0:n], m, self.square_free)
        self.temps.give(sq, m)
        self.square_count += 1
        return m

    def h_rstd(self, n):
        while self.square_count < KD:
            m = self.sum_square()
        self.squares = []
        return self.rstd(self.square_bank, KD, n, D, m)

    squares = ()

    def norm(self, scale, shift, n, *after):
        ready = []
        self.drain(self.norm_steps(scale, shift, n, ready, False, *after))
        return ready

    def norm_steps(self, scale, shift, n, ready, pairs, *after):
        h, n_hi, n_lo = self.mem["h"], self.mem["n_hi"], self.mem["n_lo"]
        inv, m = self.h_rstd(n)
        scaled = []
        parts = [(s, slice(s * SEQ, (s + 1) * SEQ)) for s in range(n // SEQ)]

        def finish():
            k, t, marks = scaled.pop(0)
            for (s, at), a in zip(parts, marks):
                b = self.act(n_hi[:, k, at], t[:, at], ACT.Identity, a, bias=shift(k, s))
                c = self.stt(n_lo[:, k, at], t[:, at], shift(k, s), n_hi[:, k, at].bitcast(F32), ALU.add,
                             ALU.subtract, b)
            self.temps.give(t, c)
            ready.append(c)

        if pairs:
            yield
        for k in range(KD):
            t, free = self.temps.take()
            scaled.append((k, t, [self.stt(t[:, at], h[:, k, at], scale(k, s), inv[:, at], ALU.mult, ALU.mult, m,
                                           free, after) for s, at in parts]))
            if k and not (pairs and k % 2 == 0):
                finish()
            if pairs and k % 2:
                finish()
                yield
        if not pairs:
            finish()
        self.banks.give(inv, self.DVE.last())

    def mod_scale(self, dest, sec):
        return lambda k, s: dest[:, sec * KD + k, s:s + 1]

    def project(self, name, at, ktiles, cols, n, sources, ready, finish, first=True, last=True,
                banks=None):
        chunk = self.next_chunk(name, at, ktiles * cols)
        hi = chunk.hi.rearrange("p (k n) -> p k n", k=ktiles)
        lo = chunk.lo.rearrange("p (k n) -> p k n", k=ktiles)
        out = []
        for t in range(cols // P):
            bank, free = self.banks.take() if banks is None else banks[t]
            for k in range(ktiles):
                c = slice(t * P, (t + 1) * P)
                xh, xl = sources(k)
                m = self.mm3(bank[:, 0:n], (hi[:, k, c], lo[:, k, c]), (xh, xl), first and k == 0,
                             last and k == ktiles - 1, chunk.ready, free, ready[k] if ready else None,
                             counted=k == ktiles - 1)
            out.append((bank, m))
        self.done_with(chunk, m)
        if last:
            for t, (bank, m) in enumerate(out):
                finish(t, bank, m)
        return out

    def project_group(self, specs, n, sources, ready):
        self.drain(self.group_steps(specs, n, sources, ready))

    def group_steps(self, specs, n, sources, ready):
        opened = []
        for name, at, cols, finish in specs:
            chunk = self.next_chunk(name, at, KD * cols)
            parts = [x.rearrange("p (k n) -> p k n", k=KD) for x in (chunk.hi, chunk.lo)]
            opened.append((chunk, parts, [self.banks.take() for _ in range(cols // P)], finish))
        yield
        for k in range(KD):
            for chunk, (hi, lo), banks, finish in opened:
                for t, (bank, free) in enumerate(banks):
                    c = slice(t * P, (t + 1) * P)
                    m = self.mm3(bank[:, 0:n], (hi[:, k, c], lo[:, k, c]), sources(k), k == 0, k == KD - 1,
                                 chunk.ready, free, ready[k], counted=k == KD - 1)
                    if k == KD - 1:
                        banks[t] = (bank, m)
                if k == KD - 1:
                    self.done_with(chunk, m)
            if k % 2 and k < KD - 1:
                yield
        for _, _, banks, finish in opened:
            for t, (bank, m) in enumerate(banks):
                finish(t, bank, m)

    def project_tokens(self, name, at, ktiles, cols, tiles, sources, ready, finish):
        chunk = self.next_chunk(name, at, ktiles * cols)
        hi = chunk.hi.rearrange("p (k n) -> p k n", k=ktiles)
        lo = chunk.lo.rearrange("p (k n) -> p k n", k=ktiles)
        for pair in range(len(tiles) // 2):
            bank, free = self.banks.take()
            for j in range(2):
                tt = tiles[2 * pair + j]
                for k in range(ktiles):
                    xh, xl = sources(k, tt)
                    m = self.mm3(bank[:, j * cols:(j + 1) * cols], (xh, xl), (hi[:, k, :], lo[:, k, :]), k == 0,
                                 k == ktiles - 1, chunk.ready, free, ready[k] if ready else None,
                                 counted=k == ktiles - 1)
            if pair == len(tiles) // 2 - 1:
                self.done_with(chunk, m)
            finish(pair, bank, m)

    def n_parts(self, k, n=TOK):
        return self.mem["n_hi"][:, k, 0:n], self.mem["n_lo"][:, k, 0:n]

    def add_gated(self, bank, m, k, gate, n, final=True):
        h = self.mem["h"]
        for s in range(n // SEQ):
            at = slice(s * SEQ, (s + 1) * SEQ)
            e = self.stt(h[:, k, at], bank[:, at], gate(k, s), h[:, k, at], ALU.mult, ALU.add, m)
        self.banks.give(bank, e)
        self.h_ready[k] = e
        if final:
            self.add_square(k, n)

    def ffn(self, w_in, w_out, dest, secs, n):
        ready = self.norm(self.mod_scale(dest, secs[1]), self.mod_scale(dest, secs[0]), n)
        self.hidden(w_in, w_out, n, ready, self.silu_gate,
                    lambda k, bank, m, final: self.add_gated(bank, m, k, self.mod_scale(dest, secs[2]), n, final))

    def silu_gate(self, j, n, g_bank, g_mark, u_bank, u_mark):
        t, free = self.temps.take()
        m = self.act(t[:, 0:n], g_bank[:, 0:n], ACT.Silu, g_mark, free)
        self.banks.give(g_bank, m)
        m = self.tt(t[:, 0:n], t[:, 0:n], u_bank[:, 0:n], ALU.mult, m, u_mark)
        self.banks.give(u_bank, m)
        return t, m

    def first_inward(self, w_in, n, ready, found):
        return self.group_steps([(w_in[0], w_in[1] + j, 2 * P,
                                  lambda t, bank, m, j=j: found[j].__setitem__(t, (bank, m))) for j in range(2)],
                                n, lambda k: self.n_parts(k, n), ready)

    def hidden(self, w_in, w_out, n, ready, gate, finish, found=None):
        a_hi, a_lo = self.mem["a_hi"], self.mem["a_lo"]
        placed = {}

        def inward(j):
            found = {}
            self.side_step()
            self.project(w_in[0], w_in[1] + j, KD, 2 * P, n, lambda k: self.n_parts(k, n), ready,
                         lambda t, bank, m: found.__setitem__(t, (bank, m)))
            gated(j, found)
            self.finish_split()

        def gated(j, found):
            t, m = gate(j, n, *found[0], *found[1])
            slot = self.a_next % A_SLOTS
            self.a_next += 1
            e = self.split(a_hi[:, slot, 0:n], a_lo[:, slot, 0:n], t[:, 0:n], m, self.a_free[slot])
            self.temps.give(t, e)
            placed[j] = (slot, e)

        def outward(half):
            tiles = list(range(half * (KF // 2), (half + 1) * (KF // 2)))
            parts = [tiles[0:6], tiles[6:11]]
            for q in range(D // 256):
                banks = None
                for i, part in enumerate(parts):
                    self.side_step()
                    at = w_out[1] + (half * (D // 256) + q) * 2 + i
                    banks = self.project(w_out[0], at, len(part), 256, n,
                                         lambda k: (a_hi[:, placed[part[k]][0], 0:n], a_lo[:, placed[part[k]][0], 0:n]),
                                         [placed[j][1] for j in part],
                                         lambda t, bank, m: finish(2 * q + t, bank, m, half == 1),
                                         first=i == 0, last=i == 1,
                                         banks=None if banks is None else [(b, mk) for b, mk in banks])
            for j in tiles:
                self.a_free[placed[j][0]] = self.PE.last()

        half = KF // 2
        if found is None:
            self.side_step()
            found = [{}, {}]
            self.drain(self.first_inward(w_in, n, ready, found))
        for j in range(2):
            gated(j, found[j])
        self.low_later = n == SEQ
        for j in range(2, half + 1):
            inward(j)
        self.low_later = False
        outward(0)
        self.low_later = n == SEQ
        for j in range(half + 1, KF):
            inward(j)
        self.low_later = False
        outward(1)

    def even_mixer(self, dest):
        mem = self.mem
        n = TOK
        start = self.barrier()
        ready = self.norm(self.mod_scale(dest, 4), self.mod_scale(dest, 3), n)
        q_t, k_t, v, o_t, u_t, vb = (mem[x] for x in ("e_q", "e_k", "e_v", "e_o", "e_u", "e_vb"))
        tables = self.SP.load(mem["stage"][:, :], self.dram["even_tables"], self.sems["stage"], 16, start)
        ws_t = mem["stage"][:, 0:4 * P].rearrange("q (g p) -> q g p", g=GROUPS_B)
        sb = mem["stage"][:, 4 * P:8 * P].rearrange("c (g p) -> c g p", g=GROUPS_B)
        src = lambda k: self.n_parts(k)
        src_t = lambda k, tt: (mem["n_hi"][:, k, tt * P:(tt + 1) * P], mem["n_lo"][:, k, tt * P:(tt + 1) * P])

        def conv(base, out):
            def finish(t, bank, m):
                tile = base + t
                x, free = self.temps.take()
                xv = x[:, :].rearrange("p (s t) -> p s t", s=2)
                bv = bank[:, :].rearrange("p (s t) -> p s t", s=2)
                w = lambda tap: self.vec("conv", tap * 8 + tile)
                m = self.act(x[:, :], bank[:, :], ACT.Copy, m, free, scale=w(1))
                m = self.stt(xv[:, :, 1:SEQ], bv[:, :, 0:SEQ - 1], w(0), xv[:, :, 1:SEQ], ALU.mult, ALU.add, m)
                m = self.stt(xv[:, :, 0:SEQ - 1], bv[:, :, 1:SEQ], w(2), xv[:, :, 0:SEQ - 1], ALU.mult, ALU.add, m)
                self.banks.give(bank, m)
                m = self.act(out[:, tile % 4, :], x[:, :], ACT.Silu, m)
                self.temps.give(x, m)
            return finish

        small = mem["small"]
        gates = small[:, 0:TT * 16].rearrange("p (t g) -> p t g", t=TT)
        gate_marks, u_marks, vb_marks = [], [], []

        def store_u(t, bank, m):
            m = self.act(u_t[:, t, :], bank[:, :], ACT.Gelu_apprx_tanh, m)
            self.banks.give(bank, m)
            u_marks.append(m)

        def store_gates(t, bank, m):
            gate_marks.append(self.columns_of(bank, m, slice(0, 16), gates, "gate_b"))

        def store_vb(c):
            def finish(pair, bank, m):
                m = self.act(vb[:, 2 * pair:2 * pair + 2, c * 256:(c + 1) * 256],
                             bank[:, :].rearrange("p (t n) -> p t n", t=2), ACT.Gelu_apprx_tanh, m)
                self.banks.give(bank, m)
                vb_marks.append(m)
            return finish

        self.project_group([("even_in", 8 + c, 256, lambda t, bank, m, c=c: store_u(2 * c + t, bank, m))
                            for c in range(2)], n, src, ready)
        self.project("even_gates", 0, KD, P, n, src, ready, store_gates)
        for c in range(2):
            self.project_tokens("even_in", 10 + c, KD, 256, range(TT), src_t, ready, store_vb(c))
        for c in range(2):
            self.project("even_in", c, KD, 256, n, src, ready, conv(2 * c, q_t))

        gv = gates.rearrange("p t (d w h) -> p t d w h", d=2, w=2)
        lf, e1, c_col, tmp = (small[:, i:i + 8 * TT].rearrange("p (t d h) -> p t d h", t=TT, d=2)
                              for i in (96, 128, 160, 192))
        m = self.log_one_plus_exp(lf, e1, gv[:, :, :, 1, :], -1.0, gate_marks, tmp)
        m_lf = self.ts(lf, lf, -1.0, None, ALU.mult, None, m)

        ss = small[:, 64:64 + TT]
        for tt in range(TT):
            sq, free = self.temps.take()
            m = self.act(sq[:, :], vb[:, tt, :], ACT.Square, free, vb_marks, accum_out=ss[:, tt:tt + 1])
            self.temps.give(sq, m)
        m = self.act(ss, ss, ACT.Sqrt, m, scale=1.0 / W_B, bias=mem["eps"][:, 0:1])
        m = self.DVE.do(lambda e: e.reciprocal(ss, ss), m)
        for tt in range(TT):
            m_vb = self.ts(vb[:, tt, :], vb[:, tt, :], ss[:, tt:tt + 1], None, ALU.mult, None, m)
        for c in range(2, 4):
            self.project("even_in", c, KD, 256, n, src, ready, conv(2 * c, k_t))
        bank, free = self.banks.take()
        bv = bank[:, 0:8 * TT].rearrange("p (t d h) -> p t d h", t=TT, d=2)
        for tt in range(TT):
            for d in range(2):
                tri = self.mat(("tri_f", "tri_b")[d])
                m = self.mm(bv[:, tt, d, :], tri, lf[:, tt, d, :], True, True, m_lf, free,
                            counted=tt == TT - 1 and d == 1)
        m_cols = self.tt(c_col, gv[:, :, :, 0, :], bv, ALU.subtract, m)
        self.banks.give(bank, m_cols)
        b_marks = []
        for g in range(GROUPS_B):
            bank, free = self.banks.take()
            for tt in range(TT):
                m = self.mm(bank[:, tt * P:(tt + 1) * P], vb[:, tt, g * P:(g + 1) * P], ws_t[:, g, :], True, True,
                            m_vb, tables, free, counted=tt == TT - 1)
            t, free = self.temps.take()
            m = self.stt(t[:, :].rearrange("p (t c) -> p t c", t=TT), bank[:, :].rearrange("p (t c) -> p t c", t=TT),
                         self.vec("sgu", g), sb[:, g, :].unsqueeze(1).broadcast_to((P, TT, P)), ALU.mult, ALU.add,
                         m, free)
            self.banks.give(bank, m)
            m = self.tt(u_t[:, g, :], t[:, :], u_t[:, g, :], ALU.mult, m, u_marks)
            self.temps.give(t, m)
            b_marks.append(m)
        for c in range(2):
            def store_v(pair, bank, m, c=c):
                m = self.act(v[:, 2 * pair:2 * pair + 2, c * 256:(c + 1) * 256],
                             bank[:, :].rearrange("p (t n) -> p t n", t=2), ACT.Copy, m)
                self.banks.give(bank, m)
            self.project_tokens("even_in", 4 + c, KD, 256, range(TT), src_t, ready, store_v)
        for c in range(2):
            def store_o(t, bank, m, c=c):
                self.banks.give(bank, self.act(o_t[:, 2 * c + t, :], bank[:, :], ACT.Sigmoid, m))
            self.project("even_in", 6 + c, KD, 256, n, src, ready, store_o)
        n_used = self.PE.last()
        for g in range(GROUPS_B):
            self.split(mem["n_hi"][:, 4 + g, :], mem["n_lo"][:, 4 + g, :], u_t[:, g, :], b_marks[g], n_used)
        self.barrier()
        self.low_on_pool = True
        self.mlstm(q_t, k_t, v, lf, c_col, m_cols)
        self.low_on_pool = False

        ready = self.head_norms(mem["e_vb"], o_t)
        for c in range(4):
            self.project("even_out", c, KD, 256, n, src, ready,
                         lambda t, bank, mk, c=c: self.add_gated(bank, mk, 2 * c + t, self.mod_scale(dest, 5), n))
        self.barrier()

    def head_norms(self, h_sum, o_t):
        mem = self.mem
        m_in = self.DVE.last()
        sum_bank, free = self.banks.take()
        for h in range(HEADS):
            sq, sq_free = self.temps.take()
            m = self.act(sq[:, :], h_sum[:, h, :], ACT.Square, sq_free, m_in)
            m_sum = self.mm(sum_bank[32 * h:32 * h + 32, :], self.mat("ones")[:, 0:32], sq[:, :], True, True, m, free,
                            counted=True)
            self.temps.give(sq, m_sum)
        sums, free = self.temps.take()
        m = self.act(sums[:, :], sum_bank[:, :], ACT.Copy, m_sum, free)
        self.banks.give(sum_bank, m)
        cols, free = self.banks.take()
        pick = self.mat("ident").rearrange("p (h x) -> p h x", h=HEADS)[:, :, 0]
        for tt in range(TT):
            m_col = self.mm(cols[:, 4 * tt:4 * tt + 4], sums[:, tt * P:(tt + 1) * P], pick, True, True, m, free,
                            counted=tt == TT - 1)
        self.temps.give(sums, m_col)
        inv = mem["small"][:, 96:96 + TT * HEADS].rearrange("p (t h) -> p t h", t=TT)
        m = self.act(inv, cols[:, 0:TT * HEADS].rearrange("p (t h) -> p t h", t=TT), ACT.Sqrt, m_col,
                     scale=1.0 / HEAD, bias=mem["eps"][:, 0:1])
        self.banks.give(cols, m)
        m_inv = self.DVE.do(lambda e: e.reciprocal(inv, inv), m)
        ready = []
        for h in range(HEADS):
            bank, free = self.banks.take()
            m = self.spread(bank, inv[:, :, h], TT, m_inv, free)
            t, free = self.temps.take()
            m = self.tt(t[:, :], bank[:, :], h_sum[:, h, :], ALU.mult, m, free)
            self.banks.give(bank, m)
            m = self.stt(t[:, :], t[:, :], self.vec("mnorm", h), o_t[:, h, :], ALU.mult, ALU.mult, m)
            m = self.split(mem["n_hi"][:, h, :], mem["n_lo"][:, h, :], t[:, :], m, m_in)
            self.temps.give(t, m)
            ready.append(m)
        return ready + [m] * (KD - HEADS)

    def columns_of(self, bank, m, rows, out, bias):
        n = rows.stop - rows.start
        x, free = self.temps.take()
        m = self.act(x[rows, :], bank[rows, :], ACT.Copy, m, free)
        self.banks.give(bank, m)
        turned, free = self.banks.take()
        for tt in range(TT):
            m2 = self.turn(turned[:, tt * n:(tt + 1) * n], x[rows, tt * P:(tt + 1) * P], m, free,
                           counted=tt == TT - 1)
        self.temps.give(x, m2)
        m = self.tt(out, turned[:, 0:TT * n].rearrange("p (t g) -> p t g", t=TT),
                    self.vec(bias, 0, n).unsqueeze(1).broadcast_to((P, TT, n)), ALU.add, m2)
        self.banks.give(turned, m)
        return m

    def log_one_plus_exp(self, out, e1, x, sign, after, tmp):
        return self.drain(self.log_steps(out, e1, x, sign, after, tmp))

    def log_steps(self, out, e1, x, sign, after, tmp):
        m = self.ts(tmp, x, -1.0, None, ALU.mult, None, *after, self.DVE.last())
        m = self.tt(e1, tmp, x, ALU.min, m)
        m = self.act(e1, e1, ACT.Exp, m)
        yield
        m = self.ts(tmp, e1, 1.0, None, ALU.add, None, m)
        ln = self.act(out, tmp, ACT.Ln, m)
        yield
        m = self.stt(e1, tmp, 1.0, e1, ALU.subtract, ALU.subtract, m)
        r = self.DVE.do(lambda e: e.reciprocal(tmp, tmp), m, ln)
        m = self.tt(e1, e1, tmp, ALU.mult, r)
        m = self.tt(out, out, e1, ALU.subtract, m, ln)
        m = self.ts(tmp, x, sign, 0.0, ALU.mult, ALU.max, m)
        return self.tt(out, out, tmp, ALU.add, m)

    def mlstm(self, q_t, k_t, v, lf, c_col, m_cols):
        mem, small = self.mem, self.mem["small"]
        h_sum = mem["e_vb"]
        scale = HEAD ** -0.5
        order = ([2, 3, 0, 1], [3, 2, 1, 0])
        state = [mem["e_c0"], mem["e_c1"]]
        n_state = [small[:, 200 + 4 * d:204 + 4 * d] for d in range(2)]
        m_state = [[small[:, 208 + 4 * (2 * d + i):212 + 4 * (2 * d + i)] for i in range(2)] for d in range(2)]
        wide = lambda ap: ap.rearrange("p (h t) -> p h t", h=HEADS)
        ones, ident = self.mat("ones"), self.mat("ident")
        tiles = Buffers(mem["e_tiles"])
        self.end_side()
        lent = [self.temps.take() for _ in range(TEMPS - 2)]
        for tile, last_use in lent:
            tiles.give(tile, *last_use)
        m_ready = [self.DVE.do(lambda e, d=d: e.memset(m_state[d][0], 0.0), m_cols) for d in range(2)]
        s_ready = [None, None]
        h_first = [None] * TT
        m_prev_used = [[None] * (TT + 2) for d in range(2)]
        w_used = [[None] * (TT + 2) for d in range(2)]

        def each_head(emit):
            for h in range(HEADS):
                m = emit(h, slice(h * P, (h + 1) * P), h == HEADS - 1)
            return m

        def item(d, step):
            tt = order[d][step]
            cols = slice(tt * P, (tt + 1) * P)
            tri, mask = self.mat(("tri_f", "tri_b")[d]), self.mat(("mask_f", "mask_b")[d])
            end = P - 1 if d == 0 else 0
            m_prev, m_next = m_state[d][step % 2], m_state[d][(step + 1) % 2]
            more = step < TT - 1
            b_bank, free = self.banks.take()
            each_head(lambda h, at, last: self.mm(b_bank[:, at], lf[:, tt, d, h:h + 1].broadcast_to((P, P)), tri,
                                                  True, True, free, m_cols))
            c_bank, free = self.banks.take()
            mc = each_head(lambda h, at, last: self.mm(c_bank[:, at], c_col[:, tt, d, h:h + 1].broadcast_to((P, P)),
                                                       ident, True, True, free, m_cols, counted=last))
            yield
            big_m, free = tiles.take()
            for h in range(HEADS):
                o, i = big_m[:, h * P:(h + 1) * P], c_bank[:, h * P:(h + 1) * P]
                if d == 1:
                    o, i = o[:, ::-1], i[:, ::-1]
                m_max = self.running_max(o, i, m_prev[:, h:h + 1], mc, free, m_ready[d])
            self.banks.give(c_bank, m_max)
            prev_ready = m_ready[d]
            m_end = wide(big_m[:, :])[:, :, end]
            m_ready[d] = self.tt(m_next, wide(b_bank[:, :])[:, :, end], m_end, ALU.add, m_max,
                                 m_prev_used[d][step])
            floor, free = tiles.take()
            for h in range(HEADS):
                rows = slice(32 * h, 32 * h + 32)
                m_floor = self.tt(floor[rows, 0:P], b_bank[rows, h * P:(h + 1) * P], big_m[rows, h * P:(h + 1) * P],
                                  ALU.add, m_max, free)
            self.banks.give(b_bank, m_floor, m_ready[d])
            dec, free = tiles.take()
            m_dec = self.tt(wide(dec[:, :]), mask.unsqueeze(1).broadcast_to((P, HEADS, P)), wide(big_m[:, :]),
                            ALU.subtract, m_max, free)
            w = small[:, 224 + 4 * (2 * d + step % 2):228 + 4 * (2 * d + step % 2)]
            m_w = self.tt(w, c_col[:, tt, d, :], m_end, ALU.subtract, m_max, w_used[d][step])
            s_bank, free = self.banks.take()
            m_s = each_head(lambda h, at, last: self.mm(s_bank[:, at], k_t[:, h, cols], q_t[:, h, cols], True, True,
                                                        free, counted=last))
            yield
            m_dec = each_head(lambda h, at, last: self.act(dec[:, at], dec[:, at], ACT.Exp, m_dec,
                                                           bias=c_col[:, tt, d, h:h + 1]))
            inter, free2 = tiles.take()
            m_int = each_head(lambda h, at, last: self.act(inter[:, at], big_m[:, at], ACT.Exp, m_max, free2,
                                                           prev_ready, scale=-1.0, bias=m_prev[:, h:h + 1]))
            m_prev_used[d][step + 1] = m_int
            m_w = self.act(w, w, ACT.Exp, m_w)
            m_floor = self.act(floor[:, 0:P], floor[:, 0:P], ACT.Exp, m_floor, scale=-1.0)
            tiles.give(big_m, m_int, m_w)
            if more:
                kt_bank, free3 = self.banks.take()
                m_k = each_head(lambda h, at, last: self.turn(kt_bank[:, at], k_t[:, h, cols], free3, counted=last))
            yield
            s, free4 = tiles.take()
            m_sc = self.stt(s[:, :], s_bank[:, :], scale, dec[:, :], ALU.mult, ALU.mult, m_s, m_dec, free4)
            self.banks.give(s_bank, m_sc)
            tiles.give(dec, m_sc)
            if step:
                qi, free5 = tiles.take()
                m_qi = self.tt(wide(qi[:, :]), q_t[:, :, cols], wide(inter[:, :]), ALU.mult, m_int, free5)
            if more:
                kw, free6 = tiles.take()
                m_w = self.ts(w, w, scale, None, ALU.mult, None, m_w)
                m_kw = self.tt(wide(kw[:, :]), wide(kt_bank[:, :]), w.unsqueeze(2).broadcast_to((P, HEADS, P)),
                               ALU.mult, m_k, m_w, free6)
                w_used[d][step + 2] = m_kw
                self.banks.give(kt_bank, m_kw)
            yield
            num, free7 = self.banks.take()
            den, free8 = self.banks.take()
            for h in range(HEADS):
                at = slice(h * P, (h + 1) * P)
                self.mm(num[:, at], v[:, tt, at], s[:, at], True, step == 0, free7, m_sc)
                if step:
                    self.mm(num[:, at], state[d][:, h, :], qi[:, at], False, True, m_qi, s_ready[d])
            for h in range(HEADS):
                m_d = self.mm(den[32 * h:32 * h + 32, 0:P], ones[:, 0:32], s[:, h * P:(h + 1) * P], True, step == 0,
                              free8, counted=h == HEADS - 1)
            if step:
                for h in range(HEADS):
                    m_d = self.mm(den[32 * h:32 * h + 32, 0:P], n_state[d][:, h:h + 1].broadcast_to((P, 32)),
                                  qi[:, h * P:(h + 1) * P], False, True, counted=h == HEADS - 1)
            tiles.give(s, m_d)
            if step:
                tiles.give(qi, m_d)
            if more:
                c_loc, free9 = self.banks.take()
                n_loc = den[:, P:P + HEADS]
                for h in range(HEADS):
                    at = slice(h * P, (h + 1) * P)
                    self.mm(c_loc[:, at], kw[:, at], v[:, tt, at], True, True, m_kw, free9)
                    m_c = self.mm(n_loc[:, h:h + 1], kw[:, at], ones[:, 0:1], True, True,
                                  counted=h == HEADS - 1)
                tiles.give(kw, m_c)
                fade = wide(inter[:, :])[:, :, end]
                st = state[d]
                if step == 0:
                    m = self.copy(st[:, :, :], wide(c_loc[:, :]), m_c)
                    m = self.copy(n_state[d], n_loc[:, 0:HEADS], m_c)
                else:
                    m = self.tt(st[:, :, :], st[:, :, :], fade.unsqueeze(2).broadcast_to((P, HEADS, P)), ALU.mult,
                                m_d, m_int)
                    m2 = self.tt(n_state[d], n_state[d], fade, ALU.mult, m_d)
                    m = self.tt(st[:, :, :], st[:, :, :], wide(c_loc[:, :]), ALU.add, m, m_c)
                    m = self.tt(n_state[d], n_state[d], n_loc[:, 0:HEADS], ALU.add, m2)
                s_ready[d] = m
                self.banks.give(c_loc, m)
                tiles.give(inter, m)
            else:
                tiles.give(inter, m_int, self.DVE.last())
            rden, free11 = tiles.take()
            m = self.act(rden[:, 0:P], den[:, 0:P], ACT.Abs, [m_c, s_ready[d]] if more else m_d, free11)
            self.banks.give(den, m)
            m = self.tt(rden[:, 0:P], rden[:, 0:P], floor[:, 0:P], ALU.max, m, m_floor)
            tiles.give(floor, m)
            m = self.DVE.do(lambda e: e.reciprocal(rden[:, 0:P], rden[:, 0:P]), m)
            yield
            r_bank, free12 = self.banks.take()
            m = each_head(lambda h, at, last: self.mm(r_bank[:, at], ident[:, 32 * h:32 * h + 1].broadcast_to((P, P)),
                                                      rden[:, 0:P], True, True, m, free12, counted=last))
            tiles.give(rden, m)
            r, free13 = tiles.take()
            m = self.act(r[:, :], r_bank[:, :], ACT.Copy, m, free13)
            self.banks.give(r_bank, m)
            yield
            if h_first[tt]:
                m = self.tt(wide(r[:, :]), wide(r[:, :]), wide(num[:, :]), ALU.mult, m)
                m = self.tt(h_sum[:, :, cols], h_sum[:, :, cols], wide(r[:, :]), ALU.add, m, h_first[tt])
            else:
                m = self.tt(h_sum[:, :, cols], wide(r[:, :]), wide(num[:, :]), ALU.mult, m)
            h_first[tt] = m
            self.banks.give(num, m)
            tiles.give(r, m)

        self.interleave([item(d, step) for step in range(TT) for d in range(2)], 2, 2)
        done = (self.PE.last(), self.ACT.last(), self.DVE.last())
        for tile, _ in lent:
            self.temps.give(tile, *done)

    def running_max(self, out, in_, start, *after):
        zeros = self.mem["zeros"][:, 0:1].broadcast_to((P, P))
        return self.DVE.do(lambda e: e.tensor_tensor_scan(out, zeros, in_, start, ALU.add, ALU.max), *after)

    def interleave(self, items, every=1, side=0):
        items, active = iter(items), []
        for n in count():
            if n % every == 0:
                new = next(items, None)
                if new is not None:
                    active.insert(0, new)
                elif not active:
                    return
            self.side_step(side)
            active = [x for x in active if next(x, "ended") != "ended"]

    def rope(self, out, bank, m, rows, cos, sin, turn, *after):
        x, free = self.temps.take()
        m = self.act(x[0:rows, 0:SEQ], bank[0:rows, 0:SEQ], ACT.Copy, m, free)
        self.banks.give(bank, m)
        self.rope_from(out, x, m, rows, cos, sin, turn, *after)

    def rope_from(self, out, x, m, rows, cos, sin, turn, *after):
        bank, free = self.banks.take()
        m = self.mm(bank[0:rows, 0:SEQ], turn[0:rows, 0:rows], x[0:rows, 0:SEQ], True, True, m, free, counted=True)
        m = self.tt(x[0:rows, SEQ:TOK], bank[0:rows, 0:SEQ], sin[0:rows, :], ALU.mult, m, *after)
        self.banks.give(bank, m)
        m = self.tt(x[0:rows, 0:SEQ], x[0:rows, 0:SEQ], cos[0:rows, :], ALU.mult, m)
        m = self.tt(out, x[0:rows, 0:SEQ], x[0:rows, SEQ:TOK], ALU.add, m)
        self.temps.give(x, m)
        return m

    def softmax(self, bank, m, scale, sink, out, out_free, done):
        col, free = self.columns.take()
        top, total = col[:, 0:1], col[:, 1:2]
        m = self.DVE.do(lambda e: e.tensor_reduce(top, bank[:, :], AX.X, ALU.max), m, free)
        if sink is None:
            m = self.ts(top, top, -scale, None, ALU.mult, None, m)
        else:
            m = self.ts(top, top, -scale, sink[1], ALU.mult, ALU.min, m)
        p, free = self.temps.take()
        m = self.act(p[:, :], bank[:, :], ACT.Exp, m, free, scale=scale, bias=top, accum_out=total)
        self.banks.give(bank, m)
        if sink is not None:
            m2 = self.act(col[:, 2:3], sink[0], ACT.Exp, bias=top)
        yield
        if sink is not None:
            m = self.tt(total, total, col[:, 2:3], ALU.add, m, m2)
        m = self.DVE.do(lambda e: e.reciprocal(total, total), m)
        m = self.ts(p[:, :], p[:, :], total, None, ALU.mult, None, m)
        self.columns.give(col, m)
        yield
        t_bank, free = self.banks.take()
        for k in range(TT):
            m2 = self.turn(t_bank[:, k * P:(k + 1) * P], p[:, k * P:(k + 1) * P], m, free, counted=k == TT - 1)
        self.temps.give(p, m2)
        m = self.act(out, t_bank[:, :].rearrange("p (k q) -> p k q", k=TT), ACT.Copy, m2, out_free)
        self.banks.give(t_bank, m)
        done.append(m)

    def odd_mixer(self, dest):
        mem = self.mem
        start = self.barrier()
        ready = self.norm(self.mod_scale(dest, 4), self.mod_scale(dest, 3), TOK)
        q_t, k_t, v = mem["o_q"], mem["o_k"], mem["o_v"]
        tables = self.SP.load(mem["stage"][:, :], self.dram["odd_tables"], self.sems["stage"], 32, start)
        cos, sin = mem["stage"][:, 0:SEQ], mem["stage"][:, SEQ:2 * SEQ]
        near = mem["stage"][:, 2 * SEQ:4 * SEQ].rearrange("q (b k) -> q b k", b=X_TILES)
        src_t = lambda k, tt: (mem["n_hi"][:, k, tt * P:(tt + 1) * P], mem["n_lo"][:, k, tt * P:(tt + 1) * P])
        swap = self.mat("swap")
        def store_k(t, bank, m):
            e = self.act(k_t[:, t, SEQ:TOK], bank[:, SEQ:TOK], ACT.Copy, m)
            self.rope(k_t[:, t, 0:SEQ], bank, e, P, cos, sin, swap, tables)
        self.project("odd_kv", 0, KD, 256, TOK, lambda k: self.n_parts(k), ready, store_k)

        def store_v(pair, bank, m):
            e = self.act(v[:, 2 * pair:2 * pair + 2, :], bank[:, :].rearrange("p (t n) -> p t n", t=2), ACT.Copy, m)
            self.banks.give(bank, e)
        self.project_tokens("odd_kv", 1, KD, 256, range(TT), src_t, ready, store_v)
        for c in range(4):
            self.project("odd_q", c, KD, 256, SEQ, lambda k: self.n_parts(k, SEQ), ready,
                         lambda t, bank, m, c=c: self.rope(q_t[:, 2 * c + t, :], bank, m, P, cos, sin, swap))
        n_read = self.PE.last()
        neg = mem["small"][:, 128:144]
        m_neg = self.ts(neg, self.vec("sink", 0, 16), -1.0, None, ALU.mult, None)
        buffers = Buffers(mem["o_p"])
        m_in = [self.DVE.last(), self.ACT.last(), m_neg]
        out_ready = []

        def heads(pair, qb, j, shared):
            kvs = (2 * pair, 2 * pair + 1)
            rows = [slice(0, C_DIM), slice(C_DIM, 2 * C_DIM)]
            if j == 0:
                shared += [(*buffers.take(), []) for _ in kvs]
            tile = pair * 4 + j
            taken = [self.banks.take() for _ in kvs]
            for i in range(2):
                self.mm(taken[i][0][:, :], q_t[rows[i], tile, qb * P:(qb + 1) * P], k_t[rows[i], pair, :], True, False,
                        taken[i][1], m_in)
            other = slice((1 - qb) * P, (2 - qb) * P)
            marks = [self.mm(bank[:, other], self.mat("ident"), near[:, qb, other], False, True, counted=True)
                     for bank, _ in taken]
            yield
            parts = []
            for i, kv in enumerate(kvs):
                buf, buf_free, done = shared[i]
                h = 4 * kv + j
                parts.append(self.softmax(taken[i][0], marks[i], C_DIM ** -0.5,
                                          (self.vec("sink", h), neg[:, h:h + 1]), buf[:, :, j * P:(j + 1) * P],
                                          buf_free, done))
            while True:
                parts = [x for x in parts if next(x, "ended") != "ended"]
                if not parts:
                    break
                yield
            if j < 3:
                return
            yield
            out, free = self.banks.take()
            for k in range(TT):
                for i, kv in enumerate(kvs):
                    buf, _, done = shared[i]
                    m = self.mm(out[rows[i], :], v[:, k, kv * C_DIM:(kv + 1) * C_DIM], buf[:, k, :], k == 0,
                                k == TT - 1, done, free, counted=k == TT - 1)
            for buf, _, _ in shared:
                buffers.give(buf, m)
            yield
            t, free = self.temps.take()
            m = self.act(t[:, :], out[:, :], ACT.Copy, m, free)
            self.banks.give(out, m)
            tiles, at = slice(pair * 4, pair * 4 + 4), slice(qb * P, (qb + 1) * P)
            m = self.split(mem["n_hi"][:, tiles, at], mem["n_lo"][:, tiles, at],
                           t[:, :].rearrange("p (j q) -> p j q", j=4), m, n_read)
            self.temps.give(t, m)
            out_ready.append(m)

        items = []
        for pair in range(C_KV // 2):
            for qb in range(X_TILES):
                shared = []
                items += [heads(pair, qb, j, shared) for j in range(4)]
        self.interleave(items)
        m = out_ready[-1]
        for c in range(4):
            self.project("odd_out", c, KD, 256, SEQ, lambda k: self.n_parts(k, SEQ), [m] * KD,
                         lambda t, bank, mk, c=c: self.add_gated(bank, mk, 2 * c + t, self.mod_scale(dest, 5), SEQ))
        self.barrier()

    def second_mixer(self, dest):
        mem, small = self.mem, self.mem["small"]
        wsc = small[:, 0:2 * KD].rearrange("p (k s) -> p k s", k=KD)
        m = self.tt(wsc, dest[:, KD:2 * KD, :], self.vec("mix_pre", 0, KD).unsqueeze(2).broadcast_to((P, KD, 2)),
                    ALU.mult, self.DVE.last())
        start = self.barrier()
        ready = self.norm(lambda k, s: wsc[:, k, s:s + 1], self.mod_scale(dest, 0), TOK, m)
        tables = self.SP.load(mem["stage"][:, 0:2 * SEQ], self.dram["mla_tables"], self.sems["stage"], 48,
                              start)
        cos, sin = mem["stage"][:, 0:SEQ], mem["stage"][:, SEQ:2 * SEQ]
        src = lambda k: self.n_parts(k)
        src_x = lambda k: self.n_parts(k, SEQ)
        src_t = lambda k, tt: (mem["n_hi"][:, k, tt * P:(tt + 1) * P], mem["n_lo"][:, k, tt * P:(tt + 1) * P])
        cq, ckv, kr = (mem["m_cqh"], mem["m_cql"]), (mem["m_ckh"], mem["m_ckl"]), mem["m_kr"]
        z_t, xs_t, b_t, c_t = mem["m_z"], mem["m_xs"], mem["m_b"], mem["m_c"]

        def latent(banks, n, weight, width, parts):
            sums, free = self.banks.take()
            for i, (bank, m) in enumerate(banks):
                sq, sq_free = self.temps.take()
                m = self.act(sq[:, 0:n], bank[:, 0:n], ACT.Square, sq_free, m)
                m = self.add_squares(sums, i, len(banks), sq[:, 0:n], m, free)
                self.temps.give(sq, m)
                banks[i] = (bank, m)
            inv, m = yield from self.rstd_steps(sums, len(banks), n, width, m)
            for k, (bank, m_sq) in enumerate(banks):
                t, free = self.temps.take()
                e = self.ts(t[:, 0:n], bank[:, 0:n], self.vec(weight, k), None, ALU.mult, None, free, m_sq)
                self.banks.give(bank, e)
                e = self.tt(t[:, 0:n], t[:, 0:n], inv[:, 0:n], ALU.mult, m, e)
                if k == len(banks) - 1:
                    self.banks.give(inv, e)
                e = self.split(parts[0][:, k, 0:n], parts[1][:, k, 0:n], t[:, 0:n], e)
                self.temps.give(t, e)

        under_way = []

        def move_on():
            under_way[:] = [x for x in under_way[::-1] if next(x, "ended") != "ended"][::-1]

        found_kv, found = [], []
        self.project_group([("in_kv", 0, 256, lambda t, bank, m: found_kv.append((bank, m)))], TOK, src, ready)
        under_way.append(latent(found_kv, TOK, "kv_norm", KV_RANK, ckv))
        for c in range(2):
            self.project("in_q", c, KD, (256, P)[c], SEQ, src_x, ready, lambda t, bank, m: found.append((bank, m)))
            move_on()
        under_way.append(latent(found, SEQ, "q_norm", Q_RANK, cq))
        dt = small[:, 64:64 + 32 * TT].rearrange("p (t g) -> p t g", t=TT)

        def store_dt_kr(t, bank, m):
            e = self.act(kr[:, :], bank[:, :], ACT.Copy, m)
            self.m_dt = self.columns_of(bank, e, slice(0, 2 * S_HEADS), dt, "dt_b")
            x, free = self.temps.take()
            e = self.act(x[0:QD, 0:SEQ], kr[0:QD, 0:SEQ], ACT.Copy, e, free)
            self.rope_from(kr[0:QD, 0:SEQ], x, e, QD, cos, sin, self.mat("turn"), tables)
        self.project("in_dt_kr", 0, KD, P, TOK, src, ready, store_dt_kr)
        move_on()

        def store_z(c):
            def finish(t, bank, m):
                self.banks.give(bank, self.act(z_t[:, 2 * c + t, :], bank[:, 0:SEQ], ACT.Silu, m))
            return finish
        def conv(base, n):
            def finish(t, bank, m):
                tile = base + t
                s = n // SEQ
                x, free = self.temps.take()
                xv = x[:, 0:n].rearrange("p (s t) -> p s t", s=s)
                bv = bank[:, 0:n].rearrange("p (s t) -> p s t", s=s)
                w = lambda tap: self.vec("sconv_w", tap * 12 + tile)
                m = self.act(x[:, 0:n], bank[:, 0:n], ACT.Identity, m, free, scale=w(2),
                             bias=self.vec("sconv_b", tile))
                for tap in (0, 1, 3, 4):
                    off = tap - 2
                    o = slice(max(0, -off), SEQ - max(0, off))
                    i = slice(max(0, off), SEQ - max(0, -off))
                    m = self.stt(xv[:, :, o], bv[:, :, i], w(tap), xv[:, :, o], ALU.mult, ALU.add, m)
                self.banks.give(bank, m)
                out = xs_t[:, tile, 0:n] if tile < 8 else b_t[:, tile - 8, 0:n] if tile < 10 else c_t[:, tile - 10, :]
                m = self.act(out, x[:, 0:n], ACT.Silu, m)
                self.temps.give(x, m)
            return finish
        for c in range(6):
            n = TOK if c < 5 else SEQ
            self.project("in_xbc", c, KD, 256, n, src if c < 5 else src_x, ready, conv(2 * c, n))
            move_on()
            if c == 1:
                scales = self.ssd_scales(dt)
            if c in (1, 2):
                next(scales)
            if c == 3:
                scan = self.drain(scales)
            if c >= 2:
                self.project("in_z", c - 2, KD, 256, SEQ, src_x, ready, store_z(c - 2))
                move_on()
            if c == 2:
                next(scales)
        self.barrier()
        gated = self.ssd(dt, *scan)
        self.barrier()
        self.latent_attention(cq, ckv, kr, cos, sin, self.ssd_norm(gated))
        self.barrier()
        mix = mem["m_mix"]
        parts = lambda k: (mem["y_hi"][:, k, :], mem["y_lo"][:, k, :])

        def store_mix(k, bank, m):
            e = self.act(mix[:, k, :], bank[:, 0:SEQ], ACT.Copy, m)
            self.banks.give(bank, e)
            self.add_square(k, SEQ, mix[:, k, :], e)
        for q in range(4):
            banks = None
            for i in range(2):
                banks = self.project("mix_out", 2 * q + i, KD, 256, SEQ, lambda k, i=i: parts(8 * i + k), None,
                                     lambda t, bank, m, q=q: store_mix(2 * q + t, bank, m),
                                     first=i == 0, last=i == 1, banks=banks)
        self.post_norm(mix, dest, 2, "mix_post")

    def post_norm(self, mix, dest, sec, weight, last=False):
        small = self.mem["small"]
        gw = small[:, 0:KD]
        m0 = self.tt(gw, dest[:, sec * KD:(sec + 1) * KD, 0], self.vec(weight, 0, KD), ALU.mult, self.DVE.last())
        inv, m = self.h_rstd(SEQ)
        h = self.mem["h"]
        for k in range(KD):
            e = self.stt(mix[:, k, :], mix[:, k, :], gw[:, k:k + 1], inv[:, 0:SEQ], ALU.mult, ALU.mult, m, m0)
            self.h_ready[k] = self.tt(h[:, k, 0:SEQ], h[:, k, 0:SEQ], mix[:, k, :], ALU.add, e)
            if not last:
                self.add_square(k, SEQ)
        self.banks.give(inv, e)

    def ssd_scales(self, dt):
        mem, small = self.mem, self.mem["small"]
        at = 64 + 32 * TT
        da, col, w = (small[:, at + i:at + i + 32 * TT].rearrange("p (t g) -> p t g", t=TT) for i in (0, 128, 256))
        fade = mem["mods"][0][:, 0:64, :].rearrange("p a b -> p (a b)").rearrange("p (t g) -> p t g", t=TT)
        neg_a = small[:, 0:32]
        m = yield from self.log_steps(da, w, dt, 1.0, [self.m_dt], col)
        m_dt = self.copy(dt, da, m)
        m2 = self.act(neg_a, self.vec("a_log", 0, 32), ACT.Exp)
        m2 = self.ts(neg_a, neg_a, -1.0, None, ALU.mult, None, m2)
        m_da = self.tt(da, dt, neg_a.unsqueeze(1).broadcast_to((P, TT, 32)), ALU.mult, m_dt, m2)
        yield
        bank, free = self.banks.take()
        for tt in range(TT):
            for d in range(2):
                g = slice(tt * 32 + d * 16, tt * 32 + d * 16 + 16)
                self.mm(bank[:, g], self.mat(("tri_f", "tri_b")[d]), da[:, tt, d * 16:d * 16 + 16], True, True,
                        m_da, free)
        m = self.mm(bank[:, P:2 * P], self.mat("ones"), da.rearrange("p t g -> p (t g)"), True, True, counted=True)
        total = bank[:, P:2 * P].rearrange("p (t g) -> p t g", t=TT)
        m_col = self.ts(col, bank[:, 0:P].rearrange("p (t g) -> p t g", t=TT), -1.0, None, ALU.mult, None, m)
        m_w = self.tt(w, total, col, ALU.add, m_col)
        m_fade = self.act(fade, total, ACT.Exp, m_w)
        self.banks.give(bank, m_fade)
        m_w = self.act(w, w, ACT.Exp, m_w)
        m_w = self.tt(w, w, dt, ALU.mult, m_w)
        return da, col, w, fade, m_da, m_col, m_w, m_fade

    def ssd(self, dt, da, col, w, fade, m_da, m_col, m_w, m_fade):
        mem = self.mem
        xs_t, b_t, c_t, z_t = mem["m_xs"], mem["m_b"], mem["m_c"], mem["m_z"]
        xs, bt, y, state = mem["s_xs"], mem["s_b"], mem["s_y"], mem["s_state"]
        cb = mem["s_cb"]
        for tt in range(TT):
            for half in range(2):
                bank, free = self.banks.take()
                for j in range(4):
                    m = self.turn(bank[:, j * P:(j + 1) * P], xs_t[:, 4 * half + j, tt * P:(tt + 1) * P], free,
                                  counted=j == 3)
                m = self.act(xs[:, tt, half * 512:(half + 1) * 512], bank[:, :], ACT.Copy, m)
                self.banks.give(bank, m)
            bank, free = self.banks.take()
            for j in range(2):
                m = self.turn(bank[:, j * P:(j + 1) * P], b_t[:, j, tt * P:(tt + 1) * P], free, counted=j == 1)
            m_xs = self.act(bt[:, tt, :], bank[:, 0:256], ACT.Copy, m)
            self.banks.give(bank, m_xs)
        bank, free = self.banks.take()
        for tt in range(X_TILES):
            for g in range(S_GROUPS):
                o = (tt * S_GROUPS + g) * P
                m = self.mm(bank[:, o:o + P], b_t[:, g, tt * P:(tt + 1) * P], c_t[:, g, tt * P:(tt + 1) * P], True,
                            True, free, counted=True)
        m_cb = self.act(cb[:, :], bank[:, :], ACT.Copy, m)
        self.banks.give(bank, m_cb)
        cbv = cb[:, :].rearrange("p (t g l) -> p t g l", t=X_TILES, g=S_GROUPS)
        wide = lambda ap: ap.rearrange("p (h l) -> p h l", h=4)
        heads = lambda ap: ap.rearrange("p k (h e) -> p k h e", h=4)
        spread = lambda ap, k: ap.rearrange("p (k h) -> p k h", k=k).unsqueeze(3).broadcast_to((P, k, 4, S_DIM))
        head = lambda ap, h: ap[:, h // 4, (h % 4) * S_DIM:(h % 4 + 1) * S_DIM]
        order = ([2, 3, 0, 1], [3, 2, 1, 0])
        y_first = [[None] * 4 for tt in range(X_TILES)]
        m_state, state_used = [None, None], [None, None]
        inputs = Buffers(mem["s_in"])
        gated = []
        opened = {}

        def scale_inputs(d, step):
            tt = order[d][step]
            xd, free = inputs.take()
            m = self.tt(heads(xd), heads(xs[:, tt, :].rearrange("p (k n) -> p k n", k=4)),
                        spread(dt[:, tt, d * 16:(d + 1) * 16], 4), ALU.mult, m_xs, free, m_cb, line=self.POOL)
            opened[d] = (xd, m)
            yield

        def outputs(d, step, quad):
            tt = order[d][step]
            cols = slice(tt * P, (tt + 1) * P)
            tri, mask = self.mat(("tri_f", "tri_b")[d]), self.mat(("mask_f", "mask_b")[d])
            g = quad // 2
            xd, m_xd = opened[d]
            a_bank, free = self.banks.take()
            for j in range(4):
                c = d * 16 + 4 * quad + j
                m = self.mm(a_bank[:, j * P:(j + 1) * P], da[:, tt, c:c + 1].broadcast_to((P, P)), tri, True, True,
                            free, m_da, counted=j == 3)
            yield
            ce, free = self.temps.take()
            m3 = self.act(ce[:, :], a_bank[:, :], ACT.Exp, m, free)
            dec, free = self.temps.take()
            m2 = self.tt(wide(dec[:, :]), wide(a_bank[:, :]), mask.unsqueeze(1).broadcast_to((P, 4, P)), ALU.add, m,
                         free, m3)
            self.banks.give(a_bank, m2)
            yield
            for j in range(4):
                o, c = slice(j * P, (j + 1) * P), d * 16 + 4 * quad + j
                m_dec = self.act(dec[:, o], dec[:, o], ACT.Exp, m2, m_col, bias=col[:, tt, c:c + 1])
            m3 = self.tt(wide(ce[:, :]), wide(ce[:, :]), c_t[:, g, cols].unsqueeze(1).broadcast_to((P, 4, P)),
                         ALU.mult, m3, line=self.POOL)
            m2 = self.tt(wide(dec[:, :]), wide(dec[:, :]), cbv[:, tt, g, :].unsqueeze(1).broadcast_to((P, 4, P)),
                         ALU.mult, m_dec, m_cb)
            yield
            y_bank, free = self.banks.take()
            for j in range(4):
                h = 4 * quad + j
                out = y_bank[(h % 2) * 64:(h % 2) * 64 + 64, (j // 2) * P:(j // 2 + 1) * P]
                self.mm(out, head(xd, h), dec[:, j * P:(j + 1) * P], True, False, m_xd, m2, free)
                m = self.mm(out, head(state[d], h), ce[:, j * P:(j + 1) * P], False, True, m_state[d], m3,
                            counted=j == 3)
            self.temps.give(dec, m)
            self.temps.give(ce, m)
            state_used[d] = m
            if quad == 3:
                inputs.give(xd, m)
            yield
            yv = y[:, 2 * quad:2 * quad + 2, cols]
            bv = y_bank[:, 0:256].rearrange("p (j l) -> p j l", j=2)
            if y_first[tt][quad]:
                e = self.tt(yv, yv, bv, ALU.add, m, y_first[tt][quad])
                self.banks.give(y_bank, e)
                for k in (2 * quad, 2 * quad + 1):
                    m = self.stt(y[:, k, cols], xs_t[:, k, cols], self.vec("ssd_d", k), y[:, k, cols], ALU.mult,
                                 ALU.add, e)
                gated.append(self.tt(yv, yv, z_t[:, 2 * quad:2 * quad + 2, cols], ALU.mult, m, line=self.POOL))
            else:
                y_first[tt][quad] = e = self.copy(yv, bv, m)
                self.banks.give(y_bank, e)

        def update(d, step):
            tt = order[d][step]
            xw, free = inputs.take()
            m = self.tt(heads(xw), heads(xs[:, tt, :].rearrange("p (k n) -> p k n", k=4)),
                        spread(w[:, tt, d * 16:(d + 1) * 16], 4), ALU.mult, m_w, m_xs, m_cb, free,
                        line=self.POOL if step else self.DVE)
            yield
            found = []
            for g in range(S_GROUPS):
                bank, free = self.banks.take()
                found.append((bank, self.mm(bank[:, :], bt[:, tt, g * P:(g + 1) * P], xw[:, 2 * g:2 * g + 2, :], True,
                                            True, m, free, counted=True)))
            inputs.give(xw, found[1][1])
            yield
            yield
            for g, (bank, m) in enumerate(found):
                part = state[d][:, 2 * g:2 * g + 2, :]
                new = bank[:, :].rearrange("p (k n) -> p k n", k=2)
                if step == 0:
                    e = self.copy(part, new, m, m_xs)
                else:
                    e = self.tt(heads(part), heads(part), spread(fade[:, tt, d * 16 + g * 8:d * 16 + (g + 1) * 8], 2),
                                ALU.mult, m_fade, state_used[d], m_state[d])
                    e = self.tt(part, part, new, ALU.add, e, m)
                self.banks.give(bank, e)
            m_state[d] = e

        items = [update(d, step) for step in range(2) for d in range(2)]
        for step in range(2, TT):
            items += [scale_inputs(d, step) for d in range(2)]
            items += [outputs(d, step, quad) for d in range(2) for quad in range(4)]
            if step < TT - 1:
                items += [update(d, step) for d in range(2)]
        self.interleave(items)
        return gated

    def ssd_norm(self, m):
        mem, y = self.mem, self.mem["s_y"]
        bank, free = self.banks.take()
        for k in range(KD):
            sq, sq_free = self.temps.take()
            m_sq = self.act(sq[:, 0:SEQ], y[:, k, :], ACT.Square, sq_free, m)
            m_sum = self.add_squares(bank, k, KD, sq[:, 0:SEQ], m_sq, free)
            self.temps.give(sq, m_sum)
        yield
        inv, m = yield from self.rstd_steps(bank, KD, SEQ, D_INNER, m_sum)
        yield
        for k in range(KD):
            t, free = self.temps.take()
            e = self.stt(t[:, 0:SEQ], y[:, k, :], self.vec("ssd_norm", k), inv[:, 0:SEQ], ALU.mult, ALU.mult, m, free)
            if k == KD - 1:
                self.banks.give(inv, e)
                self.m_y = e
            e = self.split(mem["y_hi"][:, 8 + k, :], mem["y_lo"][:, 8 + k, :], t[:, 0:SEQ], e)
            self.temps.give(t, e)
            if k % 2:
                yield

    def latent_attention(self, cq, ckv, kr, cos, sin, beside):
        mem = self.mem
        buffers = Buffers(mem["l_p"])
        turn = self.mat("turn")
        q_ready, k_ready, v_ready, ended = {}, {}, {}, {}
        opened = {}

        def group_free(g):
            return ended[g - 2] if g > 1 else None

        def queries(g, h):
            if h == 0:
                opened["q"] = self.next_chunk("q_up", g, 3 * HEADS_AT_ONCE * QD)
            chunk = opened["q"]
            hi, lo = (x.rearrange("p (k h c) -> p k h c", k=3, h=HEADS_AT_ONCE) for x in (chunk.hi, chunk.lo))
            bank, free = self.banks.take()
            for k in range(3):
                m = self.mm3(bank[0:QD, 0:SEQ], (hi[:, k, h, :], lo[:, k, h, :]), (cq[0][:, k, :], cq[1][:, k, :]),
                             k == 0, k == 2, chunk.ready, free, counted=k == 2)
            if h == HEADS_AT_ONCE - 1:
                self.done_with(chunk, m)
            yield
            x, free = self.temps.take()
            m = self.act(x[0:QD, 0:SEQ], bank[0:QD, 0:SEQ], ACT.Copy, m, free)
            self.banks.give(bank, m)
            yield
            q_ready[g, h] = self.rope_from(mem["l_q"][g % 2][0:QD, h, :], x, m, QD, cos, sin, turn, group_free(g))

        def keys(g, h):
            if h == 0:
                opened["kv"] = self.next_chunk("kv_up", g, 2 * HEADS_AT_ONCE * P)
            chunk = opened["kv"]
            hi, lo = (x.rearrange("p (k h c) -> p k h c", k=2, h=HEADS_AT_ONCE) for x in (chunk.hi, chunk.lo))
            bank, free = self.banks.take()
            for k in range(2):
                m = self.mm3(bank[:, :], (hi[:, k, h, :], lo[:, k, h, :]), (ckv[0][:, k, :], ckv[1][:, k, :]),
                             k == 0, k == 1, chunk.ready, free, counted=k == 1)
            yield
            k_g = mem["l_k"][g % 2]
            m = self.act(k_g[0:NOPE, h, :], bank[0:NOPE, :], ACT.Copy, m, group_free(g))
            self.banks.give(bank, m)
            m2 = self.copy(k_g[NOPE:QD, h, :], kr[NOPE:QD, :], group_free(g))
            k_ready[g, h] = [m, m2]

        def values(g, pair):
            chunk = opened["kv"]
            hi, lo = (x.rearrange("p (k h c) -> p k h c", k=2, h=HEADS_AT_ONCE) for x in (chunk.hi, chunk.lo))
            bank, free = self.banks.take()
            for j in range(2):
                tt = 2 * pair + j
                c = slice(tt * P, (tt + 1) * P)
                for k in range(2):
                    m = self.mm3(bank[:, j * 256:(j + 1) * 256].rearrange("p (h c) -> p h c", h=HEADS_AT_ONCE),
                                 (ckv[0][:, k, c], ckv[1][:, k, c]),
                                 (hi[:, k, :, NOPE:P], lo[:, k, :, NOPE:P]), k == 0, k == 1, free, counted=k == 1)
            if pair == 1:
                self.done_with(chunk, m)
            yield
            m = self.act(mem["l_v"][g % 2][:, 2 * pair:2 * pair + 2, :],
                         bank[:, :].rearrange("p (t c) -> p t c", t=2), ACT.Copy, m, group_free(g))
            self.banks.give(bank, m)
            v_ready.setdefault(g, []).append(m)

        def head(g, h, qb):
            bank, free = self.banks.take()
            m = self.mm(bank[:, :], mem["l_q"][g % 2][0:QD, h, qb * P:(qb + 1) * P], mem["l_k"][g % 2][0:QD, h, :],
                        True, True, free, q_ready[g, h], k_ready[g, h], counted=True)
            yield
            buf, buf_free = buffers.take()
            done = []
            yield from self.softmax(bank, m, QD ** -0.5, None, buf, buf_free, done)
            yield
            rows = slice((h % 2) * V_DIM, (h % 2) * V_DIM + V_DIM)
            out, free = self.banks.take()
            for k in range(TT):
                m = self.mm(out[rows, 0:P], mem["l_v"][g % 2][:, k, h * V_DIM:(h + 1) * V_DIM], buf[:, k, :],
                            k == 0, k == TT - 1, done, v_ready[g], free, counted=k == TT - 1)
            buffers.give(buf, m)
            ended[g] = m
            yield
            t, free = self.temps.take()
            m = self.act(t[rows, 0:P], out[rows, 0:P], ACT.Copy, m, free)
            self.banks.give(out, m)
            tile, at = (g * HEADS_AT_ONCE + h) // 2, slice(qb * P, (qb + 1) * P)
            m = self.split(mem["y_hi"][rows, tile, at], mem["y_lo"][rows, tile, at], t[rows, 0:P], m, self.m_y)
            self.temps.give(t, m)

        def projections(g):
            return ([queries(g, h) for h in range(HEADS_AT_ONCE)] + [keys(g, h) for h in range(HEADS_AT_ONCE)]
                    + [values(g, pair) for pair in range(2)])

        items = [beside] + projections(0)
        for g in range(M_HEADS // HEADS_AT_ONCE):
            ahead = projections(g + 1) if g + 1 < M_HEADS // HEADS_AT_ONCE else []
            for h in range(HEADS_AT_ONCE):
                for qb in range(X_TILES):
                    items.append(head(g, h, qb))
                    if h:
                        n = 2 if (h, qb) != (3, 1) else len(ahead)
                        items += ahead[:n]
                        ahead = ahead[n:]
        self.interleave(items)

    def second_ffn(self, dest):
        mem, small = self.mem, self.mem["small"]
        wsc = small[:, 16:16 + KD]
        m = self.tt(wsc, dest[:, 4 * KD:5 * KD, 0], self.vec("ffn_pre", 0, KD), ALU.mult, self.DVE.last())
        ready = self.norm(lambda k, s: wsc[:, k:k + 1], self.mod_scale(dest, 3), SEQ, m)
        acc = mem["f_out"]

        def gate(j, n, g_bank, g_mark, u_bank, u_mark):
            t, free = self.temps.take()
            w = lambda tap: self.vec("fconv_w", tap * KF + j)
            m = self.act(t[:, 0:n], g_bank[:, 0:n], ACT.Identity, g_mark, free, scale=w(1),
                         bias=self.vec("fconv_b", j))
            m = self.stt(t[:, 1:n], g_bank[:, 0:n - 1], w(0), t[:, 1:n], ALU.mult, ALU.add, m)
            m = self.stt(t[:, 0:n - 1], g_bank[:, 1:n], w(2), t[:, 0:n - 1], ALU.mult, ALU.add, m)
            self.banks.give(g_bank, m)
            m = self.act(t[:, 0:n], t[:, 0:n], ACT.Gelu, m)
            m = self.tt(t[:, 0:n], t[:, 0:n], u_bank[:, 0:n], ALU.mult, m, u_mark)
            self.banks.give(u_bank, m)
            return t, m

        seen = set()

        def finish(k, bank, m, final):
            if k in seen:
                e = self.tt(acc[:, k, :], acc[:, k, :], bank[:, 0:SEQ], ALU.add, m, self.DVE.last())
            else:
                e = self.copy(acc[:, k, :], bank[:, 0:SEQ], m)
            seen.add(k)
            self.banks.give(bank, e)
            if final:
                self.add_square(k, SEQ, acc[:, k, :], e)
        self.hidden(("up", 0), ("down", 0), SEQ, ready, gate, finish)
        self.post_norm(acc, dest, 5, "ffn_post", last=True)

    def compose(self):
        mem, dram, sems = self.mem, self.dram, self.sems
        mats = self.SP.load(mem["matrices"][:, :], dram["matrices"], sems["matrices"], 16)
        vecs = self.SP.load(mem["vectors"][:, :], dram["vectors"], sems["vectors"], 16)
        self.h_ready = [self.SP.load(mem["h"][:, :, :], dram["tokens"], sems["h"], 16)] * KD
        zero = self.DVE.do(lambda e: e.memset(mem["silu_c"][:, :, :, :], 0.0))
        zero = self.DVE.do(lambda e: e.memset(mem["zeros"][:, :], 0.0))
        zero = self.DVE.do(lambda e: e.memset(mem["eps"][:, :], EPS))
        self.DVE.wait(zero)
        cv = self.vec("c", 0, 4 * KD).rearrange("p (b s k) -> p b s k", b=2, s=2)
        for b in range(2):
            for s in range(2):
                m = self.act(mem["silu_c"][:, b, :, s], cv[:, b, s, :], ACT.Silu, vecs, zero)
        self.silu_c_ready = m
        for line in (self.PE, self.DVE, self.ACT):
            line.wait(mats, vecs)

        self.squares = []
        for k in range(KD):
            self.add_square(k, TOK)
        mods, mod_2 = mem["mods"], mem["mod_2"]
        half = 0.5

        def scales(dest, ones_, halves):
            for s in ones_:
                self.section(dest, s, ALU.add, 1.0)
            for s in halves:
                self.section(dest, s, ALU.mult, half)

        self.first_ffn(mods[0])
        self.finish_side()
        scales(mods[0], [4, 7], [8])
        self.modulation("ada", 36, 0, mods[1], ("ada_b", N_MOD * KD), [1, 0, 2, 3, 4, 5, 6, 7, 8])
        self.even_mixer(mods[0])
        self.ffn(("ffn_in", KF), ("ffn_out", 16), mods[0], (6, 7, 8), TOK)
        self.finish_side()
        scales(mods[1], [1, 4, 7], [2, 8])
        self.modulation("mod_2", 0, 1, mod_2, ("b_mod", 0), [0, 1, 2, 3, 4, 5])
        self.ffn(("ffn_in", 2 * KF), ("ffn_out", 32), mods[1], (0, 1, 2), TOK)
        self.finish_side()
        self.low_on_pool = True
        self.odd_mixer(mods[1])
        self.low_on_pool = False
        ctx_in = self.SP.load(mem["h"][:, :, SEQ:TOK], dram["ctx_2"], sems["h"], 32, self.PE.last(), self.ACT.last(),
                              self.DVE.last())
        scales(mod_2, [1, 4], [])
        self.ffn(("ffn_in", 3 * KF), ("ffn_out", 48), mods[1], (6, 7, 8), SEQ)
        h = mem["h"]
        inv, m = self.h_rstd(SEQ)
        for k in range(KD):
            e = self.stt(h[:, k, 0:SEQ], h[:, k, 0:SEQ], self.vec("final", k), inv[:, 0:SEQ], ALU.mult, ALU.mult, m)
            self.h_ready[k] = [e, ctx_in]
            self.add_square(k, TOK)
        self.banks.give(inv, e)
        self.barrier()
        self.low_on_pool = True
        self.second_mixer(mod_2)
        self.low_on_pool = False
        self.barrier()
        self.second_ffn(mod_2)
        out = self.SP.load(dram["out"], h[:, :, 0:SEQ], sems["out"], 16, self.h_ready)
        self.SP.wait(out)

    def first_ffn(self, dest):
        n, per = TOK, D // 256
        self.split_ahead = 1
        ready, found = [], [{}, {}]
        norm = self.norm_steps(self.mod_scale(dest, 1), self.mod_scale(dest, 0), n, ready, True)
        products = self.first_inward(("ffn_in", 0), n, ready, found)
        next(norm)

        def scale_shift(q):
            self.side = [("ada", 0, sec, q, 0, dest, ("ada_b", 0), None) for sec in (1, 0)]
            self.finish_side()
            scale = dest[:, KD + 2 * q:KD + 2 * q + 2, :]
            self.DVE.wait(self.ts(scale, scale, 1.0, None, ALU.add, None, self.DVE.last()))

        scale_shift(0)
        next(products)
        for q in range(per):
            next(norm, None)
            if q + 1 < per:
                scale_shift(q + 1)
            else:
                self.split_ahead = 4
                self.prepare_ahead(len(self.asked) - 1)
            next(products, None)
        self.drain(norm)
        self.modulation("ada", 0, 0, dest, ("ada_b", 0), [2, 3, 4, 5, 6, 7, 8])
        halved = []

        def finish(k, bank, m, final):
            if not halved:
                halved.append(self.section(dest, 2, ALU.mult, 0.5))
                self.DVE.wait(halved[0])
            self.add_gated(bank, m, k, self.mod_scale(dest, 2), n, final)
        self.hidden(("ffn_in", 0), ("ffn_out", 0), n, ready, self.silu_gate, finish, found)


def build(nc, dram):
    base = [16512]
    mem = {}

    def place(name, shape, dtype=F32, at=None):
        width = 4
        for s in shape[1:]:
            width *= s
        offset = base[0] if at is None else at
        t = nc.alloc_sbuf_tensor_at(name, shape, dtype, offset=offset)
        if at is None:
            base[0] += (width + 31) // 32 * 32
        return t

    mem["h"] = place("h", [P, KD, TOK])
    n_at = base[0]
    mem["n_hi"] = place("n_hi", [P, KD, TOK], F32R)
    mem["n_lo"] = place("n_lo", [P, KD, TOK], F32R)
    a_at = base[0]
    mem["a_hi"] = place("a_hi", [P, A_SLOTS, TOK], F32R)
    mem["a_lo"] = place("a_lo", [P, A_SLOTS, TOK], F32R)
    mem["raw"] = [place(f"raw{i}", [P, CHUNK]) for i in range(RAW_SLOTS)]
    mem["w_hi"] = [place(f"w_hi{i}", [P, CHUNK], F32R) for i in range(SPLIT_SLOTS)]
    mem["w_lo"] = [place(f"w_lo{i}", [P, CHUNK], F32R) for i in range(SPLIT_SLOTS)]
    mem["temps"] = [place(f"temp{i}", [P, TOK]) for i in range(TEMPS)]
    mem["matrices"] = place("matrices", [P, len(MATRICES) * P])
    mem["vectors"] = place("vectors", [P, N_VECTORS])
    stage_at = base[0]
    mem["stage"] = place("stage", [P, 8 * P])
    mem["mods"] = [place(f"mod{i}", [P, N_MOD * KD, 2]) for i in range(2)]
    mem["mod_2"] = place("mod_2", [P, N_MOD_2 * KD, 2])
    mem["silu_c"] = place("silu_c", [P, 2, KD, 32])
    mem["small"] = place("small", [P, 640])
    mem["columns"] = [place(f"column{i}", [P, 8]) for i in range(8)]
    mem["zeros"] = place("zeros", [P, 8])
    mem["eps"] = place("eps", [P, 8])
    assert base[0] <= 229368, base[0]
    K = 1024
    for i, x in enumerate(("e_q", "e_k", "e_v", "e_o", "e_u", "e_vb")):
        mem[x] = place(x, [P, 4, TOK], at=a_at + i * 8 * K)
    mem["e_c0"] = place("e_c0", [P, HEADS, HEAD], at=n_at)
    mem["e_c1"] = place("e_c1", [P, HEADS, HEAD], at=n_at + 2 * K)
    places = ([n_at + i * 2 * K for i in (2, 3, 8, 9, 10, 11)] + [a_at + 32 * K + i * 2 * K for i in range(4)]
              + [stage_at, stage_at + 2 * K])
    mem["e_tiles"] = [place(f"e_tile{i}", [P, TOK], at=x) for i, x in enumerate(places)]
    mem["o_q"] = place("o_q", [P, KD, SEQ], at=a_at)
    mem["o_k"] = place("o_k", [P, 2, TOK], at=a_at + 8 * K)
    mem["o_v"] = place("o_v", [P, TT, 256], at=a_at + 12 * K)
    mem["o_p"] = [place(f"o_p{i}", [P, TT, 512], at=a_at + (16 + 8 * i) * K) for i in range(4)]
    mem["m_cqh"] = place("m_cqh", [P, 3, SEQ], F32R, at=a_at)
    mem["m_cql"] = place("m_cql", [P, 3, SEQ], F32R, at=a_at + 3 * K)
    mem["m_ckh"] = place("m_ckh", [P, 2, TOK], F32R, at=a_at + 6 * K)
    mem["m_ckl"] = place("m_ckl", [P, 2, TOK], F32R, at=a_at + 10 * K)
    mem["m_kr"] = place("m_kr", [P, TOK], at=a_at + 14 * K)
    b = a_at + 16 * K
    mem["m_z"] = place("m_z", [P, KD, SEQ], at=b)
    mem["m_xs"] = place("m_xs", [P, KD, TOK], at=b + 8 * K)
    mem["m_b"] = place("m_b", [P, 2, TOK], at=b + 24 * K)
    mem["m_c"] = place("m_c", [P, 2, SEQ], at=b + 28 * K)
    mem["s_cb"] = place("s_cb", [P, TOK], at=b + 30 * K)
    mem["s_y"] = place("s_y", [P, KD, SEQ], at=n_at)
    mem["s_xs"] = place("s_xs", [P, TT, D_INNER], at=n_at + 8 * K)
    mem["s_b"] = place("s_b", [P, TT, 256], at=n_at + 24 * K)
    mem["s_state"] = [place("s_state", [P, 4, SEQ], at=n_at + 28 * K)[:, :, :], mem["m_xs"][:, 0:4, SEQ:TOK]]
    mem["s_in"] = [mem["h"][:, 0:4, SEQ:TOK], mem["h"][:, 4:8, SEQ:TOK], mem["m_xs"][:, 4:8, SEQ:TOK]]
    mem["y_hi"] = place("y_hi", [P, 16, SEQ], F32R, at=n_at)
    mem["y_lo"] = place("y_lo", [P, 16, SEQ], F32R, at=n_at + 16 * K)
    mem["l_q"] = [place(f"l_q{i}", [P, HEADS_AT_ONCE, SEQ], at=b + 16 * i * K) for i in range(2)]
    mem["l_k"] = [place(f"l_k{i}", [P, HEADS_AT_ONCE, TOK], at=b + (16 * i + 4) * K) for i in range(2)]
    mem["l_v"] = [place(f"l_v{i}", [P, TT, HEADS_AT_ONCE * V_DIM], at=b + (16 * i + 12) * K) for i in range(2)]
    mem["l_p"] = [mem["h"][:, TT * i:TT * (i + 1), SEQ + P * j:SEQ + P * (j + 1)] for i in range(2) for j in range(2)]
    mem["m_mix"] = place("m_mix", [P, KD, SEQ], at=a_at)
    mem["f_out"] = place("f_out", [P, KD, TOK], at=n_at)[:, :, SEQ:TOK]
    mem["banks"] = [nc.alloc_psum_tensor(f"bank{i}", [P, 512], F32) for i in range(8)]

    with ExitStack() as stack:
        def semaphore(name):
            return stack.enter_context(nc.semaphore(name))
        sems = {x: semaphore(f"s_{x}") for x in ("pe", "act", "dve", "sp", "pool", "matrices", "vectors", "h",
                                                 "stage", "out")}
        sems["raw"] = [semaphore(f"s_raw{i}") for i in range(RAW_SLOTS)]
        first = Program(nc, dram, mem, sems, None)
        first.compose()
        program = Program(nc, dram, mem, sems, first.asked)
        program.compose()
        assert program.asked == first.asked
        block = stack.enter_context(nc.Block())

        @block.sync
        def _(engine):
            program.SP.run(engine)

        @block.tensor
        def _(engine):
            program.PE.run(engine)

        @block.scalar
        def _(engine):
            program.ACT.run(engine)

        @block.vector
        def _(engine):
            program.DVE.run(engine)

        @block.gpsimd
        def _(engine):
            program.POOL.run(engine)


def chunks(w, cols, width=None):
    kt, n = w.shape[0] // P, w.shape[1] // cols
    out = w.reshape(kt, P, n, cols).transpose(2, 1, 0, 3).reshape(n, P, kt * cols)
    if width and width > kt * cols:
        out = np.pad(out, ((0, 0), (0, 0), (0, width - kt * cols)))
    return out


def inward_chunks(w):
    g, u = w[:, :F].reshape(D, KF, P), w[:, F:].reshape(D, KF, P)
    return chunks(np.stack([g, u], axis=2).reshape(D, 2 * F), 2 * P)


def outward_chunks(w):
    out = []
    for half in range(2):
        rows = w[half * F // 2:(half + 1) * F // 2]
        for q in range(D // 256):
            part = rows[:, q * 256:(q + 1) * 256]
            out += [chunks(part[:6 * P], 256, 6 * 256), chunks(part[6 * P:], 256, 6 * 256)]
    return np.concatenate(out)


def features(v):
    return v.reshape(-1, P).T


def kernel(**inputs):
    import concourse.bacc as bacc
    from concourse.bass_utils import run_bass_kernel_spmd

    a = {k: np.asarray(v) for k, v in inputs.items()}
    square, odd, mla = shape_constants()
    on_all = lambda v: np.broadcast_to(v.reshape(1, -1), (P, v.size))
    vectors = {
        "ada_b": features(a["ada_b"]), "b_mod": features(a["b_mod_2"]), "conv": features(a["mlstm_conv"]),
        "mnorm": features(a["mlstm_norm"]), "sgu": features(a["sgu_norm"]), "final": features(a["final_norm"]),
        "mix_pre": features(a["mix_pre_norm_2"]), "mix_post": features(a["mix_post_norm_2"]),
        "q_norm": features(a["q_norm_2"]), "kv_norm": features(a["kv_norm_2"]),
        "sconv_w": features(a["ssd_conv_w_2"]), "sconv_b": features(a["ssd_conv_b_2"]),
        "ssd_norm": features(a["ssd_norm_2"]), "ssd_d": features(np.repeat(a["ssd_d_2"].reshape(-1), S_DIM)),
        "ffn_pre": features(a["ffn_pre_norm_2"]), "ffn_post": features(a["ffn_post_norm_2"]),
        "fconv_w": features(a["ffn_conv_w_2"]), "fconv_b": features(a["ffn_conv_b_2"]),
        "c": np.concatenate([features(a[x]) for x in ("c", "c_ctx", "c_2", "c_ctx_2")], axis=1),
        "gate_b": on_all(a["mlstm_gate_b"]), "sink": on_all(a["attn_sink"]), "dt_b": on_all(a["ssd_dt_bias_2"]),
        "a_log": on_all(a["ssd_a_log_2"]),
    }
    vectors = np.concatenate([vectors[x] for x in VECTORS], axis=1)
    stream = lambda x: x[0].T.reshape(KD, P, SEQ).transpose(1, 0, 2)
    heads = [4 * kv + j for g in range(2) for j in range(4) for kv in (2 * g, 2 * g + 1)]
    qkv, q_cols = a["odd_w_qkv"][0], C_HEADS * C_DIM
    odd_q = qkv[:, :q_cols].reshape(D, C_HEADS, C_DIM)[:, heads].reshape(D, q_cols)
    odd_out = a["odd_w_out"][0].reshape(C_HEADS, C_DIM, D)[heads].reshape(q_cols, D)
    w_in, even = a["w_in_2"][0], a["even_w_in"][0]
    z_at = Q_RANK + KV_RANK + ROPE
    x_at = z_at + D_INNER
    dt_at = x_at + D_INNER + 2 * S_GROUPS * S_STATE
    kr_at = Q_RANK + KV_RANK
    dt_kr = np.concatenate([w_in[:, dt_at:], np.zeros((D, NOPE - 2 * S_HEADS), np.float32),
                            w_in[:, kr_at:kr_at + ROPE], np.zeros((D, P - QD), np.float32)], axis=1)
    gates_at = 4 * W_A
    arrays = {
        "matrices": square, "vectors": vectors, "odd_tables": odd, "mla_tables": mla,
        "tokens": np.concatenate([stream(a["x"]), stream(a["ctx"])], axis=2), "ctx_2": stream(a["ctx_2"]),
        "even_tables": np.concatenate([a["sgu_ws"][0].transpose(2, 0, 1).reshape(P, 4 * P),
                                       on_all(a["sgu_b"])], axis=1),
        "ada": np.concatenate([chunks(w, 256) for w in a["ada_w"]]),
        "mod_2": chunks(a["w_mod_2"][0], 256),
        "ffn_in": np.concatenate([inward_chunks(w) for w in a["ffn_w_in"].reshape(4, D, 2 * F)]),
        "ffn_out": np.concatenate([outward_chunks(w) for w in a["ffn_w_out"].reshape(4, F, D)]),
        "even_in": chunks(np.concatenate([even[:, :gates_at], even[:, gates_at + 16:]], axis=1), 256),
        "even_gates": chunks(np.pad(even[:, gates_at:gates_at + 16], ((0, 0), (0, P - 16))), P),
        "even_out": chunks(a["even_w_out"][0], 256),
        "odd_q": chunks(odd_q, 256), "odd_kv": chunks(qkv[:, q_cols:], 256), "odd_out": chunks(odd_out, 256),
        "in_q": np.concatenate([chunks(w_in[:, :256], 256), chunks(w_in[:, 256:Q_RANK], P, CHUNK)]),
        "in_kv": chunks(w_in[:, Q_RANK:Q_RANK + KV_RANK], 256),
        "in_dt_kr": chunks(dt_kr, P),
        "in_z": chunks(w_in[:, z_at:x_at], 256), "in_xbc": chunks(w_in[:, x_at:dt_at], 256),
        "q_up": chunks(a["w_q_up_2"][0], HEADS_AT_ONCE * QD),
        "kv_up": chunks(a["w_kv_up_2"][0], HEADS_AT_ONCE * P),
        "mix_out": np.stack([chunks(a["w_out_2"][0][i * D:(i + 1) * D], 256) for i in range(2)],
                            axis=1).reshape(8, P, CHUNK),
        "up": inward_chunks(a["w_up_2"][0]), "down": outward_chunks(a["w_down_2"][0]),
    }
    arrays = {k: np.ascontiguousarray(v) for k, v in arrays.items()}
    nc = bacc.Bacc("TRN2", target_bir_lowering=False, num_devices=1)
    dram = {k: nc.dram_tensor(k, v.shape, F32, kind="ExternalInput").ap() for k, v in arrays.items()}
    dram["out"] = nc.dram_tensor("out", (P, KD, SEQ), F32, kind="ExternalOutput").ap()
    build(nc, dram)
    got = run_bass_kernel_spmd(nc, [arrays], core_ids=[0]).results[0]["out"]
    return got.transpose(2, 1, 0).reshape(1, SEQ, D)
```
